# Optimizing a Trainium2 kernel written in Bass

```python
import jax, jax.numpy as jnp
from jax import lax
import numpy as np

D_MODEL = 1024
BATCH = 1
SEQ = 128
DEPTH = 2
DEC_BATCH = 1
DEC_SEQ = 512
PAST_LEN = 128

GRID_W = 64
N_EVEN = (DEPTH + 1) // 2
N_ODD = DEPTH // 2
EPS = 1e-6
D_A = D_MODEL // 2
A_BLOCKS = 8
A_BS = D_A // A_BLOCKS
A_CONV = 4
A_C = 8.0
D_B = D_MODEL // 2
POOL_WINDOWS = (2, 4, 8, 16)
B_GROUPS = len(POOL_WINDOWS)
B_GS = D_B // B_GROUPS
D_C = D_MODEL // 2
C_CONV = 31
HEAD_DIM = 64
N_Q_HEADS = (D_MODEL // 2) // HEAD_DIM
N_KV_HEADS = 2
D_ATT = N_Q_HEADS * HEAD_DIM
D_KV = N_KV_HEADS * HEAD_DIM
Q_BLOCK = 128
ROPE_THETA = 10000.0
D_FF = 2816
N_EXPERTS = 8
TOP_K = 2
D_FF_E = 1408
D_IN_EVEN = 2 * D_A + D_B
D_IN_ODD = 2 * D_C + D_ATT + 2 * D_KV

kernel_name = 'hybrid_diffusion_prefix_trunk_step'

def rms_norm(x, g):
    xf = x.astype(jnp.float32)
    y = xf * lax.rsqrt(jnp.mean(xf * xf, axis=-1, keepdims=True) + EPS)
    return (y * g.astype(jnp.float32)).astype(x.dtype)

def layer_norm(x, g, b):
    xf = x.astype(jnp.float32)
    mu = jnp.mean(xf, axis=-1, keepdims=True)
    xc = xf - mu
    var = jnp.mean(xc * xc, axis=-1, keepdims=True)
    return (xc * lax.rsqrt(var + EPS) * g.astype(jnp.float32) + b.astype(jnp.float32)).astype(x.dtype)

def ada_params(cond, w_mod, b_mod):
    m = jax.nn.silu(cond) @ w_mod + b_mod
    return jnp.split(m, 6, axis=-1)

def modulate(h, shift, scale):
    return h * (1 + scale) + shift

def depthwise_conv(x, w, b, pad_left, pad_right):
    C = x.shape[-1]
    y = lax.conv_general_dilated(x, w[:, None, :].astype(x.dtype), window_strides=(1,),
                                 padding=[(pad_left, pad_right)],
                                 dimension_numbers=('NWC', 'WIO', 'NWC'),
                                 feature_group_count=C)
    return y + b

def rglru_mixer(u, h0, conv_w, conv_b, w_r, b_r, w_i, b_i, lam):
    B, T, _ = u.shape
    xc = depthwise_conv(u, conv_w, conv_b, A_CONV // 2, A_CONV - 1 - A_CONV // 2)
    xd = jnp.stack([xc, xc[:, ::-1]], axis=2)
    xb = xd.reshape(B, T, 2, A_BLOCKS, A_BS)
    r = jax.nn.sigmoid(jnp.einsum('btnki,nkij->btnkj', xb, w_r).reshape(B, T, 2, D_A) + b_r)
    i = jax.nn.sigmoid(jnp.einsum('btnki,nkij->btnkj', xb, w_i).reshape(B, T, 2, D_A) + b_i)
    log_a = -A_C * r * jax.nn.softplus(-lam)
    a = jnp.exp(log_a)
    bx = jnp.sqrt(-jnp.expm1(2 * log_a)) * (i * xd)

    def step(h, ab):
        a_t, b_t = ab
        h = a_t * h + b_t
        return h, h

    h_last, hs = lax.scan(step, h0.astype(a.dtype),
                          (jnp.moveaxis(a, 1, 0), jnp.moveaxis(bx, 1, 0)))
    hs = jnp.moveaxis(hs, 0, 1)
    y = hs[:, :, 0] + hs[:, ::-1, 1]
    return y, h_last

def pool_mixer(u, w_pool, s_pool):
    B, T, _ = u.shape
    uf = u.astype(jnp.float32)
    cs = jnp.concatenate([jnp.zeros((B, 1, D_B), jnp.float32), jnp.cumsum(uf, axis=1)], axis=1)
    t = np.arange(T)
    outs = []
    for g, w in enumerate(POOL_WINDOWS):
        lo = np.maximum(t - w // 2, 0)
        hi = np.minimum(t + w // 2, T)
        sl = slice(g * B_GS, (g + 1) * B_GS)
        csg = cs[:, :, sl]
        cnt = jnp.asarray((hi - lo).astype(np.float32))[None, :, None]
        outs.append((csg[:, hi] - csg[:, lo]) / cnt - uf[:, :, sl])
    d = jnp.stack(outs, axis=2).astype(u.dtype)
    y = jnp.einsum('btgi,gij->btgj', d, w_pool).reshape(B, T, D_B)
    return y * s_pool

def even_mixer(h, h0, w_in, conv_w, conv_b, w_r, b_r, w_i, b_i, lam, w_pool, s_pool, w_out):
    z = h @ w_in
    u_a, g_a, u_b = z[..., :D_A], z[..., D_A:2 * D_A], z[..., 2 * D_A:]
    y_a, h_last = rglru_mixer(u_a, h0, conv_w, conv_b, w_r, b_r, w_i, b_i, lam)
    y_b = pool_mixer(u_b, w_pool, s_pool)
    y = jnp.concatenate([y_a * jax.nn.gelu(g_a), y_b], axis=-1) @ w_out
    return y, h_last

def odd_project(h, w_in, q_g, k_g):
    B, T, _ = h.shape
    z = h @ w_in
    o1 = 2 * D_C
    o2 = o1 + D_ATT
    o3 = o2 + D_KV
    u_c = z[..., :o1]
    q = rms_norm(z[..., o1:o2].reshape(B, T, N_Q_HEADS, HEAD_DIM), q_g)
    k = rms_norm(z[..., o2:o3].reshape(B, T, N_KV_HEADS, HEAD_DIM), k_g)
    v = z[..., o3:].reshape(B, T, N_KV_HEADS, HEAD_DIM)
    return u_c, q, k, v

def conformer_conv(u, conv_w, conv_b, ln_g, ln_b):
    val, gate = jnp.split(u, 2, axis=-1)
    g = val * jax.nn.sigmoid(gate)
    h = depthwise_conv(g, conv_w, conv_b, C_CONV // 2, C_CONV // 2)
    return jax.nn.silu(layer_norm(h, ln_g, ln_b))

def axial_rope_tables(T):
    rows = T // GRID_W
    pos = jnp.arange(rows * GRID_W)
    row = (pos // GRID_W).astype(jnp.float32)
    col = (pos % GRID_W).astype(jnp.float32)
    n_freq = HEAD_DIM // 4
    inv = ROPE_THETA ** (-jnp.arange(n_freq, dtype=jnp.float32) / n_freq)
    ang = jnp.stack([row[:, None] * inv, col[:, None] * inv], axis=1)
    return jnp.cos(ang), jnp.sin(ang)

def apply_axial_rope(x, cos, sin):
    B, T, H, _ = x.shape
    xa = x.astype(jnp.float32).reshape(B, T, H, 2, 2, HEAD_DIM // 4)
    x1, x2 = xa[..., 0, :], xa[..., 1, :]
    c = cos[None, :, None]
    s = sin[None, :, None]
    out = jnp.stack([x1 * c - x2 * s, x2 * c + x1 * s], axis=-2)
    return out.reshape(B, T, H, HEAD_DIM).astype(x.dtype)

def block_attention(q, k, v):
    B, Tq, _, _ = q.shape
    G = N_Q_HEADS // N_KV_HEADS
    nb = Tq // Q_BLOCK
    qb = q.reshape(B, nb, Q_BLOCK, N_KV_HEADS, G, HEAD_DIM).transpose(1, 0, 2, 3, 4, 5)
    scale = HEAD_DIM ** -0.5

    def one_block(qblk):
        s = jnp.einsum('bqhgd,bkhd->bhgqk', qblk, k, preferred_element_type=jnp.float32) * scale
        p = jax.nn.softmax(s, axis=-1).astype(v.dtype)
        return jnp.einsum('bhgqk,bkhd->bqhgd', p, v)

    o = lax.map(one_block, qb)
    return o.transpose(1, 0, 2, 3, 4, 5).reshape(B, Tq, D_ATT)

def odd_output(u_c, attn, conv_w, conv_b, ln_g, ln_b, w_out):
    y_c = conformer_conv(u_c, conv_w, conv_b, ln_g, ln_b)
    return jnp.concatenate([y_c, attn], axis=-1) @ w_out

def swiglu(h, w1, w3, w2):
    return (jax.nn.silu(h @ w1) * (h @ w3)) @ w2

def moe_swiglu(h, w_router, b_router, w1, w3, w2):
    logits = (h @ w_router).astype(jnp.float32) + b_router.astype(jnp.float32)
    top_v, top_i = lax.top_k(logits, TOP_K)
    gates = jax.nn.softmax(top_v, axis=-1)
    combine = jnp.sum(jax.nn.one_hot(top_i, N_EXPERTS, dtype=jnp.float32) * gates[..., None], axis=-2)
    combine = combine.astype(h.dtype)
    out = jnp.zeros_like(h)
    for e in range(N_EXPERTS):
        out = out + combine[..., e:e + 1] * swiglu(h, w1[e], w3[e], w2[e])
    return out

def setup_inputs(seed: int = 0) -> dict:
    key = jax.random.key(seed)
    ks = iter(jax.random.split(key, 64))
    f32 = jnp.float32

    def nrm(shape, scale):
        return jax.random.normal(next(ks), shape, f32) * scale

    def gain(shape):
        return 1.0 + nrm(shape, 0.02)

    D = D_MODEL
    u = jax.random.uniform(next(ks), (N_EVEN, 2, D_A), f32, minval=0.9, maxval=0.999)
    a0 = u ** (1.0 / A_C)
    lam = jnp.log(a0) - jnp.log1p(-a0)
    return {
        'x_prompt': nrm((BATCH, SEQ, D), 1.0),
        'x_sample': nrm((DEC_BATCH, DEC_SEQ, D), 1.0),
        'c': nrm((DEC_BATCH, D), 1.0),
        'state_rglru': nrm((DEC_BATCH, N_EVEN, 2, D_A), 0.5),
        'cache_k': nrm((DEC_BATCH, N_ODD, PAST_LEN, N_KV_HEADS, HEAD_DIM), 1.0),
        'cache_v': nrm((DEC_BATCH, N_ODD, PAST_LEN, N_KV_HEADS, HEAD_DIM), 1.0),
        'c_ctx': nrm((D,), 1.0),
        'w_mod': nrm((DEPTH, D, 6 * D), 0.5 * D ** -0.5),
        'b_mod': nrm((DEPTH, 6 * D), 0.01),
        'norm1': gain((DEPTH, D)),
        'norm2': gain((DEPTH, D)),
        'ev_w_in': nrm((N_EVEN, D, D_IN_EVEN), D ** -0.5),
        'a_conv_w': nrm((N_EVEN, A_CONV, D_A), A_CONV ** -0.5),
        'a_conv_b': nrm((N_EVEN, D_A), 0.01),
        'a_w_r': nrm((N_EVEN, 2, A_BLOCKS, A_BS, A_BS), A_BS ** -0.5),
        'a_b_r': nrm((N_EVEN, 2, D_A), 0.01),
        'a_w_i': nrm((N_EVEN, 2, A_BLOCKS, A_BS, A_BS), A_BS ** -0.5),
        'a_b_i': nrm((N_EVEN, 2, D_A), 0.01),
        'a_lam': lam,
        'b_w_pool': nrm((N_EVEN, B_GROUPS, B_GS, B_GS), B_GS ** -0.5),
        'b_scale': gain((N_EVEN, D_B)),
        'ev_w_out': nrm((N_EVEN, D, D), D ** -0.5),
        'od_w_in': nrm((N_ODD, D, D_IN_ODD), D ** -0.5),
        'c_conv_w': nrm((N_ODD, C_CONV, D_C), C_CONV ** -0.5),
        'c_conv_b': nrm((N_ODD, D_C), 0.01),
        'c_ln_g': gain((N_ODD, D_C)),
        'c_ln_b': nrm((N_ODD, D_C), 0.01),
        'q_norm': gain((N_ODD, HEAD_DIM)),
        'k_norm': gain((N_ODD, HEAD_DIM)),
        'od_w_out': nrm((N_ODD, D, D), D ** -0.5),
        'ff_w1': nrm((N_EVEN, D, D_FF), D ** -0.5),
        'ff_w3': nrm((N_EVEN, D, D_FF), D ** -0.5),
        'ff_w2': nrm((N_EVEN, D_FF, D), D_FF ** -0.5),
        'moe_w_router': nrm((N_ODD, D, N_EXPERTS), D ** -0.5),
        'moe_b_router': nrm((N_ODD, N_EXPERTS), 0.01),
        'moe_w1': nrm((N_ODD, N_EXPERTS, D, D_FF_E), D ** -0.5),
        'moe_w3': nrm((N_ODD, N_EXPERTS, D, D_FF_E), D ** -0.5),
        'moe_w2': nrm((N_ODD, N_EXPERTS, D_FF_E, D), D_FF_E ** -0.5),
        'norm_f': gain((D,)),
    }

def reference(x_prompt, x_sample, c, state_rglru, cache_k, cache_v, c_ctx, w_mod, b_mod,
              norm1, norm2, ev_w_in, a_conv_w, a_conv_b, a_w_r, a_b_r, a_w_i, a_b_i, a_lam,
              b_w_pool, b_scale, ev_w_out, od_w_in, c_conv_w, c_conv_b, c_ln_g, c_ln_b,
              q_norm, k_norm, od_w_out, ff_w1, ff_w3, ff_w2, moe_w_router, moe_b_router,
              moe_w1, moe_w3, moe_w2, norm_f):
    xp, xs = x_prompt, x_sample
    Bp = xp.shape[0]
    Ts = xs.shape[1]
    rope_cos, rope_sin = axial_rope_tables(Ts)
    h0_ctx = jnp.zeros((Bp, 2, D_A), xp.dtype)
    new_states, new_k, new_v = [], [], []
    for layer in range(DEPTH):
        li = layer // 2
        mp = ada_params(c_ctx, w_mod[layer], b_mod[layer])
        ms = [m[:, None, :] for m in ada_params(c, w_mod[layer], b_mod[layer])]
        hp = modulate(rms_norm(xp, norm1[layer]), mp[0], mp[1])
        hs = modulate(rms_norm(xs, norm1[layer]), ms[0], ms[1])
        if layer % 2 == 0:
            ev = (ev_w_in[li], a_conv_w[li], a_conv_b[li], a_w_r[li], a_b_r[li], a_w_i[li],
                  a_b_i[li], a_lam[li], b_w_pool[li], b_scale[li], ev_w_out[li])
            yp, h_ctx = even_mixer(hp, h0_ctx, *ev)
            ys, _ = even_mixer(hs, state_rglru[:, li], *ev)
            new_states.append(h_ctx)
        else:
            u_p, q_p, k_p, v_p = odd_project(hp, od_w_in[li], q_norm[li], k_norm[li])
            att_p = block_attention(q_p, k_p, v_p)
            yp = odd_output(u_p, att_p, c_conv_w[li], c_conv_b[li], c_ln_g[li], c_ln_b[li], od_w_out[li])
            new_k.append(k_p)
            new_v.append(v_p)
            u_s, q_s, k_s, v_s = odd_project(hs, od_w_in[li], q_norm[li], k_norm[li])
            q_s = apply_axial_rope(q_s, rope_cos, rope_sin)
            k_s = apply_axial_rope(k_s, rope_cos, rope_sin)
            k_all = jnp.concatenate([cache_k[:, li].astype(k_s.dtype), k_s], axis=1)
            v_all = jnp.concatenate([cache_v[:, li].astype(v_s.dtype), v_s], axis=1)
            att_s = block_attention(q_s, k_all, v_all)
            ys = odd_output(u_s, att_s, c_conv_w[li], c_conv_b[li], c_ln_g[li], c_ln_b[li], od_w_out[li])
        xp = xp + mp[2] * yp
        xs = xs + ms[2] * ys
        hp = modulate(rms_norm(xp, norm2[layer]), mp[3], mp[4])
        hs = modulate(rms_norm(xs, norm2[layer]), ms[3], ms[4])
        if layer % 2 == 0:
            fp = swiglu(hp, ff_w1[li], ff_w3[li], ff_w2[li])
            fs = swiglu(hs, ff_w1[li], ff_w3[li], ff_w2[li])
        else:
            fp = moe_swiglu(hp, moe_w_router[li], moe_b_router[li], moe_w1[li], moe_w3[li], moe_w2[li])
            fs = moe_swiglu(hs, moe_w_router[li], moe_b_router[li], moe_w1[li], moe_w3[li], moe_w2[li])
        xp = xp + mp[5] * fp
        xs = xs + ms[5] * fs
    y_prompt = rms_norm(xp, norm_f)
    y_sample = rms_norm(xs, norm_f)
    return (y_prompt, y_sample, jnp.stack(new_states, axis=1), jnp.stack(new_k, axis=1), jnp.stack(new_v, axis=1))


_drawn_inputs = setup_inputs


def setup_inputs(seed=0):
    import zlib

    import numpy as np

    out = dict(_drawn_inputs(seed))
    spreads = {}
    factors = {'cache_k': 8.0,
     'cache_v': 6.149,
     'norm1': 2.837,
     'norm2': 3.842,
     'a_b_r': 31.812,
     'a_b_i': 22.61,
     'b_scale': 8.0,
     'c_conv_b': 34.127,
     'c_ln_g': 64.0,
     'c_ln_b': 200.0,
     'q_norm': 34.396,
     'k_norm': 20.261,
     'moe_b_router': 22.404,
     'norm_f': 23.405,
     'a_conv_b': 3.087}
    for name, (base, spread) in spreads.items():
        noise = np.random.default_rng([zlib.crc32(name.encode()), seed]).standard_normal(out[name].shape)
        drawn = base * np.exp(spread * noise) if base else spread * noise
        out[name] = __import__('jax').numpy.asarray(drawn.astype(out[name].dtype))
    for name, factor in factors.items():
        out[name] = (out[name] * factor).astype(out[name].dtype)
    return out
```

```python
from contextlib import ExitStack

import numpy as np

import concourse.bass as bass
from concourse import mybir

F32 = mybir.dt.float32
F32R = mybir.dt.float32r
I32 = mybir.dt.int32
U32 = mybir.dt.uint32
ALU = mybir.AluOpType
ACT = mybir.ActivationFunctionType
AX_X = mybir.AxisListType.X
AX_XY = mybir.AxisListType.XY

P = 128
D = 1024
KT = D // P
TP, TS = 128, 512
T = TP + TS
TT = T // P
TH = T // 2
EPS = 1e-6
HALF_SEGS = [[(0, TP, 0), (TP, TH, 1)], [(TH, T, 1)]]
SEGS = [(0, TP, 0), (TP, T, 1)]

D_A = 512
NC = D_A // P
A_CONV = 4
C_CONV = 31
WINDOWS = (2, 4, 8, 16)
D_FF, D_FFE = 2816, 1408
JT = D_FFE // P
NE = 8
HD = 64
NH = 8
PAST = 128

UA_P, UA_S, UA_W = 2, 133, 646
UB_P, UB_S, UB_W = 8, 144, 664
GC_P, GC_S, GC_W = 15, 158, 685
PADW = 664

N_MOD = 24
N_ITEM = JT + KT
AB_ITEM = (N_ITEM - 1) // 2
M0, EIN, EOUT, FF, M1, OIN, OOUT, MOE = 0, 24, 30, 34, 72, 96, 103, 107
AB = {M0: 0, EIN: 12, EOUT: 15, FF: 17, M1: 35, OIN: 47, OOUT: 53, MOE: 57}
CC = {FF: 0, OIN: 2, MOE: 3}
A_SLOT, B_SLOT, C_SLOT = 0, 1, 2
JH = 6
WHOLE = (slice(0, D), slice(D, 2 * D))
DOWN = (slice(0, JH * P), slice(D, D + (JT - JH) * P))

N1, N2 = 96, 112
NF, ACW, ACB, BR, BI, LAM, BSC, CCB, LNG, LNB, CS, CX, ST, QN, KN = (
    0, 8, 24, 28, 36, 44, 52, 56, 60, 64, 68, 76, 84, 92, 93)
SIZES = ((192, 1), (256, 1), (TH, 1), (TH, 2))
TILES = (2, 2, 3, TT)
Y_TILES = 2 * NE + 3 * (TILES[3] - 2) + (TILES[2] - 2)
IDENT, BEFORE, SWAP = range(3)


def hybrid_trunk_step(nc, a):
    ctx = ExitStack()
    with ctx:
        def sem(name):
            return ctx.enter_context(nc.semaphore(name))

        here = [16512]

        def place(name, shape, dt=F32, at=None):
            size = 4
            for n in shape[1:]:
                size *= n
            off = here[0] if at is None else at
            if at is None:
                here[0] += (size + 31) // 32 * 32
            return nc.alloc_sbuf_tensor_at(name, shape, dt, offset=off)

        xT = place("xT", [P, KT, T])
        hh = place("hh", [P, KT, T], F32R)
        at_hl = here[0]
        hl = place("hl", [P, KT, T], F32R)
        raw, hi, lo = [], [], []
        for s in range(3):
            at_raw = here[0]
            raw.append(place(f"raw{s}", [P, 2048]))
            at_hi = here[0]
            hi.append(place(f"hi{s}", [P, 2048], F32R))
            lo.append(place(f"lo{s}", [P, 2048], F32R))
        wg = place("wg", [P, 16, P], at=at_raw)
        yf = place("yf", [P, NC, T], at=at_hi)
        wp = place("wp", [P, NC, P], at=at_hi + 4 * NC * T)
        ii = place("ii", [P, NC, T], at=at_hl)

        mats = place("mats", [P, 3, P])
        ones = place("ones", [P, P])
        par = place("par", [P, 3, P])
        mod = place("mod", [P, 2, 48, 2])
        amod = place("amod", [P, 2, 2, KT, 2])
        cs = place("cs", [P, 2, KT])
        cs_hl = place("cs_hl", [P, KT, 4], F32R)
        cs_h0 = place("cs_h0", [P, KT, 4], F32R)
        sel4 = place("sel4", [4, 2])
        rs = place("rs", [P, T])
        tmp = place("tmp", [P, 4, PADW])
        sm = place("sm", [P, 16, 8])
        edge = place("edge", [P, NC, 16])
        zeros = place("zeros", [P, P])
        wr_raw = place("wr_raw", [P, KT, NE])
        wr_hi = place("wr_hi", [P, KT, NE], F32R)
        wr_lo = place("wr_lo", [P, KT, NE], F32R)
        iota8 = place("iota8", [P, NE])
        brow = place("brow", [P, NE])
        tok_id = place("tok_id", [P, TT])
        slots = place("slots", [P, TT, 2], I32)
        ids = place("ids", [P, NE, TT], I32)
        ids_now = place("ids_now", [P, TT], I32)
        slot_w = place("slot_w", [P, NE, TT])
        size_of = place("size_of", [1, NE], I32)
        tiles_before = place("tiles_before", [1, NE], I32)
        tiles_after = place("tiles_after", [1, NE], I32)
        scratch = here[0]

        xrows = place("xrows", [P, TT, D], at=scratch)
        mrow = place("mrow", [4, N_MOD, 256], at=scratch + 4 * TT * D)
        prow = place("prow", [P, 3, P], at=scratch + 4 * TT * D + 4 * 6144)
        off = scratch
        up = place("up", [P, NC, 648], at=off)
        off += 4 * NC * 648
        xc = place("xc", [P, NC, 648], at=off)
        off += 4 * NC * 648
        ga = place("ga", [P, NC, T], at=off)
        off += 4 * NC * T
        ub = place("ub", [P, NC, UB_W], at=off)
        off += 4 * NC * UB_W
        rr = place("rr", [P, NC, T], at=off)
        off += 4 * NC * T
        th = up
        top = off
        g_hi = place("g_hi", [P, JT, T], F32R, at=scratch)
        g_lo = place("g_lo", [P, JT, T], F32R, at=scratch + 4 * JT * T)
        top = max(top, scratch + 8 * JT * T)
        off = scratch
        vp = place("vp", [P, NC, 656], at=off)
        off += 4 * NC * 656
        gp = place("gp", [P, NC, 688], at=off)
        off += 4 * NC * 688
        qf = place("qf", [P, NC, T], at=off)
        off += 4 * NC * T
        mrow1 = place("mrow1", [4, N_MOD, 256], at=scratch)
        kf = place("kf", [P, T], at=off)
        off += 4 * T
        vf = place("vf", [P, T], at=off)
        off += 4 * T
        pp = place("pp", [P, 2, T], at=off)
        hspread = place("hspread", [10, 5, P], at=off)
        hrs = place("hrs", [10, T], at=off + 4 * T)
        off += 8 * T
        kk = place("kk", [P, T], at=off)
        off += 4 * T
        vt = place("vt", [P, 6, P], at=off)
        off += 24 * P
        cos_t = place("cos_t", [P, TS], at=off)
        off += 4 * TS
        sin_t = place("sin_t", [P, TS], at=off)
        off += 4 * TS
        krow = place("krow", [P, P], at=off)
        off += 4 * P
        knew = place("knew", [P, P], at=off)
        off += 4 * P
        hsel = place("hsel", [P, 5, 16], at=off)
        off += 320
        am = place("am", [P, 4, 2], at=off)
        off += 32
        top = max(top, off)
        pt = place("pt", [P, 2, 5, TS], at=at_raw)
        ptp = place("ptp", [P, 2, P], at=at_raw + 40 * TS)
        hf = place("hf", [P, KT, T], at=scratch)
        hrows = place("hrows", [P, TT, D], at=scratch + 4 * KT * T)
        iota_t = place("iota_t", [P, T], at=scratch + 8 * KT * T)
        hot = [place("hot0", [P, TT, T], F32R, at=scratch + 8 * KT * T + 4 * T),
               place("hot1", [P, TT, T], F32R, at=scratch)]
        top = max(top, scratch + 8 * KT * T + 4 * T + 4 * TT * T)
        scratch_end, here[0] = here[0], at_hi + 8192
        lg = place("lg", [P, TT, NE])
        mx8 = place("mx8", [P, TT, 8])
        ix8 = place("ix8", [P, TT, 8], U32)
        ixf = place("ixf", [P, TT, 2])
        gw = place("gw", [P, TT, 2])
        comb = place("comb", [P, TT, NE])
        members = place("members", [P, 2, TT, NE])
        both = place("both", [P, TT, NE])
        rank = place("rank", [P, TT, NE])
        slotf = place("slotf", [P, TT, 2])
        tok_w = place("tok_w", [P, TT, NE, 4], F32R)
        base8 = place("base8", [P, NE])
        cnt = place("cnt", [P, 6, NE])
        here[0] = scratch_end
        rows_g = place("rows_g", [P, 2, D], at=at_raw)
        rows_y = place("rows_y", [P, 2, TT, P], at=at_hi)
        yb = place("yb", [P, 2, T], at=at_hi + 8192)
        rows_c = place("rows_c", [P, TT, 2, D], at=scratch)
        yrows = place("yrows", [P, TT, D], at=scratch)
        h_dram = nc.dram_tensor("h_rows", (T, D), F32).ap()
        y_dram = nc.dram_tensor("y_rows", (Y_TILES, P, D), F32).ap()
        assert top <= nc.sbuf_usable_end, (top, nc.sbuf_usable_end)

        ps = ctx.enter_context(nc.psum_tensor("ps", [P, 8, 512], F32))

        x_in = sem("x_in")
        rows_in = sem("rows_in")
        mats_in = sem("mats_in")
        small_in = sem("small_in")
        slot_in = [[sem(f"slot_{s}{h}_in") for h in range(2)] for s in "abc"]
        stored = sem("stored")
        hi_done = sem("hi_done")
        lo_done = sem("lo_done")
        gemm_out = sem("gemm_out")
        evac = sem("evac")
        prow_zero = sem("prow_zero")
        ones_set = sem("ones_set")
        x_turned = sem("x_turned")
        x_kept = sem("x_kept")
        par_turned = sem("par_turned")
        par_kept = sem("par_kept")
        cs_silu = sem("cs_silu")
        cs_split = sem("cs_split")
        csz = sem("csz")
        folded = sem("folded")
        mod_set = sem("mod_set")
        n_sq = sem("n_sq")
        n_mm = sem("n_mm")
        n_var = sem("n_var")
        n_std = sem("n_std")
        n_rs = sem("n_rs")
        n_t = sem("n_t")
        n_aff = sem("n_aff")
        n_hi = sem("n_hi")
        n_lo = sem("n_lo")
        pads = sem("pads")
        ab_lam = sem("ab_lam")
        ex_lam = sem("ex_lam")
        sp_ready = sem("sp_ready")
        chain = sem("chain")
        e_xc = sem("e_xc")
        e_pool = sem("e_pool")
        e_pmm = sem("e_pmm")
        e_gate = sem("e_gate")
        e_sig = sem("e_sig")
        e_tanh = sem("e_tanh")
        e_exp = sem("e_exp")
        e_a2 = sem("e_a2")
        e_q = sem("e_q")
        e_sqrt = sem("e_sqrt")
        e_scan = sem("e_scan")
        e_y = sem("e_y")
        e_yhi = sem("e_yhi")
        e_ylo = sem("e_ylo")
        st_last = sem("st_last")
        st_turned = sem("st_turned")
        st_kept = sem("st_kept")
        odd_in = sem("odd_in")
        gp_pads = sem("gp_pads")
        gp_set = sem("gp_set")
        o_sq = sem("o_sq")
        o_sum = sem("o_sum")
        o_var = sem("o_var")
        o_std = sem("o_std")
        o_rs = sem("o_rs")
        o_spread = sem("o_spread")
        o_qn = sem("o_qn")
        o_swap = sem("o_swap")
        o_sw_read = sem("o_sw_read")
        o_rope = sem("o_rope")
        v_turned = sem("v_turned")
        v_kept = sem("v_kept")
        c_dve = sem("c_dve")
        c_pool = sem("c_pool")
        pchain = sem("pchain")
        kv_stored = sem("kv_stored")
        a_s = sem("a_s")
        a_max = sem("a_max")
        a_exp = sem("a_exp")
        a_norm = sem("a_norm")
        a_t = sem("a_t")
        a_kept = sem("a_kept")
        a_kept5 = sem("a_kept5")
        a_pv = sem("a_pv")
        a_ohi = sem("a_ohi")
        a_olo = sem("a_olo")
        l_mean = sem("l_mean")
        l_xc = sem("l_xc")
        l_sq = sem("l_sq")
        l_vmm = sem("l_vmm")
        l_var = sem("l_var")
        l_std = sem("l_std")
        l_y = sem("l_y")
        l_silu = sem("l_silu")
        l_hi = sem("l_hi")
        l_lo = sem("l_lo")
        wr_h = sem("wr_h")
        wr_l = sem("wr_l")
        r_mm = sem("r_mm")
        r_members = sem("r_members")
        r_ranks = sem("r_ranks")
        r_d = sem("r_d")
        r_exp = sem("r_exp")
        r_tables = sem("r_tables")
        r_hot = sem("r_hot")
        r_info = sem("r_info")
        r_ids = sem("r_ids")
        ht_turned = sem("ht_turned")
        ht_kept = sem("ht_kept")
        iota_in = sem("iota_in")
        zeros_set = sem("zeros_set")
        y_zero = sem("y_zero")
        ids_copied = sem("ids_copied")
        g_rows = sem("g_rows")
        g_turned = sem("g_turned")
        g_hi_kept = sem("g_hi_kept")
        g_lo_kept = sem("g_lo_kept")
        y_turned = sem("y_turned")
        y_rows = sem("y_rows")
        out_rows = [sem("out_rows_a"), sem("out_rows_b")]
        h_stored = sem("h_stored")
        c_rows = [sem(f"c_rows_{t}") for t in range(TT)]
        c_sum = sem("c_sum")
        c_turned = sem("c_turned")
        c_added = sem("c_added")
        z_y = sem("z_y")
        z_turned = sem("z_turned")
        z_kept = sem("z_kept")
        f_silu = sem("f_silu")
        f_hi = sem("f_hi")
        f_lo = sem("f_lo")

        OIN_NEXT = [(C_SLOT, OIN + 2, CC[OIN]), (A_SLOT, OIN + 3, AB[OIN] + 4), (B_SLOT, OIN + 4, AB[OIN] + 4),
                    (A_SLOT, OIN + 5, AB[OIN] + 5), (B_SLOT, OIN + 6, AB[OIN] + 5),
                    (A_SLOT, OOUT, AB[OOUT] + 1), (B_SLOT, OOUT + 1, AB[OOUT] + 1)]

        block = ctx.enter_context(nc.Block())
        ident = mats[:, IDENT, :]

        def sil(h, width=TH):
            return tmp[:, h, 0:width]

        def gf(h, width=TH):
            return tmp[:, 2 + h, 0:width]

        def wait_apart(eng, signal, value):
            value = eng.snap(eng.to_reg(value))
            eng.wait_ge(mats_in, 16)
            eng.wait_ge(signal, value)

        def gather_tiles(width, halves):
            total = T if halves == 2 else width
            return [(g, min(P, total - P * g)) for g in range((total + P - 1) // P)]

        def gate_of(layer, which, m, c):
            return mod[:, layer, 16 + 24 * which + m, c:c + 1] if isinstance(m, int) else \
                mod[:, layer, bass.ds(16 + 24 * which + m, 1), c:c + 1].rearrange("p a b -> p (a b)")

        @block.sync
        def _(sp):
            def load(slot, use, raw_free, pieces):
                for i, (dst, src) in enumerate(pieces):
                    part = 2 * i // len(pieces)
                    if raw_free is not None and i in (0, len(pieces) // 2):
                        sp.wait_ge(mats_in, 16)
                        sp.wait_ge(lo_done, raw_free - 1 + part)
                    sp.dma_start(dst, src).then_inc(slot_in[slot][part], 16)

            def columns(w, col, n=256):
                v = w.rearrange("(k p) c -> p k c", p=P)
                h = KT // 2
                return lambda slot: [
                    (raw[slot][:, i * h * n:(i + 1) * h * n].rearrange("p (k c) -> p k c", k=h),
                     v[:, i * h:(i + 1) * h, bass.ds(col, n)]) for i in range(2)]

            def pairs(stage, n_pairs, src, first_free=True):
                def one(q, slot, free):
                    load(slot, 0, free, src(q)(slot))
                if not first_free:
                    one(0, A_SLOT, None)
                    one(1, B_SLOT, None)
                with sp.Fori(0 if first_free else 1, n_pairs) as pr:
                    for u in range(2):
                        one(2 * pr + u, u, 2 * (stage - 1) + 4 * pr + 2 * u)

            def item(w1, w3, w2, col, row, n):
                def up_proj(j, slot):
                    return [(raw[slot][:, i * D:(i + 1) * D].rearrange("p (k c) -> p k c", k=KT),
                             w.rearrange("(k p) c -> p k c", p=P)[:, :, bass.ds(col + j * P, P)])
                            for i, w in enumerate((w1, w3))]

                def down_proj(m, slot):
                    v = w2.rearrange("(k p) c -> p k c", p=P)
                    return [(raw[slot][:, at:at + (k1 - k0) * P].rearrange("p (k c) -> p k c", k=k1 - k0),
                             v[:, bass.ds(row + k0, k1 - k0), bass.ds(m * P, P)]) for k0, k1, at in ((0, JH, 0), (JH, JT, D))]

                with sp.Fori(0, JT // 2) as pr:
                    for u in range(2):
                        load(u, 0, 2 * (n - 1) + 4 * pr + 2 * u, up_proj(2 * pr + u, u))
                load(C_SLOT, 0, 2 * (n + JT - 2), up_proj(JT - 1, C_SLOT))
                load(A_SLOT, 0, 2 * (n + JT - 2), down_proj(0, A_SLOT))
                load(B_SLOT, 0, 2 * (n + JT - 1), down_proj(1, B_SLOT))
                with sp.Fori(1, KT // 2) as pr:
                    for u in range(2):
                        load(u, 0, 2 * (n + JT - 1) + 4 * pr + 2 * u, down_proj(2 * pr + u, u))

            for i in range(2):
                load(i, 0, None, columns(a["w_mod"][0], i * 256)(i))
            with sp.Fori(1, N_MOD // 2) as pr:
                for u in range(2):
                    load(u, 0, 4 * pr + 2 * u - 2, columns(a["w_mod"][0], (2 * pr + u) * 256)(u))
            pairs(EIN, 3, lambda q: columns(a["ev_w_in"][0], q * 256))
            pairs(EOUT, 2, lambda q: columns(a["ev_w_out"][0], q * 256))
            with sp.Fori(0, 2) as f:
                item(a["ff_w1"][0], a["ff_w3"][0], a["ff_w2"][0], f * D_FFE, f * JT, FF + N_ITEM * f)

            pairs(M1, N_MOD // 2, lambda q: columns(a["w_mod"][1], q * 256))

            sp.wait_ge(evac, 2 * M1)
            sp.dma_start(cos_t[:, :], a["const_cos"]).then_inc(odd_in, 16)
            sp.dma_start(sin_t[:, :], a["const_sin"]).then_inc(odd_in, 16)
            sp.dma_start(krow[:, :], a["cache_k"][0, 0].rearrange("t h d -> t (h d)")).then_inc(odd_in, 16)
            sp.dma_start(vt[:, 1, :], a["cache_v"][0, 0].rearrange("t h d -> t (h d)")).then_inc(odd_in, 16)
            sp.dma_start(hsel[:, :, :], a["const_hsel"]).then_inc(odd_in, 16)
            sp.dma_start(hspread[:, :, :], a["const_hspread"]).then_inc(odd_in, 16)

            w = a["od_w_in"][0]
            wv = w.rearrange("(k p) c -> p k c", p=P)

            def q_columns(slot, c):
                dst = raw[slot][:, :].rearrange("p (k j e d) -> p k j e d", k=KT, j=2, e=2)
                src = wv[:, :, 2 * D_A:2 * D_A + 512].rearrange("p k (e j d) -> p k e j d", e=2, j=4)
                return [(dst[:, k:k + 4, j, e, :], src[:, k:k + 4, e, 2 * c + j, :]) for k in (0, 4) for j in range(2) for e in range(2)]

            load(A_SLOT, 0, 2 * (OIN - 1), q_columns(A_SLOT, 0))
            load(B_SLOT, 0, 2 * OIN, q_columns(B_SLOT, 1))
            load(C_SLOT, 0, None, columns(w, 2 * D_A + 512)(C_SLOT))
            for c in range(3, 7):
                load((c - 3) % 2, 0, 2 * (OIN + (0, 1, 3, 4)[c - 3] + 1), columns(w, (c - 3) * 256)((c - 3) % 2))

            wo = a["od_w_out"][0]

            def out_columns(slot, c):
                v = wo[0:D_A, :].rearrange("(k p) c -> p k c", p=P)
                u = wo[D_A:D, :].rearrange("(e k d) c -> e d k c", e=2, d=HD)
                dst = raw[slot][:, :].rearrange("p (k c) -> p k c", k=KT)
                cols = slice(c * 256, (c + 1) * 256)
                return [(dst[:, 0:2, :], v[:, 0:2, cols]), (dst[:, 2:4, :], v[:, 2:4, cols])] + [
                    (dst[e * HD:(e + 1) * HD, 4:8, :], u[e, :, :, cols]) for e in range(2)]

            for c in range(4):
                load(c % 2, 0, 2 * (OIN + (5, 6, 7, 8)[c] + 1), out_columns(c % 2, c))

            with sp.Fori(0, NE) as e:
                item(a["moe_w1"][0, bass.ds(e, 1)].rearrange("o a b -> (o a) b"), a["moe_w3"][0, bass.ds(e, 1)].rearrange("o a b -> (o a) b"),
                     a["moe_w2"][0, bass.ds(e, 1)].rearrange("o a b -> (o a) b"), 0, 0, MOE + N_ITEM * e)

            sp.wait_ge(st_kept, 1)
            sp.dma_start(a["new_state"].rearrange("b e n (c p) -> (b e n c) p", p=P), sm[0:8, 0:16, :].rearrange("p a b -> p (a b)")).then_inc(stored, 16)
            for t in range(TT):
                sp.wait_ge(z_kept, 2 * (t + 1))
                dst = a["y_prompt"][0] if t == 0 else a["y_sample"][0, (t - 1) * P:t * P, :]
                sp.dma_start(dst, yrows[:, t, :]).then_inc(stored, 16)
            sp.wait_ge(stored, 16 * (1 + TT))

        @block.scalar
        def _(act):
            for t in range(TT):
                src = a["x_prompt"][0] if t == 0 else a["x_sample"][0, (t - 1) * P:t * P, :]
                act.dma_start(xrows[:, t, :], src).then_inc(x_in, 16)
            act.dma_start(mats[:, :, :], a["const_mats"].rearrange("m p c -> p m c")).then_inc(mats_in, 16)
            act.wait_ge(prow_zero, 1)
            rows = [
                (0, 0, 96, a["b_mod"].rearrange("l (j p) -> (l j) p", p=P)),
                (0, N1, 16, a["norm1"].rearrange("l (j p) -> (l j) p", p=P)),
                (0, N2, 16, a["norm2"].rearrange("l (j p) -> (l j) p", p=P)),
                (1, NF, 8, a["norm_f"].rearrange("(j p) -> j p", p=P)),
                (1, ACW, 16, a["a_conv_w"][0].rearrange("t (c p) -> (t c) p", p=P)),
                (1, ACB, 4, a["a_conv_b"][0].rearrange("(c p) -> c p", p=P)),
                (1, BR, 8, a["a_b_r"][0].rearrange("n (c p) -> (n c) p", p=P)),
                (1, BI, 8, a["a_b_i"][0].rearrange("n (c p) -> (n c) p", p=P)),
                (1, LAM, 8, a["a_lam"][0].rearrange("n (c p) -> (n c) p", p=P)),
                (1, BSC, 4, a["b_scale"][0].rearrange("(c p) -> c p", p=P)),
                (1, CCB, 4, a["c_conv_b"][0].rearrange("(c p) -> c p", p=P)),
                (1, LNG, 4, a["c_ln_g"][0].rearrange("(c p) -> c p", p=P)),
                (1, LNB, 4, a["c_ln_b"][0].rearrange("(c p) -> c p", p=P)),
                (1, CS, 8, a["c"][0].rearrange("(c p) -> c p", p=P)),
                (1, CX, 8, a["c_ctx"].rearrange("(c p) -> c p", p=P)),
                (1, ST, 8, a["state_rglru"][0, 0].rearrange("n (c p) -> (n c) p", p=P)),
                (2, 0, 4 * C_CONV, a["c_conv_w"][0].rearrange("t (c p) -> (t c) p", p=P)),
            ]
            for s, r, n, src in rows:
                act.dma_start(prow[r:r + n, s, :], src).then_inc(rows_in, 16)
            for r, src in ((QN, a["q_norm"]), (KN, a["k_norm"])):
                for h in range(2):
                    act.dma_start(prow[r:r + 1, 1, h * HD:(h + 1) * HD], src).then_inc(rows_in, 16)
            act.dma_start(edge[:, :, :], a["const_edge"].rearrange("(o g) c -> o g c", o=1).to_broadcast([P, NC, 16])).then_inc(small_in, 16)
            act.dma_start(sel4[:, :], a["const_sel4"]).then_inc(small_in, 16)
            act.dma_start(iota8[:, :], a["const_iota"].to_broadcast([P, NE])).then_inc(small_in, 16)
            act.dma_start(tok_id[:, :], a["const_tok"]).then_inc(small_in, 16)
            act.dma_start(brow[:, :], a["moe_b_router"].to_broadcast([P, NE])).then_inc(small_in, 16)
            act.dma_start(wr_raw[:, :, :], a["moe_w_router"][0].rearrange("(k p) e -> p k e", p=P)).then_inc(small_in, 16)
            act.wait_ge(ones_set, 2)
            for i, w in enumerate((a["a_w_r"], a["a_w_i"])):
                v = w[0].rearrange("n (c e) k j -> e k n c j", e=2)
                for e in range(2):
                    for n in range(2):
                        act.dma_start(wg[e * 64:(e + 1) * 64, 8 * n + 4 * i:8 * n + 4 * i + 4, e * 64:(e + 1) * 64],
                                      v[e, :, n]).then_inc(small_in, 16)
            act.dma_start(wp[:, :, :], a["b_w_pool"][0].rearrange("g i j -> i g j")).then_inc(small_in, 16)

            def split_hi(slot, n, use, parts=WHOLE, fine=False):
                for h in range(2):
                    act.wait_ge(slot_in[slot][h], 16 * (use + 1))
                    act.wait_ge(gemm_out, 2 * (n - 2) + (h + 1 if fine else 2))
                    act.activation(hi[slot][:, parts[h]], raw[slot][:, parts[h]], ACT.Copy).then_inc(hi_done, 1)

            for s in range(2):
                for h in range(2):
                    act.wait_ge(slot_in[s][h], 16)
                    act.activation(hi[s][:, h * 1024:(h + 1) * 1024], raw[s][:, h * 1024:(h + 1) * 1024],
                                   ACT.Copy).then_inc(hi_done, 1)
            for g in range(1, 10, 2):
                act.wait_ge(x_turned, g + 1)
                act.wait_ge(x_kept, g)
                t, q = g // 2, g % 2
                act.activation(xT[:, 4 * q:4 * q + 4, t * P:(t + 1) * P],
                               ps[:, 1 + g % 3, :].rearrange("p (k c) -> p k c", k=4), ACT.Copy).then_inc(x_kept, 1)
            act.wait_ge(par_kept, 1)
            act.activation(cs[:, 0, :], par[:, 1, CX:CX + KT], ACT.Silu)
            act.activation(cs[:, 1, :], par[:, 1, CS:CS + KT], ACT.Silu).then_inc(cs_silu, 1)

            def mod_evac(slot, n, q, mrow=mrow):
                act.wait_ge(gemm_out, 2 * n + 2)
                act.activation(mrow[:, bass.ds(q, 1), :].rearrange("p a c -> p (a c)"), ps[0:4, 4 * slot, 0:256], ACT.Copy).then_inc(evac, 2)

            with act.Fori(0, N_MOD // 2) as pr:
                for u in range(2):
                    n = 2 * pr + u
                    mod_evac(u, n, n)
                    split_hi(u, n + 2, pr + 1, fine=True)
            act.wait_ge(ab_lam, 1)
            act.activation(sm[:, 1, :], sm[:, 0, :], ACT.Exp, scale=-1.0).then_inc(ex_lam, 1)

            def norm_act(i, h=None):
                for k in range(KT):
                    if k >= 2:
                        act.wait_ge(n_mm, KT * i + k - 1)
                    elif i:
                        act.wait_ge(n_lo, KT * i)
                    act.activation(tmp[:, k % 2, 0:T], xT[:, k, :], ACT.Square).then_inc(n_sq, 1)
                act.wait_ge(n_var, i + 1)
                act.activation(rs[:, :], rs[:, :], ACT.Sqrt).then_inc(n_std, 1)
                for k in range(KT):
                    act.wait_ge(n_aff, KT * i + k + 1)
                    act.activation(hh[:, k, :], tmp[:, k % 2, 0:T] if h is None else h[:, k, :], ACT.Copy).then_inc(n_hi, 1)

            act.wait_ge(small_in, 16 * 15)
            act.activation(wr_hi[:, :, :], wr_raw[:, :, :], ACT.Copy).then_inc(wr_h, 1)
            act.wait_ge(x_kept, 10)
            norm_act(0)

            act.wait_ge(pads, 2)
            for c in range(6):
                n, slot = EIN + c, c % 2
                for h in range(2):
                    act.wait_ge(gemm_out, 2 * n + h + 1)
                    for i in range(2):
                        m = 2 * c + i
                        last = None
                        for lo_t, hi_t, cond in HALF_SEGS[h]:
                            src = ps[:, 4 * slot + 2 * h + i, lo_t - TH * h:hi_t - TH * h]
                            s0, p0 = (0, TP)[cond], 0
                            if m < 4:
                                p0 = (UA_P, UA_S)[cond] + lo_t - s0
                                last = act.activation(up[:, m, p0:p0 + hi_t - lo_t], src, ACT.Copy)
                            elif m < 8:
                                last = act.activation(ga[:, m - 4, lo_t:hi_t], src, ACT.Gelu_apprx_tanh)
                            else:
                                p0 = (UB_P, UB_S)[cond] + lo_t - s0
                                last = act.activation(ub[:, m - 8, p0:p0 + hi_t - lo_t], src, ACT.Copy)
                    last.then_inc(evac, 1)
                split_hi(slot, n + 2, AB[EIN] + 1 + c // 2)

            for n in range(2):
                for c in range(NC):
                    it = NC * n + c
                    act.wait_ge(e_gate, it + 1)
                    if n:
                        act.wait_ge(e_scan, c + 1)
                    for kind, (dst, b) in enumerate(((rr, BR), (ii, BI))):
                        for (lo_t, hi_t, cond) in SEGS:
                            last = act.activation(dst[:, c, lo_t:hi_t], ps[:, 4 * (it % 2) + 2 * kind + cond, 0:hi_t - lo_t],
                                                  ACT.Sigmoid, bias=par[:, 1, b + it:b + it + 1])
                    last.then_inc(e_sig, 1)
                act.wait_ge(sp_ready, 1)
                for c in range(NC):
                    it = NC * n + c
                    act.wait_ge(e_sig, NC * (n + 1))
                    act.wait_ge(e_xc, NC)
                    if n:
                        act.wait_ge(e_scan, NC)
                    act.activation(th[:, c, 0:T], rr[:, c, :], ACT.Tanh, scale=sm[:, 6, it:it + 1]).then_inc(e_tanh, 1)
                    act.wait_ge(e_tanh, it + 1)
                    act.activation(rr[:, c, :], rr[:, c, :], ACT.Exp, scale=sm[:, 7, it:it + 1]).then_inc(e_exp, 1)
                for c in range(NC):
                    it = NC * n + c
                    act.wait_ge(e_q, it + 1)
                    act.activation(th[:, c, 0:T], th[:, c, 0:T], ACT.Sqrt).then_inc(e_sqrt, 1)
            for c in range(NC):
                act.wait_ge(e_y, c + 1)
                act.activation(hh[:, c, :], tmp[:, 2 + c % 2, 0:T], ACT.Copy).then_inc(e_yhi, 1)
            act.wait_ge(st_turned, 1)
            act.activation(sm[0:8, 0:16, :].rearrange("p a b -> p (a b)"), ps[0:8, 2, 0:P], ACT.Copy).then_inc(st_kept, 1)

            for c in range(4):
                split_hi(c % 2, EOUT + c + 2, (AB[EOUT] + 1 + c // 2) if c < 2 else AB[FF])
            act.wait_ge(evac, 2 * FF)
            norm_act(1)

            def ff13_evac(slot, n, j, f):
                for h in range(2):
                    act.wait_ge(gemm_out, 2 * n + h + 1)
                    act.activation(sil(h), ps[:, 4 * (slot % 2) + 2 * h, 0:TH], ACT.Silu).then_inc(f_silu, 1)
                for h in range(2):
                    act.wait_ge(evac, 2 * n + h + 1)
                    act.activation(g_hi[:, bass.ds(j, 1), h * TH:(h + 1) * TH].rearrange("p a c -> p (a c)"),
                                   gf(h), ACT.Copy).then_inc(f_hi, 1)

            with act.Fori(0, 2) as f:
                n0, u0 = FF + N_ITEM * f, AB[FF] + AB_ITEM * f
                with act.Fori(0, JT // 2 - 1) as pr:
                    for u in range(2):
                        ff13_evac(u, n0 + 2 * pr + u, 2 * pr + u, f)
                        split_hi(u, n0 + 2 * pr + u + 2, u0 + pr + 1)
                ff13_evac(A_SLOT, n0 + JT - 3, JT - 3, f)
                split_hi(C_SLOT, n0 + JT - 1, f)
                ff13_evac(B_SLOT, n0 + JT - 2, JT - 2, f)
                split_hi(A_SLOT, n0 + JT, u0 + JT // 2, DOWN)
                ff13_evac(C_SLOT, n0 + JT - 1, JT - 1, f)
                split_hi(B_SLOT, n0 + JT + 1, u0 + JT // 2, DOWN)
                with act.Fori(0, KT // 2 - 1) as pr:
                    for u in range(2):
                        split_hi(u, n0 + JT + 2 + 2 * pr + u, u0 + JT // 2 + 1 + pr, DOWN)
                for u in range(2):
                    split_hi(u, n0 + N_ITEM + u, u0 + AB_ITEM)

            act.wait_ge(evac, 2 * M1)
            with act.Fori(0, N_MOD // 2 - 1) as pr:
                for u in range(2):
                    mod_evac(u, M1 + 2 * pr + u, 2 * pr + u, mrow1)
                    split_hi(u, M1 + 2 * pr + u + 2, AB[M1] + pr + 1, fine=True)
            for u in range(2):
                mod_evac(u, M1 + N_MOD - 2 + u, N_MOD - 2 + u, mrow1)
                split_hi(u, OIN + u, AB[OIN] + 3, fine=True)
            norm_act(2)

            act.wait_ge(gp_pads, 1)
            for c in range(7):
                n = OIN + c
                for h in range(2):
                    act.wait_ge(gemm_out, 2 * n + h + 1)
                    for i in range(2):
                        bank = 4 * (c % 2) + 2 * h + i
                        if c < 3:
                            dst = (qf[:, 2 * c + i, :] if c < 2 else (kf, vf)[i])
                            last = act.activation(dst[:, h * TH:(h + 1) * TH] if c < 2 else dst[:, h * TH:(h + 1) * TH],
                                                  ps[:, bank, 0:TH], ACT.Copy)
                        elif c < 5:
                            last = act.activation(vp[:, 2 * (c - 3) + i, h * TH:(h + 1) * TH], ps[:, bank, 0:TH], ACT.Copy)
                        else:
                            for lo_t, hi_t, cond in HALF_SEGS[h]:
                                p0 = (GC_P, GC_S)[cond] + lo_t - (0, TP)[cond]
                                last = act.activation(gp[:, 2 * (c - 5) + i, p0:p0 + hi_t - lo_t],
                                                      ps[:, bank, lo_t - TH * h:hi_t - TH * h], ACT.Sigmoid)
                    last.then_inc(evac, 1)
                split_hi(*OIN_NEXT[c])

            act.wait_ge(n_lo, 3 * KT)
            for i in range(5):
                if i >= 2:
                    act.wait_ge(o_sum, i - 1)
                act.activation(tmp[:, i % 2, 0:T], qf[:, i, :] if i < 4 else kf[:, :], ACT.Square).then_inc(o_sq, 1)
            act.wait_ge(o_var, 1)
            act.activation(hrs[:, :], hrs[:, :], ACT.Sqrt).then_inc(o_std, 1)
            act.wait_ge(v_turned, 1)
            act.activation(vt[:, 2:6, :], ps[:, 4, 0:512].rearrange("p (a b) -> p a b", a=4), ACT.Copy).then_inc(v_kept, 1)

            def kept(s):
                h, t = s // TT, s % TT
                act.wait_ge(a_t, s + 1)
                if h >= 2:
                    act.wait_ge(a_pv, h - 1)
                if t == 0:
                    act.activation(ptp[:, h % 2, :], ps[:, 4, 0:P], ACT.Copy).then_inc(a_kept, 1)
                else:
                    act.activation(pt[:, h % 2, 0:4, (t - 1) * P:t * P], ps[:, 4, 0:512].rearrange("p (k c) -> p k c", k=4),
                                   ACT.Copy).then_inc(a_kept, 1)

            def head_hi(h):
                act.wait_ge(a_pv, h + 1)
                r = slice(HD * (h // 4), HD * (h // 4) + HD)
                act.activation(hh[r, 4 + h % 4, 0:TP], ps[r, 7, 0:TP], ACT.Copy)
                act.activation(hh[r, 4 + h % 4, TP:T], ps[r, 6, 0:TS], ACT.Copy).then_inc(a_ohi, 1)

            for s in range(NH * TT + 4):
                if s == 4:
                    act.wait_ge(v_kept, 2)
                    act.dma_start(a["new_k"][0, 0].rearrange("t h d -> t (h d)"), knew[:, :]).then_inc(kv_stored, 16)
                    act.dma_start(a["new_v"][0, 0].rearrange("t h d -> t (h d)"), vt[:, 0, :]).then_inc(kv_stored, 16)
                if s < NH * TT:
                    act.wait_ge(a_max, s + 1)
                    if s >= 2:
                        act.wait_ge(a_t, s - 1)
                    width = P if s % TT == 0 else T
                    src = ps[:, 2 * (s % 2), 0:P] if s % TT == 0 else ps[:, 2 * (s % 2):2 * (s % 2) + 2, 0:TH]
                    dst = pp[:, s % 2, 0:width] if s % TT == 0 else pp[:, s % 2, :].rearrange("p (a b) -> p a b", a=2)
                    act.activation(dst, src, ACT.Exp, scale=HD ** -0.5, bias=am[:, 1, s % 2:s % 2 + 1],
                                   accum_out=am[:, 2, s % 2:s % 2 + 1]).then_inc(a_exp, 1)
                if 2 <= s < NH * TT + 2:
                    kept(s - 2)
                if s >= 8 and (s - 3) % TT == 0:
                    head_hi((s - 8) // TT)
            for c in range(NC):
                act.wait_ge(l_xc, c + 1)
                if c >= 2:
                    act.wait_ge(l_vmm, c - 1)
                for lo_t, hi_t, cond in SEGS:
                    p0 = (0, GC_S - 15)[cond]
                    last = act.activation(tmp[:, c % 2, lo_t:hi_t], vp[:, c, p0:p0 + hi_t - lo_t], ACT.Square)
                last.then_inc(l_sq, 1)
            act.wait_ge(l_var, 1)
            act.activation(rs[:, :], rs[:, :], ACT.Sqrt).then_inc(l_std, 1)
            for c in range(NC):
                act.wait_ge(l_y, c + 1)
                if c >= 2:
                    act.wait_ge(l_lo, c - 1)
                elif c == 0:
                    act.wait_ge(l_vmm, NC)
                act.activation(tmp[:, c % 2, 0:T], tmp[:, 2 + c % 2, 0:T], ACT.Silu, scale=par[:, 1, LNG + c:LNG + c + 1],
                               bias=par[:, 1, LNB + c:LNB + c + 1]).then_inc(l_silu, 1)
                act.wait_ge(l_silu, c + 1)
                act.activation(hh[:, c, :], tmp[:, c % 2, 0:T], ACT.Copy).then_inc(l_hi, 1)

            for c in range(4):
                split_hi(c % 2, OOUT + c + 2, (AB[OOUT] + 3) if c < 2 else AB[MOE])
            act.wait_ge(evac, 2 * MOE)
            norm_act(3, hf)
            for g in range(2 * TT):
                act.wait_ge(ht_turned, g + 1)
                act.activation(hrows[:, g // 2, 512 * (g % 2):512 * (g % 2) + 512], ps[:, g % 4, :], ACT.Copy).then_inc(ht_kept, 1)
                if g == 3:
                    act.wait_ge(r_d, 1)
                    act.activation(gw[:, :, 1], gw[:, :, 1], ACT.Exp).then_inc(r_exp, 1)

            def tables(e):
                return (act.value_load(size_of[0:1, bass.ds(e, 1)], min_val=0, max_val=len(SIZES) - 1),
                        act.value_load(tiles_before[0:1, bass.ds(e, 1)], min_val=0, max_val=NE * TT))

            def w13(e, width, halves):
                n0, u0, f = MOE + N_ITEM * e, AB[MOE] + AB_ITEM * e, 2 + e

                fine = halves == 1

                def silu(slot, n):
                    for h in range(halves):
                        act.wait_ge(gemm_out, 2 * n + h + 1)
                        act.activation(sil(h, width), ps[:, 4 * (slot % 2) + 2 * h, 0:width], ACT.Silu).then_inc(f_silu, 2 // halves)

                def kept(n, j):
                    for h in range(halves):
                        act.wait_ge(evac, 2 * n + 2 // halves * (h + 1))
                        act.activation(g_hi[:, bass.ds(j, 1), h * TH:h * TH + width].rearrange("p a c -> p (a c)"),
                                       gf(h, width), ACT.Copy).then_inc(f_hi, 2 // halves)

                with act.Fori(0, JT // 2 - 1) as pr:
                    for u in range(2):
                        silu(u, n0 + 2 * pr + u)
                        split_hi(u, n0 + 2 * pr + u + 2, u0 + pr + 1, fine=fine)
                        kept(n0 + 2 * pr + u, 2 * pr + u)
                silu(A_SLOT, n0 + JT - 3)
                for u in range(2):
                    act.wait_ge(out_rows[u], 16 + 16 * KT * e)
                split_hi(C_SLOT, n0 + JT - 1, 3 + e)
                kept(n0 + JT - 3, JT - 3)
                silu(B_SLOT, n0 + JT - 2)
                split_hi(A_SLOT, n0 + JT, u0 + JT // 2, DOWN, fine=fine)
                kept(n0 + JT - 2, JT - 2)
                silu(C_SLOT, n0 + JT - 1)
                split_hi(B_SLOT, n0 + JT + 1, u0 + JT // 2, DOWN)
                kept(n0 + JT - 1, JT - 1)

            def gather(e, width, halves, before):
                for g, rows in gather_tiles(width, halves):
                    act.wait_ge(g_turned, before + g + 1)
                    act.activation(hh[:, :, g * P:g * P + rows].rearrange("p (a b) c -> p a b c", a=2),
                                   ps[:, 2 * (g % 2):2 * (g % 2) + 2, :].rearrange("p a (b c) -> p a b c", b=4)[:, :, :, 0:rows],
                                   ACT.Copy).then_inc(g_hi_kept, 1)

            def w2(e, width, halves, last):
                n0, u0 = MOE + N_ITEM * e, AB[MOE] + AB_ITEM * e
                fine = halves == 1

                def kept(u, n, m):
                    if m is not None:
                        act.wait_ge(y_turned, KT * e + m - 1)
                    for h in range(halves):
                        act.wait_ge(gemm_out, 2 * n + 2 // halves * (h + 1))
                        act.activation(yb[:, u, h * TH:h * TH + width], ps[:, 4 + 2 * u + h, 0:width], ACT.Copy).then_inc(evac, 2 // halves)

                for u in range(2):
                    split_hi(u, n0 + JT + 2 + u, u0 + JT // 2 + 1, DOWN, fine=fine)
                    kept(u, n0 + JT + u, None)
                with act.Fori(1, KT // 2 - 1) as pr:
                    for u in range(2):
                        split_hi(u, n0 + JT + 2 + 2 * pr + u, u0 + JT // 2 + 1 + pr, DOWN, fine=fine)
                        kept(u, n0 + JT + 2 * pr + u, 2 * pr + u)
                for u in range(2):
                    if not last:
                        split_hi(u, n0 + N_ITEM + u, u0 + AB_ITEM, fine=fine)
                    kept(u, n0 + N_ITEM - 2 + u, KT - 2 + u)

            def expert(e, size, last):
                for i, (width, halves) in enumerate(SIZES):
                    with act.If(size == i):
                        w13(e, width, halves)
                if not last:
                    size_next, before_next = tables(e + 1)
                    for i, (width, halves) in enumerate(SIZES):
                        with act.If(size_next == i):
                            gather(e + 1, width, halves, before_next)
                for i, (width, halves) in enumerate(SIZES):
                    with act.If(size == i):
                        w2(e, width, halves, last)

            act.wait_ge(r_tables, 1)
            size, before = tables(0)
            for i, (width, halves) in enumerate(SIZES):
                with act.If(size == i):
                    gather(0, width, halves, before)
            with act.Fori(0, NE - 1) as e:
                expert(e, tables(e)[0], False)
            expert(NE - 1, tables(NE - 1)[0], True)

            for k in range(KT):
                act.wait_ge(c_added, KT * (TT - 1) + k + 1)
                if k >= 2:
                    act.wait_ge(n_mm, KT * 4 + k - 1)
                act.activation(tmp[:, k % 2, 0:T], xT[:, k, :], ACT.Square).then_inc(n_sq, 1)
            act.wait_ge(n_var, 5)
            act.activation(rs[:, :], rs[:, :], ACT.Sqrt).then_inc(n_std, 1)
            for g in range(1, 2 * TT, 2):
                act.wait_ge(z_turned, g + 1)
                act.wait_ge(z_kept, g)
                act.activation(yrows[:, g // 2, 512 * (g % 2):512 * (g % 2) + 512], ps[:, g % 4, :], ACT.Copy).then_inc(z_kept, 1)

        @block.tensor
        def _(pe):
            def passes(out, w_hi, w_lo, v_hi, v_lo, first, last):
                pe.matmul(out, w_hi, v_hi, start=first, stop=False, skip_group_check=True)
                pe.matmul(out, w_hi, v_lo, start=False, stop=False, skip_group_check=True)
                return pe.matmul(out, w_lo, v_hi, start=False, stop=last, skip_group_check=True)

            def begin(n):
                pe.wait_ge(lo_done, 2 * n + 1)
                pe.wait_ge(evac, 2 * (n - 1))

            def second(n):
                pe.wait_ge(lo_done, 2 * n + 2)

            def down(slot, k, of):
                at = k * P if k < JH else D + (k - JH) * P
                return of[slot][:, at:at + P]

            def mod_chunk(slot, n):
                wh = hi[slot][:, :].rearrange("p (k c) -> p k c", k=KT)
                wl = lo[slot][:, :].rearrange("p (k c) -> p k c", k=KT)
                for k in range(KT):
                    if k == KT // 2:
                        last.then_inc(gemm_out, 1)
                        second(n)
                    pe.matmul(ps[0:4, 4 * slot, 0:256], cs_hl[:, k, :], wh[:, k, :], start=k == 0, stop=False, skip_group_check=True)
                    last = pe.matmul(ps[0:4, 4 * slot, 0:256], cs_h0[:, k, :], wl[:, k, :], start=False, stop=k == KT - 1, skip_group_check=True)
                last.then_inc(gemm_out, 1)

            def gemm_pair(slot, n, ready=None, bank=None):
                wh = hi[slot][:, :].rearrange("p (k c) -> p k c", k=KT)
                wl = lo[slot][:, :].rearrange("p (k c) -> p k c", k=KT)
                bank = 4 * (slot % 2) if bank is None else bank
                for h in range(2):
                    for i in range(2):
                        for k in range(KT):
                            if ready and h == 0 and i == 0:
                                pe.wait_ge(ready[0], ready[1] + k + 1)
                            if h == 0 and i == 0 and k == KT // 2:
                                second(n)
                            last = passes(ps[:, bank + 2 * h + i, 0:TH], wh[:, k, i * P:(i + 1) * P], wl[:, k, i * P:(i + 1) * P],
                                          hh[:, k, h * TH:(h + 1) * TH], hl[:, k, h * TH:(h + 1) * TH], k == 0, k == KT - 1)
                    last.then_inc(gemm_out, 1)

            def norm_pe(i):
                for k in range(KT):
                    pe.wait_ge(n_sq, KT * i + k + 1)
                    for h in range(2):
                        last = pe.matmul(ps[:, 6 + h, 0:TH], ones[:, :], tmp[:, k % 2, h * TH:(h + 1) * TH],
                                         start=k == 0, stop=k == KT - 1, skip_group_check=True)
                    last.then_inc(n_mm, 1)

            pe.wait_ge(x_in, 16 * TT)
            pe.wait_ge(mats_in, 16)
            for g in range(10):
                t, q = g // 2, g % 2
                if g >= 3:
                    pe.wait_ge(x_kept, g - 2)
                for k in range(4):
                    last = pe.transpose(ps[:, 1 + g % 3, k * P:(k + 1) * P], xrows[:, t, (4 * q + k) * P:(4 * q + k + 1) * P], ident)
                last.then_inc(x_turned, 1)
            pe.wait_ge(rows_in, 16 * 21)
            for s in range(3):
                last = pe.transpose(ps[:, 5, s * P:(s + 1) * P], prow[:, s, :], ident)
            last.then_inc(par_turned, 1)
            pe.wait_ge(cs_split, 1)
            for s in range(2):
                pe.wait_ge(lo_done, 2 * s + 1)
                mod_chunk(s, s)
            with pe.Fori(1, N_MOD // 2) as pr:
                for u in range(2):
                    begin(2 * pr + u)
                    mod_chunk(u, 2 * pr + u)
            pe.wait_ge(evac, 2 * N_MOD)
            pe.wait_ge(small_in, 16 * 15)

            def fold(mrow):
                for j in range(48):
                    last = pe.matmul(ps[:, 5, 2 * j:2 * j + 2], mrow[:, j // 2, (j % 2) * P:(j % 2 + 1) * P], sel4[:, :],
                                     start=True, stop=True, skip_group_check=True)
                last.then_inc(folded, 1)

            fold(mrow)
            norm_pe(0)
            for c in range(6):
                begin(EIN + c)
                gemm_pair(c % 2, EIN + c, (n_lo, 0) if c == 0 else None)

            pe.wait_ge(evac, 2 * EOUT)
            for it in range(2 * NC):
                n, c = it // NC, it % NC
                pe.wait_ge(e_xc, c + 1)
                if it >= 2:
                    pe.wait_ge(e_sig, it - 1)
                for kind in range(2):
                    for lo_t, hi_t, cond in SEGS:
                        p0 = (0, UA_S - 2)[cond]
                        last = pe.matmul(ps[:, 4 * (it % 2) + 2 * kind + cond, 0:hi_t - lo_t], wg[:, 8 * n + 4 * kind + c, :],
                                         xc[:, c, p0:p0 + hi_t - lo_t], start=True, stop=True)
                last.then_inc(e_gate, 1)
            pe.wait_ge(e_sig, 2 * NC)
            for g in range(NC):
                pe.wait_ge(e_pool, g + 1)
                if g >= 2:
                    pe.wait_ge(e_ylo, g - 1)
                for lo_t, hi_t, cond in SEGS:
                    p0 = (UB_P, UB_S)[cond]
                    last = pe.matmul(ps[:, 2 * (g % 2) + cond, 0:hi_t - lo_t], wp[:, g, :], ub[:, g, p0:p0 + hi_t - lo_t],
                                     start=True, stop=True)
                last.then_inc(e_pmm, 1)
            pe.wait_ge(st_last, 1)
            pe.wait_ge(e_ylo, NC)
            pe.transpose(ps[0:8, 2, 0:P], sm[:, 8, :], ident).then_inc(st_turned, 1)

            pe.wait_ge(e_ylo, 2 * NC)
            pe.wait_ge(st_kept, 1)
            for c in range(4):
                begin(EOUT + c)
                gemm_pair(c % 2, EOUT + c)
            norm_pe(1)

            def ff13(slot, n, ready=None):
                begin(n)
                wh = hi[slot][:, :].rearrange("p (w k c) -> p w k c", w=2, k=KT)
                wl = lo[slot][:, :].rearrange("p (w k c) -> p w k c", w=2, k=KT)
                for h in range(2):
                    for w in range(2):
                        if h == 0 and w == 1:
                            second(n)
                        for k in range(KT):
                            last = passes(ps[:, 4 * (slot % 2) + 2 * h + w, 0:TH], wh[:, w, k, :], wl[:, w, k, :],
                                          hh[:, k, h * TH:(h + 1) * TH], hl[:, k, h * TH:(h + 1) * TH], k == 0, k == KT - 1)
                    last.then_inc(gemm_out, 1)

            def ff2(slot, n, hidden):
                begin(n)
                for h in range(2):
                    for k in range(JT):
                        if h == 0 and k == JH:
                            second(n)
                        if h == 0 and k == JT - 1:
                            pe.wait_ge(f_lo, hidden)
                        if k == 0 and h == 0:
                            pe.wait_ge(f_lo, hidden - 2)
                        last = passes(ps[:, 4 + 2 * slot + h, 0:TH], down(slot, k, hi), down(slot, k, lo),
                                      g_hi[:, k, h * TH:(h + 1) * TH], g_lo[:, k, h * TH:(h + 1) * TH], k == 0, k == JT - 1)
                    last.then_inc(gemm_out, 1)

            pe.wait_ge(n_lo, 2 * KT)
            with pe.Fori(0, 2) as f:
                n0 = FF + N_ITEM * f
                with pe.Fori(0, JT // 2) as pr:
                    for u in range(2):
                        ff13(u, n0 + 2 * pr + u)
                ff13(C_SLOT, n0 + JT - 1)
                with pe.Fori(0, KT // 2) as pr:
                    for u in range(2):
                        ff2(u, n0 + JT + 2 * pr + u, 2 * JT * (f + 1))

            with pe.Fori(0, N_MOD // 2) as pr:
                for u in range(2):
                    begin(M1 + 2 * pr + u)
                    mod_chunk(u, M1 + 2 * pr + u)
            pe.wait_ge(evac, 2 * OIN)
            fold(mrow1)
            norm_pe(2)
            for c in range(7):
                begin(OIN + c)
                gemm_pair((A_SLOT, B_SLOT, C_SLOT, A_SLOT, B_SLOT, A_SLOT, B_SLOT)[c], OIN + c, (n_lo, 2 * KT) if c == 0 else None, 4 * (c % 2))
            pe.wait_ge(evac, 2 * OOUT)
            pe.wait_ge(odd_in, 16 * 6)
            for i in range(5):
                pe.wait_ge(o_sq, i + 1)
                for h in range(2):
                    last = pe.matmul(ps[0:10, 4 + h, 0:TH], hsel[:, i, 0:10], tmp[:, i % 2, h * TH:(h + 1) * TH],
                                     start=i == 0, stop=i == 4, skip_group_check=True)
                last.then_inc(o_sum, 1)
            pe.wait_ge(o_var, 1)
            for t in range(4):
                last = pe.transpose(ps[:, 4, t * P:(t + 1) * P], vf[:, (t + 1) * P:(t + 2) * P], ident)
            last.then_inc(v_turned, 1)
            pe.transpose(ps[:, 5, 0:P], vf[:, 0:P], ident)
            pe.transpose(ps[:, 5, P:2 * P], krow[:, :], ident)
            pe.wait_ge(o_rs, 1)

            def spread(i):
                if i >= 2:
                    pe.wait_ge(o_qn, i - 1)
                for h in range(2):
                    last = pe.matmul(ps[:, 2 * (i % 2) + h, 0:TH], hspread[:, i, :], hrs[:, h * TH:(h + 1) * TH],
                                     start=True, stop=True)
                last.then_inc(o_spread, 1)

            def swap(i):
                pe.wait_ge(o_qn, i + 1)
                if i >= 2:
                    pe.wait_ge(o_sw_read, i - 1)
                pe.matmul(ps[:, 6 + i % 2, 0:TS], mats[:, SWAP, :], (qf[:, i, :] if i < 4 else kf[:, :])[:, TP:T],
                          start=True, stop=True).then_inc(o_swap, 1)

            for i in range(5):
                spread(i)
                if i >= 1:
                    swap(i - 1)
            swap(4)
            pe.transpose(ps[:, 5, 2 * P:3 * P], kf[:, 0:P], ident).then_inc(v_turned, 1)

            def turn(s):
                pe.wait_ge(a_norm, s + 1)
                if s:
                    pe.wait_ge(a_kept, s)
                if s > 1:
                    pe.wait_ge(a_kept5, s - 1 - (s - 1) // TT)
                if s % TT == 0:
                    pe.transpose(ps[:, 4, 0:P], pp[:, s % 2, 0:P], ident).then_inc(a_t, 1)
                    return
                for k in range(5):
                    last = pe.transpose(ps[:, 4 + k // 4, (k % 4) * P:(k % 4 + 1) * P], pp[:, s % 2, k * P:(k + 1) * P], ident)
                last.then_inc(a_t, 1)

            def weigh(h):
                kv, r = h // 4, slice(HD * (h // 4), HD * (h // 4) + HD)
                pe.wait_ge(a_kept, TT * (h + 1))
                pe.wait_ge(a_kept5, (TT - 1) * (h + 1))
                if h:
                    pe.wait_ge(a_ohi, h)
                    pe.wait_ge(a_olo, h)
                pe.matmul(ps[r, 7, 0:TP], vt[:, 0, r], ptp[:, h % 2, :], start=True, stop=True)
                for k in range(5):
                    last = pe.matmul(ps[r, 6, 0:TS], vt[:, 1 + k, r], pt[:, h % 2, k, :], start=k == 0, stop=k == 4)
                last.then_inc(a_pv, 1)

            pe.wait_ge(v_kept, 2)
            pe.wait_ge(o_rope, 5)
            for s in range(NH * TT + 3):
                if s < NH * TT:
                    h, t = s // TT, s % TT
                    r = slice(HD * (h // 4), HD * (h // 4) + HD)
                    if s >= 2:
                        pe.wait_ge(a_exp, s - 1)
                    q = qf[r, h % 4, t * P:(t + 1) * P]
                    if t == 0:
                        last = pe.matmul(ps[:, 2 * (s % 2), 0:P], q, kf[r, 0:P], start=True, stop=True)
                    else:
                        for i in range(2):
                            last = pe.matmul(ps[:, 2 * (s % 2) + i, 0:TH], q, kk[r, i * TH:(i + 1) * TH], start=True, stop=True)
                    last.then_inc(a_s, 1)
                if s >= 7 and (s - 2) % TT == 0:
                    weigh((s - 7) // TT)
                if 2 <= s < NH * TT + 2:
                    turn(s - 2)
            pe.wait_ge(c_dve, 3)
            pe.wait_ge(c_pool, 1)
            pe.wait_ge(a_exp, NH * TT)
            for c in range(NC):
                for lo_t, hi_t, cond in SEGS:
                    p0 = (0, GC_S - 15)[cond]
                    last = pe.matmul(ps[:, cond, 0:hi_t - lo_t], ones[:, :], vp[:, c, p0:p0 + hi_t - lo_t],
                                     start=c == 0, stop=c == NC - 1, skip_group_check=True)
            last.then_inc(l_mean, 1)
            for c in range(NC):
                pe.wait_ge(l_sq, c + 1)
                for lo_t, hi_t, cond in SEGS:
                    last = pe.matmul(ps[:, 2 + cond, 0:hi_t - lo_t], ones[:, :], tmp[:, c % 2, lo_t:hi_t],
                                     start=c == 0, stop=c == NC - 1, skip_group_check=True)
                last.then_inc(l_vmm, 1)
            pe.wait_ge(a_olo, NH)
            pe.wait_ge(l_lo, NC)
            for c in range(4):
                begin(OOUT + c)
                gemm_pair(c % 2, OOUT + c)
            norm_pe(3)

            pe.wait_ge(n_lo, 4 * KT)
            pe.wait_ge(wr_l, 1)
            for t in range(TT):
                for k in range(KT):
                    vh, vl = hh[:, k, t * P:(t + 1) * P], hl[:, k, t * P:(t + 1) * P]
                    out = ps[:, 5, NE * t:NE * (t + 1)]
                    pe.matmul(out, vh, wr_hi[:, k, :], start=k == 0, stop=False, skip_group_check=True)
                    pe.matmul(out, vh, wr_lo[:, k, :], start=False, stop=False, skip_group_check=True)
                    last = pe.matmul(out, vl, wr_hi[:, k, :], start=False, stop=k == KT - 1, skip_group_check=True)
            last.then_inc(r_mm, 1)
            for g in range(2 * TT):
                if g >= 4:
                    pe.wait_ge(ht_kept, g - 3)
                for k in range(4):
                    last = pe.transpose(ps[:, g % 4, k * P:(k + 1) * P], hf[:, 4 * (g % 2) + k, (g // 2) * P:(g // 2 + 1) * P], ident)
                last.then_inc(ht_turned, 1)
                if g == 5:
                    pe.wait_ge(r_members, 1)
                    for t in range(TT + 1):
                        out = ps[:, 4, NE * t:NE * (t + 1)]
                        for b in range(min(t, TT)):
                            last = pe.matmul(out, ones[:, :], both[:, b, :], start=b == 0, stop=t == TT and b == TT - 1, skip_group_check=True)
                        if t < TT:
                            last = pe.matmul(out, mats[:, BEFORE, :], both[:, t, :], start=t == 0, stop=True, skip_group_check=True)
                    last.then_inc(r_ranks, 1)
            for e in range(NE):
                pe.wait_ge(r_hot, e + 1)
                if e >= 2:
                    pe.wait_ge(r_ids, e - 1)
                for g in range(TT):
                    for t in range(TT):
                        last = pe.matmul(ps[:, 6 + e % 2, 4 * g:4 * g + 4], hot[e % 2][:, t, g * P:(g + 1) * P], tok_w[:, t, e, :],
                                         start=t == 0, stop=t == TT - 1, skip_group_check=True)
                last.then_inc(r_info, 1)

            def tables(e):
                return (pe.value_load(size_of[0:1, bass.ds(e, 1)], min_val=0, max_val=len(SIZES) - 1),
                        pe.value_load(tiles_before[0:1, bass.ds(e, 1)], min_val=0, max_val=NE * TT))

            def gather(e, width, halves, before):
                for g, rows in gather_tiles(width, halves):
                    if g >= 2:
                        wait_apart(pe, g_lo_kept, before + g - 1)
                    wait_apart(pe, g_rows, 16 * (before + min(len(gather_tiles(width, halves)), g - g % 2 + 2)))
                    for k in range(KT):
                        last = pe.transpose(ps[:, 2 * (g % 2) + k // 4, (k % 4) * P:(k % 4) * P + rows],
                                            rows_g[0:rows, g % 2, k * P:(k + 1) * P], ident[0:rows, 0:rows])
                    last.then_inc(g_turned, 1)

            def w13(e, width, halves, before):
                n0 = MOE + N_ITEM * e

                def chunk(slot, n):
                    begin(n)
                    wh = hi[slot][:, :].rearrange("p (w k c) -> p w k c", w=2, k=KT)
                    wl = lo[slot][:, :].rearrange("p (w k c) -> p w k c", w=2, k=KT)
                    for h in range(halves):
                        cols = slice(h * TH, h * TH + width)
                        for w in range(2):
                            if h == 0 and w == 1:
                                second(n)
                            for k in range(KT):
                                last = passes(ps[:, 4 * (slot % 2) + 2 * h + w, 0:width], wh[:, w, k, :], wl[:, w, k, :],
                                              hh[:, k, cols], hl[:, k, cols], k == 0, k == KT - 1)
                            if halves == 1 or w == 1:
                                last.then_inc(gemm_out, 1)

                wait_apart(pe, g_lo_kept, before + len(gather_tiles(width, halves)))
                with pe.Fori(0, JT // 2) as pr:
                    for u in range(2):
                        chunk(u, n0 + 2 * pr + u)
                chunk(C_SLOT, n0 + JT - 1)

            def w2(e, width, halves, gathered):
                n0 = MOE + N_ITEM * e

                def chunk(slot, m):
                    begin(n0 + JT + m)
                    for h in range(halves):
                        cols = slice(h * TH, h * TH + width)
                        for k in range(JT):
                            if h == 0 and k == JH:
                                if halves == 1:
                                    last.then_inc(gemm_out, 1)
                                second(n0 + JT + m)
                            last = passes(ps[:, 4 + 2 * slot + h, 0:width], down(slot, k, hi), down(slot, k, lo),
                                          g_hi[:, k, cols], g_lo[:, k, cols], k == 0, k == JT - 1)
                        last.then_inc(gemm_out, 1)

                def turn(u, m, first=False):
                    pe.wait_ge(evac, 2 * (n0 + JT + m + 1))
                    if not first:
                        pe.wait_ge(y_rows, KT * e + m - 1)
                    for g, rows in gather_tiles(width, halves):
                        last = pe.transpose(ps[0:rows, 2 * u + g // 4, (g % 4) * P:(g % 4 + 1) * P],
                                            yb[:, u, g * P:g * P + rows], ident)
                    last.then_inc(y_turned, 1)

                pe.wait_ge(f_lo, 2 * JT * (e + 3))
                chunk(A_SLOT, 0)
                chunk(B_SLOT, 1)
                if gathered is not None:
                    pe.wait_ge(g_lo_kept, gathered)
                turn(A_SLOT, 0, True)
                chunk(A_SLOT, 2)
                turn(B_SLOT, 1, True)
                with pe.Fori(1, KT // 2 - 1) as pr:
                    chunk(B_SLOT, 2 * pr + 1)
                    turn(A_SLOT, 2 * pr)
                    chunk(A_SLOT, 2 * pr + 2)
                    turn(B_SLOT, 2 * pr + 1)
                chunk(B_SLOT, KT - 1)
                turn(A_SLOT, KT - 2)
                turn(B_SLOT, KT - 1)

            def expert(e, last):
                size, before = tables(e)
                for i, (width, halves) in enumerate(SIZES):
                    with pe.If(size == i):
                        w13(e, width, halves, before)
                if not last:
                    size_next, before_next = tables(e + 1)
                    wait_apart(pe, evac, 2 * (MOE + N_ITEM * e + JT))
                    for i, (width, halves) in enumerate(SIZES):
                        with pe.If(size_next == i):
                            gather(e + 1, width, halves, before_next)
                    gathered = pe.value_load(tiles_after[0:1, bass.ds(e + 1, 1)], min_val=1, max_val=NE * TT)
                for i, (width, halves) in enumerate(SIZES):
                    with pe.If(size == i):
                        w2(e, width, halves, None if last else gathered)
                wait_apart(pe, y_rows, KT * (e + 1))

            pe.wait_ge(r_tables, 1)
            size, before = tables(0)
            for i, (width, halves) in enumerate(SIZES):
                with pe.If(size == i):
                    gather(0, width, halves, before)
            with pe.Fori(0, NE - 1) as e:
                expert(e, False)
            expert(NE - 1, True)

            for t in range(TT):
                pe.wait_ge(c_sum, t + 1)
                if t >= 2:
                    pe.wait_ge(c_added, KT * (t - 1))
                for k in range(KT):
                    last = pe.transpose(ps[:, 2 * (t % 2) + k // 4, (k % 4) * P:(k % 4 + 1) * P], rows_c[:, t, 0, k * P:(k + 1) * P], ident)
                last.then_inc(c_turned, 1)
            norm_pe(4)
            for g in range(2 * TT):
                t, q = g // 2, g % 2
                for k in range(4):
                    if t == 0:
                        pe.wait_ge(z_y, 4 * q + k + 1)
                    if g >= 4 and k == 0:
                        pe.wait_ge(z_kept, g - 3)
                    last = pe.transpose(ps[:, g % 4, k * P:(k + 1) * P], xT[:, 4 * q + k, t * P:(t + 1) * P], ident)
                last.then_inc(z_turned, 1)

        @block.vector
        def _(dve):
            links = [0]

            def link(ins):
                links[0] += 1
                ins.then_inc(chain, 1)
                dve.wait_ge(chain, links[0])

            def split_lo(slot, n, parts=WHOLE):
                for h in range(2):
                    dve.wait_ge(hi_done, 2 * n + h + 1)
                    dve.tensor_tensor(lo[slot][:, parts[h]], raw[slot][:, parts[h]], hi[slot][:, parts[h]].bitcast(F32),
                                      ALU.subtract).then_inc(lo_done, 1)

            dve.memset(prow[:, :, :], 0.0).then_inc(prow_zero, 1)
            dve.memset(ones[:, :], 1.0).then_inc(ones_set, 1)
            dve.memset(wg[:, :, :], 0.0).then_inc(ones_set, 1)
            dve.memset(cs_h0[:, :, :].bitcast(F32), 0.0).then_inc(csz, 1)
            for g in range(0, 10, 2):
                dve.wait_ge(x_turned, g + 1)
                if g >= 2:
                    dve.wait_ge(x_kept, g)
                t, q = g // 2, g % 2
                dve.tensor_copy(xT[:, 4 * q:4 * q + 4, t * P:(t + 1) * P],
                                ps[:, 1 + g % 3, :].rearrange("p (k c) -> p k c", k=4)).then_inc(x_kept, 1)
            dve.wait_ge(par_turned, 1)
            dve.tensor_copy(par[:, :, :], ps[:, 5, 0:3 * P].rearrange("p (s c) -> p s c", s=3)).then_inc(par_kept, 1)
            dve.wait_ge(cs_silu, 1)
            dve.wait_ge(csz, 1)
            for h in range(2):
                link(dve.tensor_copy(cs_hl[:, :, h], cs[:, h, :]))
                dve.tensor_copy(cs_h0[:, :, h], cs[:, h, :])
                last = dve.tensor_tensor(cs_hl[:, :, 2 + h], cs[:, h, :], cs_hl[:, :, h].bitcast(F32), ALU.subtract)
            last.then_inc(cs_split, 1)
            dve.wait_ge(par_kept, 1)
            lam = par[:, 1, LAM:LAM + 8]
            link(dve.tensor_scalar(sm[:, 2, :], lam, -1.0, None, ALU.mult))
            dve.tensor_tensor(sm[:, 0, :], lam, sm[:, 2, :], ALU.max).then_inc(ab_lam, 1)
            split_lo(0, 0)
            split_lo(1, 1)
            with dve.Fori(0, N_MOD // 2) as pr:
                for u in range(2):
                    split_lo(u, 2 * pr + u + 2)
            dve.wait_ge(ex_lam, 1)
            link(dve.tensor_scalar(sm[:, 3, :], sm[:, 1, :], 2.0, None, ALU.add))
            link(dve.reciprocal(sm[:, 3, :], sm[:, 3, :]))
            link(dve.tensor_tensor(sm[:, 3, :], sm[:, 1, :], sm[:, 3, :], ALU.mult))
            link(dve.tensor_tensor(sm[:, 4, :], sm[:, 3, :], sm[:, 3, :], ALU.mult))
            link(dve.tensor_scalar(sm[:, 5, :], sm[:, 4, :], 1.0 / 15, None, ALU.mult))
            for odd in (13, 11, 9, 7, 5, 3):
                link(dve.scalar_tensor_tensor(out=sm[:, 5, :], in0=sm[:, 5, :], scalar=1.0 / odd, in1=sm[:, 4, :],
                                              op0=ALU.add, op1=ALU.mult))
            link(dve.scalar_tensor_tensor(out=sm[:, 5, :], in0=sm[:, 5, :], scalar=1.0, in1=sm[:, 3, :],
                                          op0=ALU.add, op1=ALU.mult))
            link(dve.tensor_scalar(sm[:, 5, :], sm[:, 5, :], 2.0, None, ALU.mult))
            link(dve.scalar_tensor_tensor(out=sm[:, 5, :], in0=sm[:, 2, :], scalar=0.0, in1=sm[:, 5, :],
                                          op0=ALU.max, op1=ALU.add))
            dve.tensor_scalar(sm[:, 6, :], sm[:, 5, :], 8.0, None, ALU.mult)
            dve.tensor_scalar(sm[:, 7, :], sm[:, 5, :], -8.0, None, ALU.mult).then_inc(sp_ready, 1)

            def mod_params(layer):
                dve.wait_ge(folded, layer + 1)
                for c in range(2):
                    last = dve.tensor_tensor(mod[:, layer, :, c], ps[:, 5, 0:96].rearrange("p (j c) -> p j c", c=2)[:, :, c],
                                             par[:, 0, 48 * layer:48 * layer + 48], ALU.add)
                link(last)
                for w in range(2):
                    for c in range(2):
                        g0 = (N1, N2)[w] + KT * layer
                        last = dve.scalar_tensor_tensor(out=amod[:, layer, w, :, c], in0=mod[:, layer, 24 * w + 8:24 * w + 16, c], scalar=1.0,
                                                        in1=par[:, 0, g0:g0 + KT], op0=ALU.add, op1=ALU.mult)
                last.then_inc(mod_set, 1)

            mod_params(0)
            dve.wait_ge(wr_h, 1)
            dve.tensor_tensor(wr_lo[:, :, :], wr_raw[:, :, :], wr_hi[:, :, :].bitcast(F32), ALU.subtract).then_inc(wr_l, 1)

            def norm_dve(i, h=None):
                dve.wait_ge(n_mm, KT * (i + 1))
                dve.tensor_scalar(rs[:, :].rearrange("p (h t) -> p h t", h=2), ps[:, 6:8, 0:TH], 1.0 / D, EPS,
                                  ALU.mult, ALU.add).then_inc(n_var, 1)
                dve.wait_ge(n_std, i + 1)
                dve.reciprocal(rs[:, :], rs[:, :]).then_inc(n_rs, 1)
                dve.wait_ge(n_rs, i + 1)

                def t_of(k):
                    if k >= 2:
                        dve.wait_ge(n_aff, KT * i + k - 1)
                    dve.tensor_tensor(tmp[:, 2 + k % 2, 0:T], xT[:, k, :], rs[:, :], ALU.mult).then_inc(n_t, 1)

                t_of(0)
                t_of(1)
                for k in range(KT):
                    dve.wait_ge(n_hi, KT * i + k + 1)
                    dve.tensor_tensor(hl[:, k, :], tmp[:, k % 2, 0:T] if h is None else h[:, k, :], hh[:, k, :].bitcast(F32), ALU.subtract).then_inc(n_lo, 1)
                    if k + 2 < KT:
                        t_of(k + 2)

            norm_dve(0)
            for c in range(2):
                split_lo(c % 2, EIN + c + 2)
            for c in range(NC):
                dve.wait_ge(evac, 2 * (EIN + c // 2 + 1))
                w = UA_W - 3
                link(dve.tensor_scalar(xc[:, c, 0:w], up[:, c, 0:w], par[:, 1, ACW + c:ACW + c + 1], par[:, 1, ACB + c:ACB + c + 1],
                                       ALU.mult, ALU.add))
                for j in range(1, A_CONV):
                    ins = dve.scalar_tensor_tensor(out=xc[:, c, 0:w], in0=up[:, c, j:j + w], scalar=par[:, 1, ACW + 4 * j + c:ACW + 4 * j + c + 1],
                                                   in1=xc[:, c, 0:w], op0=ALU.mult, op1=ALU.add)
                    if j < A_CONV - 1:
                        link(ins)
                ins.then_inc(e_xc, 1)
                if c % 2:
                    split_lo(0, EIN + 4 + c // 2 * 2)
                    split_lo(1, EIN + 5 + c // 2 * 2)
            for g in range(NC):
                dve.wait_ge(evac, 2 * (EIN + 4 + g // 2 + 1))
                if g:
                    dve.wait_ge(e_pool, g)
                w, half = 2, 1
                left, right = 1, UB_W
                link(dve.tensor_tensor(tmp[:, 0, 1:UB_W], ub[:, g, 1:UB_W], ub[:, g, 0:UB_W - 1], ALU.add))
                level = 0
                while w < WINDOWS[g]:
                    left, right = left + half, right - half
                    link(dve.tensor_tensor(tmp[:, (level + 1) % 2, left:right], tmp[:, level % 2, left - half:right - half],
                                           tmp[:, level % 2, left + half:right + half], ALU.add))
                    w, half, level = 2 * w, w, level + 1
                buf = tmp[:, level % 2, :]
                link(dve.tensor_scalar(buf[:, 8:UB_S + TS], buf[:, 8:UB_S + TS], 1.0 / w, None, ALU.mult))
                for start, size in ((UB_P, TP), (UB_S, TS)):
                    for e, at in ((0, start), (1, start + size - 8)):
                        last = dve.tensor_tensor(buf[:, at:at + 8], buf[:, at:at + 8], edge[:, g, 8 * e:8 * e + 8], ALU.mult)
                link(last)
                dve.tensor_tensor(ub[:, g, 8:UB_S + TS], buf[:, 8:UB_S + TS], ub[:, g, 8:UB_S + TS], ALU.subtract).then_inc(e_pool, 1)

            for n in range(2):
                for c in range(NC):
                    it = NC * n + c
                    dve.wait_ge(e_a2, it + 1)
                    dve.scalar_tensor_tensor(out=th[:, c, 0:T], in0=tmp[:, 2 + it % 2, 0:T], scalar=1.0, in1=th[:, c, 0:T],
                                             op0=ALU.add, op1=ALU.mult).then_inc(e_q, 1)
                    for lo_t, hi_t, cond in SEGS:
                        p0 = (0, UA_S - 2)[cond]
                        last = dve.tensor_tensor(ii[:, c, lo_t:hi_t], ii[:, c, lo_t:hi_t], xc[:, c, p0:p0 + hi_t - lo_t], ALU.mult)
                    link(last)
                for c in range(NC):
                    it = NC * n + c
                    dve.wait_ge(e_sqrt, it + 1)
                    link(dve.tensor_tensor(th[:, c, 0:T], th[:, c, 0:T], ii[:, c, :], ALU.mult))
                    dst = (yf, ii)[n]
                    for lo_t, hi_t, cond in SEGS:
                        h0 = par[:, 1, ST + it:ST + it + 1] if cond else 0.0
                        if n == 0:
                            o, da, db = (x[:, c, lo_t:hi_t] for x in (dst, rr, th))
                        else:
                            back = slice(hi_t - 1, lo_t - 1 if lo_t else None, -1)
                            o, da, db = (x[:, c, back] for x in (dst, rr, th))
                        last = dve.tensor_tensor_scan(o, da, db, h0, ALU.mult, ALU.add)
                    last.then_inc(e_scan, 1)
            dve.wait_ge(e_scan, 2 * NC)
            dve.tensor_copy(sm[:, 8, 0:4], yf[:, :, TP - 1])
            dve.tensor_copy(sm[:, 8, 4:8], ii[:, :, 0]).then_inc(st_last, 1)
            for g in range(NC):
                dve.wait_ge(e_pmm, g + 1)
                for lo_t, hi_t, cond in SEGS:
                    last = dve.tensor_scalar(hh[:, 4 + g, lo_t:hi_t], ps[:, 2 * (g % 2) + cond, 0:hi_t - lo_t],
                                             par[:, 1, BSC + g:BSC + g + 1], None, ALU.mult)
                link(last)
                for lo_t, hi_t, cond in SEGS:
                    last = dve.scalar_tensor_tensor(out=hl[:, 4 + g, lo_t:hi_t], in0=ps[:, 2 * (g % 2) + cond, 0:hi_t - lo_t],
                                                    scalar=par[:, 1, BSC + g:BSC + g + 1], in1=hh[:, 4 + g, lo_t:hi_t].bitcast(F32),
                                                    op0=ALU.mult, op1=ALU.subtract)
                last.then_inc(e_ylo, 1)
            for c in range(NC):
                link(dve.tensor_tensor(yf[:, c, :], yf[:, c, :], ii[:, c, :], ALU.add))
                if c >= 2:
                    dve.wait_ge(e_yhi, c - 1)
                dve.tensor_tensor(tmp[:, 2 + c % 2, 0:T], yf[:, c, :], ga[:, c, :], ALU.mult).then_inc(e_y, 1)
                if c >= 1:
                    dve.wait_ge(e_yhi, c)
                    dve.tensor_tensor(hl[:, c - 1, :], tmp[:, 2 + (c - 1) % 2, 0:T], hh[:, c - 1, :].bitcast(F32), ALU.subtract).then_inc(e_ylo, 1)
            dve.wait_ge(e_yhi, NC)
            dve.tensor_tensor(hl[:, NC - 1, :], tmp[:, 2 + (NC - 1) % 2, 0:T], hh[:, NC - 1, :].bitcast(F32), ALU.subtract).then_inc(e_ylo, 1)

            def residual(bank, m, h, layer, which):
                last = None
                for lo_t, hi_t, cond in HALF_SEGS[h]:
                    x = xT[:, bass.ds(m, 1), lo_t:hi_t].rearrange("p a t -> p (a t)")
                    last = dve.scalar_tensor_tensor(out=x, in0=ps[:, bank, lo_t - TH * h:hi_t - TH * h], scalar=gate_of(layer, which, m, cond),
                                                    in1=x, op0=ALU.mult, op1=ALU.add)
                return last

            def residual_pair(slot, n, c, layer):
                for h in range(2):
                    dve.wait_ge(gemm_out, 2 * n + h + 1)
                    for i in range(2):
                        last = residual(4 * (slot % 2) + 2 * h + i, 2 * c + i, h, layer, 0)
                    last.then_inc(evac, 1)

            for c in range(4):
                residual_pair(c % 2, EOUT + c, c, 0)
                split_lo(c % 2, EOUT + c + 2)
            norm_dve(1)

            def ff13_evac(slot, n, j, f):
                dve.wait_ge(lo_done, 2 * n + 4)
                for h in range(2):
                    dve.wait_ge(f_silu, 2 * JT * f + 2 * j + h + 1)
                    dve.tensor_tensor(gf(h), sil(h), ps[:, 4 * (slot % 2) + 2 * h + 1, 0:TH], ALU.mult).then_inc(evac, 1)
                for h in range(2):
                    dve.wait_ge(f_hi, 2 * JT * f + 2 * j + h + 1)
                    v = [x[:, bass.ds(j, 1), h * TH:(h + 1) * TH].rearrange("p a c -> p (a c)") for x in (g_lo, g_hi)]
                    dve.tensor_tensor(v[0], gf(h), v[1].bitcast(F32), ALU.subtract).then_inc(f_lo, 1)

            def ff2_evac(slot, n, m):
                for h in range(2):
                    dve.wait_ge(gemm_out, 2 * n + h + 1)
                    residual(4 + 2 * slot + h, m, h, 0, 1).then_inc(evac, 1)

            with dve.Fori(0, 2) as f:
                n0 = FF + N_ITEM * f
                with dve.Fori(0, JT // 2 - 1) as pr:
                    for u in range(2):
                        ff13_evac(u, n0 + 2 * pr + u, 2 * pr + u, f)
                        split_lo(u, n0 + 2 * pr + u + 2)
                ff13_evac(A_SLOT, n0 + JT - 3, JT - 3, f)
                split_lo(C_SLOT, n0 + JT - 1)
                ff13_evac(B_SLOT, n0 + JT - 2, JT - 2, f)
                split_lo(A_SLOT, n0 + JT, DOWN)
                ff13_evac(C_SLOT, n0 + JT - 1, JT - 1, f)
                split_lo(B_SLOT, n0 + JT + 1, DOWN)
                with dve.Fori(0, KT // 2 - 1) as pr:
                    for u in range(2):
                        ff2_evac(u, n0 + JT + 2 * pr + u, 2 * pr + u)
                        split_lo(u, n0 + JT + 2 + 2 * pr + u, DOWN)
                for u in range(2):
                    ff2_evac(u, n0 + N_ITEM - 2 + u, KT - 2 + u)
                    split_lo(u, n0 + N_ITEM + u)

            with dve.Fori(0, N_MOD // 2) as pr:
                for u in range(2):
                    split_lo(u, M1 + 2 * pr + u + 2)
            mod_params(1)
            norm_dve(2)
            for c in range(5):
                split_lo(*OIN_NEXT[c][:2])
            for c in range(NC):
                if c % 2 == 0:
                    dve.wait_ge(evac, 2 * (OIN + 5 + c // 2 + 1))
                for lo_t, hi_t, cond in SEGS:
                    p0 = (GC_P, GC_S)[cond]
                    last = dve.tensor_tensor(gp[:, c, p0:p0 + hi_t - lo_t], gp[:, c, p0:p0 + hi_t - lo_t], vp[:, c, lo_t:hi_t], ALU.mult)
                last.then_inc(gp_set, 1)
                if c % 2:
                    split_lo(*OIN_NEXT[5 + c // 2][:2])

            conv_w = GC_W - 30
            todo = [(c, j) for c in range(NC - 1) for j in range(C_CONV)]

            def taps(n):
                for c, j in todo[:n]:
                    w = par[:, 2, NC * j + c:NC * j + c + 1]
                    if j == 0:
                        dve.wait_ge(gp_set, NC)
                        ins = dve.tensor_scalar(vp[:, c, 0:conv_w], gp[:, c, 0:conv_w], w, par[:, 1, CCB + c:CCB + c + 1], ALU.mult, ALU.add)
                    else:
                        ins = dve.scalar_tensor_tensor(out=vp[:, c, 0:conv_w], in0=gp[:, c, j:j + conv_w], scalar=w, in1=vp[:, c, 0:conv_w],
                                                       op0=ALU.mult, op1=ALU.add)
                    if j == C_CONV - 1:
                        ins.then_inc(c_dve, 1)
                    else:
                        link(ins)
                del todo[:n]

            taps(4)
            dve.wait_ge(o_sum, 5)
            dve.tensor_scalar(hrs[:, :].rearrange("p (h t) -> p h t", h=2), ps[0:10, 4:6, 0:TH], 1.0 / HD, EPS, ALU.mult, ALU.add).then_inc(o_var, 1)
            taps(2)
            dve.wait_ge(o_std, 1)
            dve.reciprocal(hrs[:, :], hrs[:, :]).then_inc(o_rs, 1)
            taps(2)

            def qn(i):
                x = qf[:, i, :] if i < 4 else kf[:, :]
                g = QN if i < 4 else KN
                dve.wait_ge(o_spread, i + 1)
                dve.scalar_tensor_tensor(out=x.rearrange("p (h t) -> p h t", h=2), in0=ps[:, 2 * (i % 2):2 * (i % 2) + 2, 0:TH],
                                         scalar=par[:, 1, g:g + 1], in1=x.rearrange("p (h t) -> p h t", h=2),
                                         op0=ALU.mult, op1=ALU.mult).then_inc(o_qn, 1)

            def rope(i):
                x = (qf[:, i, :] if i < 4 else kf[:, :])[:, TP:T]
                y = x if i < 4 else kk[:, TP:T]
                dve.wait_ge(o_swap, i + 1)
                if i:
                    dve.wait_ge(o_rope, i)
                dve.tensor_tensor(tmp[:, 2, 0:TS], ps[:, 6 + i % 2, 0:TS], sin_t[:, :], ALU.mult).then_inc(o_sw_read, 1)
                dve.wait_ge(o_qn, i + 1)
                link(dve.tensor_tensor(y, x, cos_t[:, :], ALU.mult))
                dve.wait_ge(o_sw_read, i + 1)
                dve.tensor_tensor(y, y, tmp[:, 2, 0:TS], ALU.add).then_inc(o_rope, 1)

            for i in range(5):
                qn(i)
                if i:
                    rope(i - 1)
            rope(4)
            dve.wait_ge(v_turned, 2)
            dve.tensor_copy(vt[:, 0, :], ps[:, 5, 0:P])
            dve.tensor_copy(kk[:, 0:P], ps[:, 5, P:2 * P])
            dve.tensor_copy(knew[:, :], ps[:, 5, 2 * P:3 * P]).then_inc(v_kept, 1)

            def head_lo(h):
                dve.wait_ge(a_ohi, h + 1)
                r = slice(HD * (h // 4), HD * (h // 4) + HD)
                dve.tensor_tensor(hl[r, 4 + h % 4, 0:TP], ps[r, 7, 0:TP], hh[r, 4 + h % 4, 0:TP].bitcast(F32), ALU.subtract)
                dve.tensor_tensor(hl[r, 4 + h % 4, TP:T], ps[r, 6, 0:TS], hh[r, 4 + h % 4, TP:T].bitcast(F32), ALU.subtract).then_inc(a_olo, 1)

            for s in range(NH * TT + 4):
                if s < NH * TT:
                    dve.wait_ge(a_s, s + 1)
                    if s >= 2:
                        dve.wait_ge(a_exp, s - 1)
                    if s % TT == 0:
                        link(dve.reduce_max(am[:, 0, s % 2:s % 2 + 1], ps[:, 2 * (s % 2), 0:P], AX_X))
                    else:
                        link(dve.reduce_max(am[:, 0, s % 2:s % 2 + 1], ps[:, 2 * (s % 2):2 * (s % 2) + 2, 0:TH], AX_XY))
                    dve.tensor_scalar(am[:, 1, s % 2:s % 2 + 1], am[:, 0, s % 2:s % 2 + 1], -HD ** -0.5, None, ALU.mult).then_inc(a_max, 1)
                if 1 <= s < NH * TT + 1:
                    u = s - 1
                    width = P if u % TT == 0 else T
                    dve.wait_ge(a_exp, u + 1)
                    link(dve.reciprocal(am[:, 3, u % 2:u % 2 + 1], am[:, 2, u % 2:u % 2 + 1]))
                    dve.tensor_scalar(pp[:, u % 2, 0:width], pp[:, u % 2, 0:width], am[:, 3, u % 2:u % 2 + 1], None, ALU.mult).then_inc(a_norm, 1)
                if 2 <= s < NH * TT + 2 and (s - 2) % TT:
                    u = s - 2
                    h, t = u // TT, u % TT
                    dve.wait_ge(a_t, u + 1)
                    if h >= 2:
                        dve.wait_ge(a_pv, h - 1)
                    dve.tensor_copy(pt[:, h % 2, 4, (t - 1) * P:t * P], ps[:, 5, 0:P]).then_inc(a_kept5, 1)
                if s >= 8 and (s - 3) % TT == 0:
                    head_lo((s - 8) // TT)
                taps(2)
            taps(len(todo))
            dve.wait_ge(l_mean, 1)
            for c in range(NC):
                for lo_t, hi_t, cond in SEGS:
                    p0 = (0, GC_S - 15)[cond]
                    last = dve.scalar_tensor_tensor(out=vp[:, c, p0:p0 + hi_t - lo_t], in0=ps[:, cond, 0:hi_t - lo_t], scalar=-1.0 / D_A,
                                                    in1=vp[:, c, p0:p0 + hi_t - lo_t], op0=ALU.mult, op1=ALU.add)
                last.then_inc(l_xc, 1)
            dve.wait_ge(l_vmm, NC)
            for lo_t, hi_t, cond in SEGS:
                last = dve.tensor_scalar(rs[:, lo_t:hi_t], ps[:, 2 + cond, 0:hi_t - lo_t], 1.0 / D_A, EPS, ALU.mult, ALU.add)
            last.then_inc(l_var, 1)
            dve.wait_ge(l_std, 1)
            link(dve.reciprocal(rs[:, :], rs[:, :]))

            def ln_lo(c):
                dve.wait_ge(l_hi, c + 1)
                dve.tensor_tensor(hl[:, c, :], tmp[:, c % 2, 0:T], hh[:, c, :].bitcast(F32), ALU.subtract).then_inc(l_lo, 1)

            for c in range(NC):
                if c >= 2:
                    dve.wait_ge(l_silu, c - 1)
                for lo_t, hi_t, cond in SEGS:
                    p0 = (0, GC_S - 15)[cond]
                    last = dve.tensor_tensor(tmp[:, 2 + c % 2, lo_t:hi_t], vp[:, c, p0:p0 + hi_t - lo_t], rs[:, lo_t:hi_t], ALU.mult)
                last.then_inc(l_y, 1)
                if c:
                    ln_lo(c - 1)
            ln_lo(NC - 1)

            for c in range(4):
                residual_pair(c % 2, OOUT + c, c, 1)
                split_lo(c % 2, OOUT + c + 2)
            norm_dve(3, hf)

            dve.wait_ge(r_mm, 1)
            for t in range(TT):
                last = dve.tensor_tensor(lg[:, t, :], ps[:, 5, NE * t:NE * (t + 1)], brow[:, :], ALU.add)
            link(last)
            for t in range(TT):
                last = dve.max(mx8[:, t, :], lg[:, t, :])
            link(last)
            for t in range(TT):
                last = dve.max_index(ix8[:, t, :], mx8[:, t, :], lg[:, t, :])
            link(last)
            dve.tensor_tensor(gw[:, :, 1], mx8[:, :, 1], mx8[:, :, 0], ALU.subtract).then_inc(r_d, 1)
            link(dve.tensor_copy(ixf[:, :, :], ix8[:, :, 0:2]))
            for t in range(TT):
                for k in range(2):
                    last = dve.tensor_scalar(members[:, k, t, :], iota8[:, :], ixf[:, t, k:k + 1], None, ALU.is_equal)
            link(last)
            dve.tensor_tensor(both[:, :, :], members[:, 0, :, :], members[:, 1, :, :], ALU.add).then_inc(r_members, 1)
            dve.wait_ge(r_exp, 1)
            link(dve.tensor_scalar(gw[:, :, 0], gw[:, :, 1], 1.0, None, ALU.add))
            link(dve.reciprocal(gw[:, :, 0], gw[:, :, 0]))
            link(dve.tensor_tensor(gw[:, :, 1], gw[:, :, 1], gw[:, :, 0], ALU.mult))
            for t in range(TT):
                link(dve.tensor_scalar(comb[:, t, :], members[:, 1, t, :], gw[:, t, 1:2], None, ALU.mult))
                last = dve.scalar_tensor_tensor(out=comb[:, t, :], in0=members[:, 0, t, :], scalar=gw[:, t, 0:1], in1=comb[:, t, :],
                                                op0=ALU.mult, op1=ALU.add)
            link(last)
            link(dve.tensor_copy(tok_w[:, :, :, 1], comb[:, :, :]))
            dve.tensor_tensor(tok_w[:, :, :, 2], comb[:, :, :], tok_w[:, :, :, 1].bitcast(F32), ALU.subtract)
            for t in range(TT):
                for c in (0, 3):
                    last = dve.tensor_scalar(tok_w[:, t, :, c], iota8[:, :], 0.0, tok_id[:, t:t + 1], ALU.mult, ALU.add)
            link(last)
            dve.wait_ge(r_ranks, 1)
            link(dve.tensor_copy(cnt[:, 0, :], ps[:, 4, NE * TT:NE * (TT + 1)]))
            for i, (width, halves) in enumerate(SIZES[:-1]):
                last = dve.tensor_scalar(cnt[:, 1 + i, :], cnt[:, 0, :], float(width), None, ALU.is_gt)
            link(last)
            link(dve.tensor_tensor(cnt[:, 0, :], cnt[:, 1, :], cnt[:, 2, :], ALU.add))
            link(dve.tensor_tensor(cnt[:, 0, :], cnt[:, 0, :], cnt[:, 3, :], ALU.add))
            link(dve.tensor_copy(size_of[:, :], cnt[0:1, 0, :]))
            link(dve.tensor_scalar(cnt[:, 4, :], cnt[:, 1, :], 0.0, float(TILES[0]), ALU.mult, ALU.add))
            for i in range(len(SIZES) - 1):
                link(dve.scalar_tensor_tensor(out=cnt[:, 4, :], in0=cnt[:, 1 + i, :], scalar=float(TILES[i + 1] - TILES[i]), in1=cnt[:, 4, :],
                                              op0=ALU.mult, op1=ALU.add))
            link(dve.memset(cnt[:, 5, :], 1.0))
            link(dve.tensor_tensor_scan(cnt[:, 0, :], cnt[:, 5, :], cnt[:, 4, :], 0.0, ALU.mult, ALU.add))
            link(dve.tensor_copy(tiles_after[:, :], cnt[0:1, 0, :]))
            link(dve.tensor_tensor(cnt[:, 0, :], cnt[:, 0, :], cnt[:, 4, :], ALU.subtract))
            dve.tensor_scalar(base8[:, :], cnt[:, 0, :], float(P), None, ALU.mult)
            dve.tensor_copy(tiles_before[:, :], cnt[0:1, 0, :]).then_inc(r_tables, 1)
            link(dve.tensor_copy(rank[:, :, :], ps[:, 4, 0:NE * TT].rearrange("p (t e) -> p t e", t=TT)))
            for t in range(TT):
                last = dve.tensor_tensor(lg[:, t, :], rank[:, t, :], base8[:, :], ALU.add)
            link(last)
            for k in range(2):
                link(dve.tensor_tensor(comb[:, :, :], lg[:, :, :], members[:, k, :, :], ALU.mult))
                link(dve.tensor_reduce(slotf[:, :, k], comb[:, :, :], AX_X, ALU.add))
            link(dve.tensor_copy(slots[:, :, :], slotf[:, :, :]))
            link(dve.scalar_tensor_tensor(out=rank[:, :, :], in0=rank[:, :, :], scalar=1.0, in1=both[:, :, :], op0=ALU.add, op1=ALU.mult))
            link(dve.tensor_scalar(rank[:, :, :], rank[:, :, :], -1.0, None, ALU.add))

            def info(e):
                dve.wait_ge(r_info, e + 1)
                v = ps[:, 6 + e % 2, 0:4 * TT].rearrange("p (g c) -> p g c", c=4)
                dve.tensor_copy(ids[:, e, :], v[:, :, 0])
                link(dve.tensor_copy(slot_w[:, e, :], v[:, :, 1]))
                dve.tensor_tensor(slot_w[:, e, :], slot_w[:, e, :], v[:, :, 2], ALU.add).then_inc(r_ids, 1)

            dve.wait_ge(iota_in, 16)
            for e in range(NE):
                if e == 1:
                    dve.wait_ge(ht_turned, 2 * TT)
                elif e >= 2:
                    dve.wait_ge(r_info, e - 1)
                for t in range(TT):
                    last = dve.tensor_scalar(hot[e % 2][:, t, :], iota_t[:, :], rank[:, t, e:e + 1], None, ALU.is_equal)
                last.then_inc(r_hot, 1)
                if e:
                    info(e - 1)
            info(NE - 1)

            def tables(e):
                return (dve.value_load(size_of[0:1, bass.ds(e, 1)], min_val=0, max_val=len(SIZES) - 1),
                        dve.value_load(tiles_before[0:1, bass.ds(e, 1)], min_val=0, max_val=NE * TT))

            def w13(e, width, halves):
                n0, f = MOE + N_ITEM * e, 2 + e

                def gate(slot, n, j):
                    dve.wait_ge(f_lo, 2 * JT * f + 2 * j)
                    for h in range(halves):
                        dve.wait_ge(gemm_out, 2 * n + 2 // halves * (h + 1))
                        dve.wait_ge(f_silu, 2 * JT * f + 2 * j + 2 // halves * (h + 1))
                        dve.tensor_tensor(gf(h, width), sil(h, width), ps[:, 4 * (slot % 2) + 2 * h + 1, 0:width],
                                          ALU.mult).then_inc(evac, 2 // halves)

                def rest(j):
                    for h in range(halves):
                        dve.wait_ge(f_hi, 2 * JT * f + 2 * j + 2 // halves * (h + 1))
                        v = [x[:, bass.ds(j, 1), h * TH:h * TH + width].rearrange("p a c -> p (a c)") for x in (g_lo, g_hi)]
                        dve.tensor_tensor(v[0], gf(h, width), v[1].bitcast(F32), ALU.subtract).then_inc(f_lo, 2 // halves)

                with dve.Fori(0, JT // 2 - 1) as pr:
                    for u in range(2):
                        gate(u, n0 + 2 * pr + u, 2 * pr + u)
                        split_lo(u, n0 + 2 * pr + u + 2)
                        rest(2 * pr + u)
                gate(A_SLOT, n0 + JT - 3, JT - 3)
                split_lo(C_SLOT, n0 + JT - 1)
                rest(JT - 3)
                gate(B_SLOT, n0 + JT - 2, JT - 2)
                split_lo(A_SLOT, n0 + JT, DOWN)
                rest(JT - 2)
                gate(C_SLOT, n0 + JT - 1, JT - 1)
                split_lo(B_SLOT, n0 + JT + 1, DOWN)
                rest(JT - 1)

            def gather(e, width, halves, before):
                for g, rows in gather_tiles(width, halves):
                    dve.wait_ge(g_hi_kept, before + g + 1)
                    dve.tensor_tensor(hl[:, :, g * P:g * P + rows].rearrange("p (a b) c -> p a b c", a=2),
                                      ps[:, 2 * (g % 2):2 * (g % 2) + 2, :].rearrange("p a (b c) -> p a b c", b=4)[:, :, :, 0:rows],
                                      hh[:, :, g * P:g * P + rows].bitcast(F32).rearrange("p (a b) c -> p a b c", a=2),
                                      ALU.subtract).then_inc(g_lo_kept, 1)

            def w2(e, width, halves, last):
                n0 = MOE + N_ITEM * e

                def rows_of(u, pr):
                    dve.wait_ge(y_turned, KT * e + 2 * pr + u + 1)
                    if not isinstance(pr, int) or pr > 0:
                        dve.wait_ge(out_rows[u], 16 + 16 * KT * e + 32 * pr)
                    for g, rows in gather_tiles(width, halves):
                        ins = dve.tensor_scalar(rows_y[0:rows, u, g, :], ps[0:rows, 2 * u + g // 4, (g % 4) * P:(g % 4 + 1) * P],
                                                slot_w[0:rows, bass.ds(e, 1), g:g + 1].rearrange("p a b -> p (a b)"), None, ALU.mult)
                    ins.then_inc(y_rows, 1)

                split_lo(A_SLOT, n0 + JT + 2, DOWN)
                rows_of(A_SLOT, 0)
                split_lo(B_SLOT, n0 + JT + 3, DOWN)
                rows_of(B_SLOT, 0)
                with dve.Fori(1, KT // 2 - 1) as pr:
                    for u in range(2):
                        split_lo(u, n0 + JT + 2 + 2 * pr + u, DOWN)
                        rows_of(u, pr)
                for u in range(2):
                    if not last:
                        split_lo(u, n0 + N_ITEM + u)
                    rows_of(u, KT // 2 - 1)

            def expert(e, last):
                size, before = tables(e)
                for i, (width, halves) in enumerate(SIZES):
                    with dve.If(size == i):
                        w13(e, width, halves)
                if not last:
                    size_next, before_next = tables(e + 1)
                    for i, (width, halves) in enumerate(SIZES):
                        with dve.If(size_next == i):
                            gather(e + 1, width, halves, before_next)
                for i, (width, halves) in enumerate(SIZES):
                    with dve.If(size == i):
                        w2(e, width, halves, last)

            size, before = tables(0)
            for i, (width, halves) in enumerate(SIZES):
                with dve.If(size == i):
                    gather(0, width, halves, before)
            with dve.Fori(0, NE - 1) as e:
                expert(e, False)
            expert(NE - 1, True)

            for t in range(TT + 1):
                if t < TT:
                    dve.wait_ge(c_rows[t], 32)
                    dve.tensor_tensor(rows_c[:, t, 0, :], rows_c[:, t, 0, :], rows_c[:, t, 1, :], ALU.add).then_inc(c_sum, 1)
                if t:
                    dve.wait_ge(c_turned, t)
                    for k in range(KT):
                        x = xT[:, k, (t - 1) * P:t * P]
                        dve.scalar_tensor_tensor(out=x, in0=ps[:, 2 * ((t - 1) % 2) + k // 4, (k % 4) * P:(k % 4 + 1) * P],
                                                 scalar=gate_of(1, 1, k, int(t > 1)), in1=x, op0=ALU.mult, op1=ALU.add).then_inc(c_added, 1)

            dve.wait_ge(n_mm, KT * 5)
            dve.tensor_scalar(rs[:, :].rearrange("p (h t) -> p h t", h=2), ps[:, 6:8, 0:TH], 1.0 / D, EPS,
                              ALU.mult, ALU.add).then_inc(n_var, 1)
            dve.wait_ge(n_std, 5)
            link(dve.reciprocal(rs[:, :], rs[:, :]))
            for k in range(KT):
                dve.scalar_tensor_tensor(out=xT[:, k, :], in0=xT[:, k, :], scalar=par[:, 1, NF + k:NF + k + 1], in1=rs[:, :],
                                         op0=ALU.mult, op1=ALU.mult).then_inc(z_y, 1)
            for g in range(0, 2 * TT, 2):
                dve.wait_ge(z_turned, g + 1)
                if g:
                    dve.wait_ge(z_kept, g)
                dve.tensor_copy(yrows[:, g // 2, 512 * (g % 2):512 * (g % 2) + 512], ps[:, g % 4, :]).then_inc(z_kept, 1)

        @block.gpsimd
        def _(pool):
            pool.wait_ge(x_turned, 10)
            pool.wait_ge(folded, 1)
            pool.memset(zeros[:, :], 0.0).then_inc(zeros_set, 1)
            pool.wait_ge(zeros_set, 1)
            pool.memset(up[:, :, :], 0.0).then_inc(pads, 1)
            pool.memset(ub[:, :, :], 0.0).then_inc(pads, 1)

            def norm_pool(i, layer, which, h=None):
                for k in range(KT):
                    pool.wait_ge(n_t, KT * i + k + 1)
                    if k >= 2:
                        pool.wait_ge(n_lo, KT * i + k - 1)
                    for lo_t, hi_t, cond in SEGS:
                        last = pool.tensor_scalar((tmp[:, k % 2, :] if h is None else h[:, k, :])[:, lo_t:hi_t], tmp[:, 2 + k % 2, lo_t:hi_t],
                                                  amod[:, layer, which, k, cond:cond + 1], mod[:, layer, 24 * which + k, cond:cond + 1],
                                                  ALU.mult, ALU.add)
                    last.then_inc(n_aff, 1)

            pool.wait_ge(mod_set, 1)
            norm_pool(0, 0, 0)
            for it in range(2 * NC):
                pool.wait_ge(e_exp, it + 1)
                pool.wait_ge(e_pool, NC)
                if it >= 2:
                    pool.wait_ge(e_q, it - 1)
                c = it % NC
                pool.tensor_tensor(tmp[:, 2 + it % 2, 0:T], rr[:, c, :], rr[:, c, :], ALU.mult).then_inc(e_a2, 1)
            norm_pool(1, 0, 1)
            with pool.Fori(0, Y_TILES) as i:
                wait_apart(pool, evac, 2 * (FF + i))
                pool.dma_start(y_dram[bass.ds(i, 1)].rearrange("o p (a c) -> p (o a) c", c=P),
                               zeros[:, :].rearrange("p (o c) -> p o c", o=1).to_broadcast([P, D // P, P])).then_inc(y_zero, 16)
            pool.wait_ge(folded, 2)
            pool.memset(gp[:, :, :], 0.0).then_inc(gp_pads, 1)
            pool.wait_ge(mod_set, 2)
            norm_pool(2, 1, 0)
            pool.wait_ge(gp_set, NC)
            pool.wait_ge(par_kept, 1)
            c, conv_w = NC - 1, GC_W - 30
            for j in range(C_CONV):
                w = par[:, 2, NC * j + c:NC * j + c + 1]
                if j == 0:
                    pool.tensor_scalar(vp[:, c, 0:conv_w], gp[:, c, 0:conv_w], w, par[:, 1, CCB + c:CCB + c + 1], ALU.mult, ALU.add).then_inc(pchain, 1)
                else:
                    pool.tensor_scalar(tmp[:, 3, 0:conv_w], gp[:, c, j:j + conv_w], w, None, ALU.mult).then_inc(pchain, 1)
                    pool.wait_ge(pchain, 2 * j)
                    ins = pool.tensor_tensor(vp[:, c, 0:conv_w], vp[:, c, 0:conv_w], tmp[:, 3, 0:conv_w], ALU.add)
                    ins.then_inc(c_pool if j == C_CONV - 1 else pchain, 1)
                    if j < C_CONV - 1:
                        pool.wait_ge(pchain, 2 * j + 1)
            pool.wait_ge(kv_stored, 32)
            pool.wait_ge(evac, 2 * MOE)
            pool.dma_start(iota_t[:, :], a["const_iota_t"].to_broadcast([P, T])).then_inc(iota_in, 16)
            norm_pool(3, 1, 1, hf)
            for t in range(TT):
                pool.wait_ge(ht_kept, 2 * (t + 1))
                pool.dma_start(h_dram[t * P:(t + 1) * P, :], hrows[:, t, :]).then_inc(out_rows[t] if t < 2 else h_stored, 16)

            def tables(e):
                return (pool.value_load(size_of[0:1, bass.ds(e, 1)], min_val=0, max_val=len(SIZES) - 1),
                        pool.value_load(tiles_before[0:1, bass.ds(e, 1)], min_val=0, max_val=Y_TILES - TT))

            def gather(width, halves, before):
                for g, rows in gather_tiles(width, halves):
                    if g >= 2:
                        wait_apart(pool, g_turned, before + g - 1)
                    pool.indirect_dma_start(rows_g[0:rows, g % 2, :], None, h_dram,
                                            bass.IndirectOffsetOnAxis(ap=ids_now[0:rows, g:g + 1], axis=0)).then_inc(g_rows, 16)

            def gather_any(e):
                size, before = tables(e)
                pool.tensor_copy(ids_now[:, :], ids[:, bass.ds(e, 1), :].rearrange("p a g -> p (a g)")).then_inc(ids_copied, 1)
                wait_apart(pool, ids_copied, e + 1)
                for i, (width, halves) in enumerate(SIZES):
                    with pool.If(size == i):
                        gather(width, halves, before)

            def store(e, width, halves, before):
                full = len(gather_tiles(width, halves)) - 1
                rows = gather_tiles(width, halves)[-1][1]
                with pool.Fori(0, KT // 2) as pr:
                    for u in range(2):
                        m = 2 * pr + u
                        wait_apart(pool, y_rows, KT * e + m + 1)
                        pool.dma_start(y_dram[bass.ds(before, full), :, bass.ds(m * P, P)].rearrange("g p c -> p g c"),
                                       rows_y[:, u, 0:full, :]).then_inc(out_rows[u], 16)
                        pool.dma_start(y_dram[bass.ds(before + full, 1), 0:rows, bass.ds(m * P, P)].rearrange("g p c -> p (g c)"),
                                       rows_y[0:rows, u, full, :]).then_inc(out_rows[u], 16)

            def store_any(e):
                size, before = tables(e)
                for i, (width, halves) in enumerate(SIZES):
                    with pool.If(size == i):
                        store(e, width, halves, before)

            pool.wait_ge(r_tables, 1)
            pool.wait_ge(r_ids, 1)
            for u in range(2):
                pool.wait_ge(out_rows[u], 16)
            pool.wait_ge(h_stored, 16 * (TT - 2))
            pool.wait_ge(y_zero, 16 * Y_TILES)
            gather_any(0)
            pool.wait_ge(r_ids, NE)
            with pool.Fori(0, NE - 1) as e:
                wait_apart(pool, lo_done, 2 * (MOE + N_ITEM * e + JT))
                gather_any(e + 1)
                store_any(e)
            store_any(NE - 1)
            for u in range(2):
                pool.wait_ge(out_rows[u], 16 + 16 * KT * NE)
            for t in range(TT):
                for k in range(2):
                    pool.indirect_dma_start(rows_c[:, t, k, :], None, y_dram.rearrange("g p c -> (g p) c"),
                                            bass.IndirectOffsetOnAxis(ap=slots[:, t, k:k + 1], axis=0)).then_inc(c_rows[t], 16)


def shape_constants():
    f = np.float32
    mats = np.zeros((3, P, P), f)
    mats[0] = np.eye(P)
    mats[1] = np.triu(np.ones((P, P)), 1)
    swap = np.zeros((P, P), f)
    for d in range(P):
        half = d % 32 // 16
        swap[d + 16 - 32 * half, d] = 2 * half - 1
    mats[2] = swap
    edge = np.ones((4, 16), f)
    for g, w in enumerate((2, 4, 8, 16)):
        for e in range(8):
            edge[g, e] = w / min(w, e + w // 2)
            edge[g, 8 + e] = w / min(w, 8 - e + w // 2)
    t = np.arange(512)
    inv = f(10000.0) ** (-np.arange(16, dtype=f) / f(16))
    ang = np.stack([(t // 64).astype(f)[:, None] * inv, (t % 64).astype(f)[:, None] * inv], axis=1)
    d = np.arange(P) % 64
    table = ang[:, d // 32, d % 16].T
    hsel = np.zeros((P, 5, 16), f)
    hspread = np.zeros((10, 5, P), f)
    for i in range(5):
        for e in range(2):
            r = 8 + e if i == 4 else i + 4 * e
            hsel[64 * e:64 * e + 64, i, r] = 1
            hspread[r, i, 64 * e:64 * e + 64] = 1
    return {"const_mats": mats, "const_edge": edge, "const_sel4": np.array([[1, 0], [0, 1], [1, 0], [0, 1]], f),
            "const_cos": np.cos(table).astype(f), "const_sin": np.sin(table).astype(f), "const_hsel": hsel,
            "const_hspread": hspread, "const_iota": np.arange(8, dtype=f)[None],
            "const_tok": (np.arange(P)[:, None] + P * np.arange(5)[None]).astype(f), "const_iota_t": np.arange(640, dtype=f)[None]}


_INS = ["x_prompt", "x_sample", "c", "state_rglru", "cache_k", "cache_v", "c_ctx", "w_mod", "b_mod", "norm1", "norm2",
        "ev_w_in", "a_conv_w", "a_conv_b", "a_w_r", "a_b_r", "a_w_i", "a_b_i", "a_lam", "b_w_pool", "b_scale", "ev_w_out",
        "od_w_in", "c_conv_w", "c_conv_b", "c_ln_g", "c_ln_b", "q_norm", "k_norm", "od_w_out", "ff_w1", "ff_w3", "ff_w2",
        "moe_w_router", "moe_b_router", "moe_w1", "moe_w3", "moe_w2", "norm_f"]
_OUTS = [("y_prompt", (1, TP, D)), ("y_sample", (1, TS, D)), ("new_state", (1, 1, 2, D_A)),
         ("new_k", (1, 1, TP, 2, HD)), ("new_v", (1, 1, TP, 2, HD))]


def kernel(**inputs):
    import numpy as _np
    import concourse.bacc as _bacc
    from concourse import mybir as _mybir
    from concourse.bass_utils import run_bass_kernel_spmd as _run

    nc = _bacc.Bacc("TRN2", target_bir_lowering=False, num_devices=1)
    given = {name: _np.ascontiguousarray(inputs[name]) for name in _INS}
    given.update(shape_constants())
    arrays, aps = {}, {}
    for name, v in given.items():
        arrays[f"in_{name}_dram"] = v
        aps[name] = nc.dram_tensor(f"in_{name}_dram", v.shape, _mybir.dt.from_np(v.dtype), kind="ExternalInput").ap()
    for name, shape in _OUTS:
        aps[name] = nc.dram_tensor(f"out_{name}_dram", shape, F32, kind="ExternalOutput").ap()
    hybrid_trunk_step(nc, aps)
    r = _run(nc, [arrays], core_ids=[0])
    return tuple(r.results[0][f"out_{name}_dram"] for name, _ in _OUTS)
```

```python
from contextlib import ExitStack

import numpy as np

import concourse.bass as bass
from concourse import mybir

F32 = mybir.dt.float32
F32R = mybir.dt.float32r
I32 = mybir.dt.int32
U32 = mybir.dt.uint32
ALU = mybir.AluOpType
ACT = mybir.ActivationFunctionType
AX_X = mybir.AxisListType.X
AX_XY = mybir.AxisListType.XY

P = 128
D = 1024
KT = D // P
TP, TS = 128, 512
T = TP + TS
TT = T // P
TH = T // 2
EPS = 1e-6
HALF_SEGS = [[(0, TP, 0), (TP, TH, 1)], [(TH, T, 1)]]
SEGS = [(0, TP, 0), (TP, T, 1)]

D_A = 512
NC = D_A // P
A_CONV = 4
C_CONV = 31
WINDOWS = (2, 4, 8, 16)
D_FF, D_FFE = 2816, 1408
JT = D_FFE // P
NE = 8
HD = 64
NH = 8
PAST = 128

UA_P, UA_S, UA_W = 2, 133, 646
UB_P, UB_S, UB_W = 8, 144, 664
GC_P, GC_S, GC_W = 15, 158, 685
PADW = 664

N_MOD = 24
N_ITEM = JT + KT
AB_ITEM = (N_ITEM - 1) // 2
M0, EIN, EOUT, FF, M1, OIN, OOUT, MOE = 0, 24, 30, 34, 72, 96, 103, 107
AB = {M0: 0, EIN: 12, EOUT: 15, FF: 17, M1: 35, OIN: 47, OOUT: 53, MOE: 57}
CC = {FF: 0, OIN: 2, MOE: 3}
A_SLOT, B_SLOT, C_SLOT = 0, 1, 2
X_AFTER = 4
JH = 6
WHOLE = (slice(0, D), slice(D, 2 * D))
DOWN = (slice(0, JH * P), slice(D, D + (JT - JH) * P))

N1, N2 = 96, 112
NF, ACW, ACB, BR, BI, LAM, BSC, CCB, LNG, LNB, CS, CX, ST, QN, KN = (
    0, 8, 24, 28, 36, 44, 52, 56, 60, 64, 68, 76, 84, 92, 93)
SIZES = ((128, 1), (192, 1), (256, 1), (TH, 1), (TH, 2))
TILES = (1, 2, 2, 3, TT)
Y_TILES = NE * TILES[0] + 3 * (TILES[4] - TILES[0]) + (TILES[3] - TILES[0])
IDENT, BEFORE, SWAP = range(3)


def hybrid_trunk_step(nc, a):
    ctx = ExitStack()
    with ctx:
        def sem(name):
            return ctx.enter_context(nc.semaphore(name))

        here = [16512]

        def place(name, shape, dt=F32, at=None):
            size = 4
            for n in shape[1:]:
                size *= n
            off = here[0] if at is None else at
            if at is None:
                here[0] += (size + 31) // 32 * 32
            return nc.alloc_sbuf_tensor_at(name, shape, dt, offset=off)

        xT = place("xT", [P, KT, T])
        at_hl = here[0] + 4 * KT * T
        h_both = place("h_both", [P, 2, KT, T], F32R)
        hh, hl = h_both[:, 0], h_both[:, 1]
        raw, hi, lo = [], [], []
        for s in range(3):
            at_raw = here[0]
            raw.append(place(f"raw{s}", [P, 2048]))
            at_hi = here[0]
            hi.append(place(f"hi{s}", [P, 2048], F32R))
            lo.append(place(f"lo{s}", [P, 2048], F32R))
        wg = place("wg", [P, 16, P], at=at_raw)
        yf = place("yf", [P, NC, T], at=at_hi)
        wp = place("wp", [P, NC, P], at=at_hi + 4 * NC * T)
        ii = place("ii", [P, NC, T], at=at_hl)

        mats = place("mats", [P, 3, P])
        ones = place("ones", [P, P])
        par = place("par", [P, 3, P])
        mod = place("mod", [P, 2, 48, 2])
        amod = place("amod", [P, 2, 2, KT, 2])
        cs = place("cs", [P, 2, KT])
        cs_hl = place("cs_hl", [P, KT, 4], F32R)
        cs_h0 = place("cs_h0", [P, KT, 4], F32R)
        sel4 = place("sel4", [4, 2])
        rs = place("rs", [P, T])
        tmp = place("tmp", [P, 4, PADW])
        sm = place("sm", [P, 16, 8])
        edge = place("edge", [P, NC, 16])
        zeros = place("zeros", [P, P])
        act_warm = place("act_warm", [1, 8])
        wr_raw = place("wr_raw", [P, KT, NE])
        wr_hi = place("wr_hi", [P, KT, NE], F32R)
        wr_lo = place("wr_lo", [P, KT, NE], F32R)
        iota8 = place("iota8", [P, NE])
        brow = place("brow", [P, NE])
        tok_id = place("tok_id", [P, TT])
        slots = place("slots", [P, TT, 2], I32)
        ids = place("ids", [P, NE, TT], I32)
        ids_now = place("ids_now", [P, TT], I32)
        slot_w = place("slot_w", [P, NE, TT])
        size_of = place("size_of", [1, NE], I32)
        tiles_before = place("tiles_before", [1, NE], I32)
        tiles_after = place("tiles_after", [1, NE], I32)
        scratch = here[0]

        xrows = place("xrows", [P, TT, D], at=scratch)
        mrow = place("mrow", [4, N_MOD, 256], at=scratch + 4 * TT * D)
        prow = place("prow", [P, 3, P], at=scratch + 4 * TT * D + 4 * 6144)
        off = scratch
        up = place("up", [P, NC, 648], at=off)
        off += 4 * NC * 648
        xc = place("xc", [P, NC, 648], at=off)
        off += 4 * NC * 648
        ga = place("ga", [P, NC, T], at=off)
        off += 4 * NC * T
        ub = place("ub", [P, NC, UB_W], at=off)
        off += 4 * NC * UB_W
        rr = place("rr", [P, NC, T], at=off)
        off += 4 * NC * T
        th = up
        top = off
        g_both = place("g_both", [P, 2, JT, T], F32R, at=scratch)
        g_hi, g_lo = g_both[:, 0], g_both[:, 1]
        top = max(top, scratch + 8 * JT * T)
        off = scratch
        vp = place("vp", [P, NC, 656], at=off)
        off += 4 * NC * 656
        gp = place("gp", [P, NC, 688], at=off)
        off += 4 * NC * 688
        qf = place("qf", [P, NC, T], at=off)
        off += 4 * NC * T
        mrow1 = place("mrow1", [4, N_MOD, 256], at=scratch)
        kf = place("kf", [P, T], at=off)
        off += 4 * T
        vf = place("vf", [P, T], at=off)
        off += 4 * T
        pp = place("pp", [P, 2, T], at=off)
        hspread = place("hspread", [10, 5, P], at=off)
        hrs = place("hrs", [10, T], at=off + 4 * T)
        off += 8 * T
        kk = place("kk", [P, T], at=off)
        off += 4 * T
        vt = place("vt", [P, 6, P], at=off)
        off += 24 * P
        cos_t = place("cos_t", [P, TS], at=off)
        off += 4 * TS
        sin_t = place("sin_t", [P, TS], at=off)
        off += 4 * TS
        krow = place("krow", [P, P], at=off)
        off += 4 * P
        knew = place("knew", [P, P], at=off)
        off += 4 * P
        hsel = place("hsel", [P, 5, 16], at=off)
        off += 320
        am = place("am", [P, 4, 2], at=off)
        off += 32
        top = max(top, off)
        pt = place("pt", [P, 2, 5, TS], at=at_raw)
        ptp = place("ptp", [P, 2, P], at=at_raw + 40 * TS)
        hf = place("hf", [P, KT, T], at=scratch)
        hrows = place("hrows", [P, TT, D], at=scratch + 4 * KT * T)
        iota_t = place("iota_t", [P, T], at=scratch + 8 * KT * T)
        hot = [place("hot0", [P, TT, T], F32R, at=scratch + 8 * KT * T + 4 * T),
               place("hot1", [P, TT, T], F32R, at=scratch)]
        top = max(top, scratch + 8 * KT * T + 4 * T + 4 * TT * T)
        scratch_end, here[0] = here[0], at_hi + 8192
        lg = place("lg", [P, TT, NE])
        mx8 = place("mx8", [P, TT, 8])
        ix8 = place("ix8", [P, TT, 8], U32)
        ixf = place("ixf", [P, TT, 2])
        gw = place("gw", [P, TT, 2])
        comb = place("comb", [P, TT, NE])
        members = place("members", [P, 2, TT, NE])
        both = place("both", [P, TT, NE])
        rank = place("rank", [P, TT, NE])
        slotf = place("slotf", [P, TT, 2])
        tok_w = place("tok_w", [P, TT, NE, 4], F32R)
        base8 = place("base8", [P, NE])
        cnt = place("cnt", [P, 3 + len(SIZES), NE])
        lgt = place("lgt", [NE, T])
        info_t = place("info_t", [4, T])
        assert here[0] <= at_hi + 16384
        here[0] = scratch_end
        rows_g = place("rows_g", [P, 2, D], at=at_raw)
        rows_y = place("rows_y", [P, 2, TT, P], at=at_hi)
        yb = place("yb", [P, 2, T], at=at_hi + 8192)
        rows_c = place("rows_c", [P, TT, 2, D], at=scratch)
        yrows = place("yrows", [P, TT, D], at=scratch)
        h_dram = nc.dram_tensor("h_rows", (T, D), F32).ap()
        y_dram = nc.dram_tensor("y_rows", (Y_TILES, P, D), F32).ap()
        assert top <= nc.sbuf_usable_end, (top, nc.sbuf_usable_end)

        ps = ctx.enter_context(nc.psum_tensor("ps", [P, 8, 512], F32))

        x_in = sem("x_in")
        rows_in = sem("rows_in")
        mats_in = sem("mats_in")
        small_in = sem("small_in")
        slot_in = [[sem(f"slot_{s}{h}_in") for h in range(2)] for s in "abc"]
        stored = sem("stored")
        hi_done = sem("hi_done")
        lo_done = sem("lo_done")
        gemm_out = sem("gemm_out")
        evac = sem("evac")
        prow_zero = sem("prow_zero")
        ones_set = sem("ones_set")
        x_turned = sem("x_turned")
        x_kept = sem("x_kept")
        par_turned = sem("par_turned")
        par_kept = sem("par_kept")
        cs_silu = sem("cs_silu")
        cs_split = sem("cs_split")
        csz = sem("csz")
        folded = sem("folded")
        mod_set = sem("mod_set")
        n_sq = sem("n_sq")
        n_mm = sem("n_mm")
        n_var = sem("n_var")
        n_std = sem("n_std")
        n_rs = sem("n_rs")
        n_t = sem("n_t")
        n_aff = sem("n_aff")
        n_hi = sem("n_hi")
        n_lo = sem("n_lo")
        pads = sem("pads")
        ab_lam = sem("ab_lam")
        ex_lam = sem("ex_lam")
        sp_ready = sem("sp_ready")
        chain = sem("chain")
        e_xc = sem("e_xc")
        e_pool = sem("e_pool")
        e_pmm = sem("e_pmm")
        e_gate = sem("e_gate")
        e_sig = sem("e_sig")
        e_tanh = sem("e_tanh")
        e_exp = sem("e_exp")
        e_a2 = sem("e_a2")
        e_q = sem("e_q")
        e_sqrt = sem("e_sqrt")
        e_scan = sem("e_scan")
        e_y = sem("e_y")
        e_yhi = sem("e_yhi")
        e_ylo = sem("e_ylo")
        st_last = sem("st_last")
        st_turned = sem("st_turned")
        st_kept = sem("st_kept")
        odd_in = sem("odd_in")
        gp_pads = sem("gp_pads")
        gp_set = sem("gp_set")
        o_sq = sem("o_sq")
        o_sum = sem("o_sum")
        o_var = sem("o_var")
        o_std = sem("o_std")
        o_rs = sem("o_rs")
        o_spread = sem("o_spread")
        o_qn = sem("o_qn")
        o_swap = sem("o_swap")
        o_sw_read = sem("o_sw_read")
        o_rope = sem("o_rope")
        v_turned = sem("v_turned")
        v_kept = sem("v_kept")
        c_dve = sem("c_dve")
        c_pool = sem("c_pool")
        pchain = sem("pchain")
        kv_stored = sem("kv_stored")
        a_s = sem("a_s")
        a_max = sem("a_max")
        a_exp = sem("a_exp")
        a_norm = sem("a_norm")
        a_t = sem("a_t")
        a_kept = sem("a_kept")
        a_kept5 = sem("a_kept5")
        a_pv = sem("a_pv")
        a_ohi = sem("a_ohi")
        a_olo = sem("a_olo")
        l_mean = sem("l_mean")
        l_xc = sem("l_xc")
        l_sq = sem("l_sq")
        l_vmm = sem("l_vmm")
        l_var = sem("l_var")
        l_std = sem("l_std")
        l_y = sem("l_y")
        l_silu = sem("l_silu")
        l_hi = sem("l_hi")
        l_lo = sem("l_lo")
        wr_h = sem("wr_h")
        wr_l = sem("wr_l")
        r_mm = sem("r_mm")
        r_mm_kept = sem("r_mm_kept")
        r_turned = sem("r_turned")
        r_members = sem("r_members")
        r_ranks = sem("r_ranks")
        r_d = sem("r_d")
        r_exp = sem("r_exp")
        r_tables = sem("r_tables")
        r_hot = sem("r_hot")
        r_info = sem("r_info")
        r_info_kept = sem("r_info_kept")
        r_info_turned = sem("r_info_turned")
        r_ids = sem("r_ids")
        ht_turned = sem("ht_turned")
        ht_kept = sem("ht_kept")
        iota_in = sem("iota_in")
        zeros_set = sem("zeros_set")
        y_zero = sem("y_zero")
        ids_copied = sem("ids_copied")
        g_rows = sem("g_rows")
        g_turned = sem("g_turned")
        g_hi_kept = sem("g_hi_kept")
        g_lo_kept = sem("g_lo_kept")
        y_turned = sem("y_turned")
        y_rows = sem("y_rows")
        out_rows = [sem("out_rows_a"), sem("out_rows_b")]
        h_stored = sem("h_stored")
        c_rows = [sem(f"c_rows_{t}") for t in range(TT)]
        c_sum = sem("c_sum")
        c_turned = sem("c_turned")
        c_added = sem("c_added")
        z_y = sem("z_y")
        z_turned = sem("z_turned")
        z_kept = sem("z_kept")
        f_silu = sem("f_silu")
        f_hi = sem("f_hi")
        f_lo = sem("f_lo")

        OIN_NEXT = [(C_SLOT, OIN + 2, CC[OIN]), (A_SLOT, OIN + 3, AB[OIN] + 4), (B_SLOT, OIN + 4, AB[OIN] + 4),
                    (A_SLOT, OIN + 5, AB[OIN] + 5), (B_SLOT, OIN + 6, AB[OIN] + 5),
                    (A_SLOT, OOUT, AB[OOUT] + 1), (B_SLOT, OOUT + 1, AB[OOUT] + 1)]

        block = ctx.enter_context(nc.Block())
        ident = mats[:, IDENT, :]

        def sil(h, width=TH):
            return tmp[:, h, 0:width]

        def gf(h, width=TH):
            return tmp[:, 2 + h, 0:width]

        def wait_apart(eng, signal, value):
            value = eng.snap(eng.to_reg(value))
            eng.wait_ge(mats_in, 16)
            eng.wait_ge(signal, value)

        def wide(width, halves):
            return halves == 1 and 2 * width <= 512

        def gather_tiles(width, halves):
            total = T if halves == 2 else width
            return [(g, min(P, total - P * g)) for g in range((total + P - 1) // P)]

        def gate_of(layer, which, m, c):
            return mod[:, layer, 16 + 24 * which + m, c:c + 1] if isinstance(m, int) else \
                mod[:, layer, bass.ds(16 + 24 * which + m, 1), c:c + 1].rearrange("p a b -> p (a b)")

        @block.sync
        def _(sp):
            def load(slot, raw_free, pieces):
                for i, (dst, src) in enumerate(pieces):
                    part = 2 * i // len(pieces)
                    if raw_free is not None and i in (0, len(pieces) // 2):
                        sp.wait_ge(mats_in, 16)
                        sp.wait_ge(lo_done, raw_free - 1 + part)
                    sp.dma_start(dst, src).then_inc(slot_in[slot][part], 16)

            def columns(w, col, n=256):
                v = w.rearrange("(k p) c -> p k c", p=P)
                h = KT // 2
                return lambda slot: [
                    (raw[slot][:, i * h * n:(i + 1) * h * n].rearrange("p (k c) -> p k c", k=h),
                     v[:, i * h:(i + 1) * h, bass.ds(col, n)]) for i in range(2)]

            def pairs(stage, n_pairs, w, start=0):
                with sp.Fori(start, n_pairs) as pr:
                    for u in range(2):
                        load(u, 2 * (stage - 1) + 4 * pr + 2 * u, columns(w, (2 * pr + u) * 256)(u))

            def item(w1, w3, w2, col, row, n):
                def up_proj(j, slot):
                    return [(raw[slot][:, i * D:(i + 1) * D].rearrange("p (k c) -> p k c", k=KT),
                             w.rearrange("(k p) c -> p k c", p=P)[:, :, bass.ds(col + j * P, P)])
                            for i, w in enumerate((w1, w3))]

                def down_proj(m, slot):
                    v = w2.rearrange("(k p) c -> p k c", p=P)
                    return [(raw[slot][:, at:at + (k1 - k0) * P].rearrange("p (k c) -> p k c", k=k1 - k0),
                             v[:, bass.ds(row + k0, k1 - k0), bass.ds(m * P, P)]) for k0, k1, at in ((0, JH, 0), (JH, JT, D))]

                with sp.Fori(0, JT // 2) as pr:
                    for u in range(2):
                        load(u, 2 * (n - 1) + 4 * pr + 2 * u, up_proj(2 * pr + u, u))
                load(C_SLOT, 2 * (n + JT - 2), up_proj(JT - 1, C_SLOT))
                load(A_SLOT, 2 * (n + JT - 2), down_proj(0, A_SLOT))
                load(B_SLOT, 2 * (n + JT - 1), down_proj(1, B_SLOT))
                with sp.Fori(1, KT // 2) as pr:
                    for u in range(2):
                        load(u, 2 * (n + JT - 1) + 4 * pr + 2 * u, down_proj(2 * pr + u, u))

            for i in range(2):
                load(i, None, columns(a["w_mod"][0], i * 256)(i))
            pairs(M0, N_MOD // 2, a["w_mod"][0], 1)
            pairs(EIN, 3, a["ev_w_in"][0])
            pairs(EOUT, 2, a["ev_w_out"][0])
            with sp.Fori(0, 2) as f:
                item(a["ff_w1"][0], a["ff_w3"][0], a["ff_w2"][0], f * D_FFE, f * JT, FF + N_ITEM * f)

            pairs(M1, N_MOD // 2, a["w_mod"][1])

            sp.wait_ge(evac, 2 * M1)
            sp.dma_start(cos_t[:, :], a["const_cos"]).then_inc(odd_in, 16)
            sp.dma_start(sin_t[:, :], a["const_sin"]).then_inc(odd_in, 16)
            sp.dma_start(krow[:, :], a["cache_k"][0, 0].rearrange("t h d -> t (h d)")).then_inc(odd_in, 16)
            sp.dma_start(vt[:, 1, :], a["cache_v"][0, 0].rearrange("t h d -> t (h d)")).then_inc(odd_in, 16)
            sp.dma_start(hsel[:, :, :], a["const_hsel"]).then_inc(odd_in, 16)
            sp.dma_start(hspread[:, :, :], a["const_hspread"]).then_inc(odd_in, 16)

            w = a["od_w_in"][0]
            wv = w.rearrange("(k p) c -> p k c", p=P)

            def q_columns(slot, c):
                dst = raw[slot][:, :].rearrange("p (k j e d) -> p k j e d", k=KT, j=2, e=2)
                src = wv[:, :, 2 * D_A:2 * D_A + 512].rearrange("p k (e j d) -> p k e j d", e=2, j=4)
                return [(dst[:, k:k + 4, j, e, :], src[:, k:k + 4, e, 2 * c + j, :]) for k in (0, 4) for j in range(2) for e in range(2)]

            load(A_SLOT, 2 * (OIN - 1), q_columns(A_SLOT, 0))
            load(B_SLOT, 2 * OIN, q_columns(B_SLOT, 1))
            load(C_SLOT, None, columns(w, 2 * D_A + 512)(C_SLOT))
            for c in range(3, 7):
                load((c - 3) % 2, 2 * (OIN + (0, 1, 3, 4)[c - 3] + 1), columns(w, (c - 3) * 256)((c - 3) % 2))

            wo = a["od_w_out"][0]

            def out_columns(slot, c):
                v = wo[0:D_A, :].rearrange("(k p) c -> p k c", p=P)
                u = wo[D_A:D, :].rearrange("(e k d) c -> e d k c", e=2, d=HD)
                dst = raw[slot][:, :].rearrange("p (k c) -> p k c", k=KT)
                cols = slice(c * 256, (c + 1) * 256)
                return [(dst[:, 0:2, :], v[:, 0:2, cols]), (dst[:, 2:4, :], v[:, 2:4, cols])] + [
                    (dst[e * HD:(e + 1) * HD, 4:8, :], u[e, :, :, cols]) for e in range(2)]

            for c in range(4):
                load(c % 2, 2 * (OIN + (5, 6, 7, 8)[c] + 1), out_columns(c % 2, c))

            with sp.Fori(0, NE) as e:
                item(a["moe_w1"][0, bass.ds(e, 1)].rearrange("o a b -> (o a) b"), a["moe_w3"][0, bass.ds(e, 1)].rearrange("o a b -> (o a) b"),
                     a["moe_w2"][0, bass.ds(e, 1)].rearrange("o a b -> (o a) b"), 0, 0, MOE + N_ITEM * e)

            sp.wait_ge(st_kept, 1)
            sp.dma_start(a["new_state"].rearrange("b e n (c p) -> (b e n c) p", p=P), sm[0:8, 0:16, :].rearrange("p a b -> p (a b)")).then_inc(stored, 16)
            for t in range(TT):
                sp.wait_ge(z_kept, 2 * (t + 1))
                dst = a["y_prompt"][0] if t == 0 else a["y_sample"][0, (t - 1) * P:t * P, :]
                sp.dma_start(dst, yrows[:, t, :]).then_inc(stored, 16)
            sp.wait_ge(stored, 16 * (1 + TT))

        @block.scalar
        def _(act):
            act.dma_start(mats[:, :, :], a["const_mats"].rearrange("m p c -> p m c")).then_inc(mats_in, 16)
            act.wait_ge(prow_zero, 1)
            rows = [
                (0, 0, 96, a["b_mod"].rearrange("l (j p) -> (l j) p", p=P)),
                (0, N1, 16, a["norm1"].rearrange("l (j p) -> (l j) p", p=P)),
                (0, N2, 16, a["norm2"].rearrange("l (j p) -> (l j) p", p=P)),
                (1, NF, 8, a["norm_f"].rearrange("(j p) -> j p", p=P)),
                (1, ACW, 16, a["a_conv_w"][0].rearrange("t (c p) -> (t c) p", p=P)),
                (1, ACB, 4, a["a_conv_b"][0].rearrange("(c p) -> c p", p=P)),
                (1, BR, 8, a["a_b_r"][0].rearrange("n (c p) -> (n c) p", p=P)),
                (1, BI, 8, a["a_b_i"][0].rearrange("n (c p) -> (n c) p", p=P)),
                (1, LAM, 8, a["a_lam"][0].rearrange("n (c p) -> (n c) p", p=P)),
                (1, BSC, 4, a["b_scale"][0].rearrange("(c p) -> c p", p=P)),
                (1, CCB, 4, a["c_conv_b"][0].rearrange("(c p) -> c p", p=P)),
                (1, LNG, 4, a["c_ln_g"][0].rearrange("(c p) -> c p", p=P)),
                (1, LNB, 4, a["c_ln_b"][0].rearrange("(c p) -> c p", p=P)),
                (1, CS, 8, a["c"][0].rearrange("(c p) -> c p", p=P)),
                (1, CX, 8, a["c_ctx"].rearrange("(c p) -> c p", p=P)),
                (1, ST, 8, a["state_rglru"][0, 0].rearrange("n (c p) -> (n c) p", p=P)),
                (2, 0, 4 * C_CONV, a["c_conv_w"][0].rearrange("t (c p) -> (t c) p", p=P)),
            ]
            for s, r, n, src in rows:
                act.dma_start(prow[r:r + n, s, :], src).then_inc(rows_in, 16)
            for r, src in ((QN, a["q_norm"]), (KN, a["k_norm"])):
                for h in range(2):
                    act.dma_start(prow[r:r + 1, 1, h * HD:(h + 1) * HD], src).then_inc(rows_in, 16)

            def split_hi(slot, n, use, parts=WHOLE, fine=False, which=(0, 1)):
                for h in which:
                    act.wait_ge(slot_in[slot][h], 16 * (use + 1))
                    act.wait_ge(gemm_out, 2 * (n - 2) + (h + 1 if fine else 2))
                    act.activation(hi[slot][:, parts[h]], raw[slot][:, parts[h]], ACT.Copy).then_inc(hi_done, 1)

            for s in range(2):
                for h in range(2):
                    act.wait_ge(slot_in[s][h], 16)
                    act.activation(hi[s][:, h * 1024:(h + 1) * 1024], raw[s][:, h * 1024:(h + 1) * 1024],
                                   ACT.Copy).then_inc(hi_done, 1)
            act.wait_ge(par_kept, 1)
            act.activation(cs[:, 0, :], par[:, 1, CX:CX + KT], ACT.Silu)
            act.activation(cs[:, 1, :], par[:, 1, CS:CS + KT], ACT.Silu).then_inc(cs_silu, 1)

            def mod_evac(slot, n, q, mrow=mrow):
                act.wait_ge(gemm_out, 2 * n + 2)
                act.activation(mrow[:, bass.ds(q, 1), :].rearrange("p a c -> p (a c)"), ps[0:4, 4 * slot, 0:256], ACT.Copy).then_inc(evac, 2)

            def mod_pairs(start, end):
                with act.Fori(start, end) as pr:
                    for u in range(2):
                        n = 2 * pr + u
                        mod_evac(u, n, n)
                        split_hi(u, n + 2, pr + 1, fine=True)

            mod_pairs(0, X_AFTER)
            for g in range(1, 10, 2):
                act.wait_ge(x_turned, g + 1)
                act.wait_ge(x_kept, g)
                t, q = g // 2, g % 2
                act.activation(xT[:, 4 * q:4 * q + 4, t * P:(t + 1) * P],
                               ps[:, 1 + g % 3, :].rearrange("p (k c) -> p k c", k=4), ACT.Copy).then_inc(x_kept, 1)
            mod_pairs(X_AFTER, N_MOD // 2)
            act.wait_ge(ab_lam, 1)
            act.activation(sm[:, 1, :], sm[:, 0, :], ACT.Exp, scale=-1.0).then_inc(ex_lam, 1)

            def squares(i, ready):
                for k in range(KT):
                    if k >= 4:
                        act.wait_ge(n_mm, KT * i + k - 3)
                    act.wait_ge(*ready(k))
                    act.activation(tmp[:, k % 4, 0:T], xT[:, k, :], ACT.Square).then_inc(n_sq, 1)

            def norm_act(i, ready, h=None):
                if i:
                    act.wait_ge(n_lo, KT * i)
                squares(i, ready)
                act.wait_ge(n_var, i + 1)
                act.activation(rs[:, :], rs[:, :], ACT.Sqrt).then_inc(n_std, 1)
                for k in range(KT):
                    act.wait_ge(n_aff, KT * i + k + 1)
                    act.activation(hh[:, k, :], tmp[:, k % 2, 0:T] if h is None else h[:, k, :], ACT.Copy).then_inc(n_hi, 1)

            act.wait_ge(small_in, 16 * 15)
            act.activation(wr_hi[:, :, :], wr_raw[:, :, :], ACT.Copy).then_inc(wr_h, 1)
            norm_act(0, lambda k: (x_kept, 10))

            act.wait_ge(pads, 2)
            for c in range(6):
                n, slot = EIN + c, c % 2
                for h in range(2):
                    act.wait_ge(gemm_out, 2 * n + h + 1)
                    for i in range(2):
                        m = 2 * c + i
                        last = None
                        for lo_t, hi_t, cond in HALF_SEGS[h]:
                            src = ps[:, 4 * slot + 2 * h + i, lo_t - TH * h:hi_t - TH * h]
                            s0, p0 = (0, TP)[cond], 0
                            if m < 4:
                                p0 = (UA_P, UA_S)[cond] + lo_t - s0
                                last = act.activation(up[:, m, p0:p0 + hi_t - lo_t], src, ACT.Copy)
                            elif m < 8:
                                last = act.activation(ga[:, m - 4, lo_t:hi_t], src, ACT.Gelu_apprx_tanh)
                            else:
                                p0 = (UB_P, UB_S)[cond] + lo_t - s0
                                last = act.activation(ub[:, m - 8, p0:p0 + hi_t - lo_t], src, ACT.Copy)
                    last.then_inc(evac, 1)
                split_hi(slot, n + 2, AB[EIN] + 1 + c // 2)

            for n in range(2):
                for c in range(NC):
                    it = NC * n + c
                    act.wait_ge(e_gate, it + 1)
                    if n:
                        act.wait_ge(e_scan, c + 1)
                    for kind, (dst, b) in enumerate(((rr, BR), (ii, BI))):
                        for (lo_t, hi_t, cond) in SEGS:
                            last = act.activation(dst[:, c, lo_t:hi_t], ps[:, 4 * (it % 2) + 2 * kind + cond, 0:hi_t - lo_t],
                                                  ACT.Sigmoid, bias=par[:, 1, b + it:b + it + 1])
                    last.then_inc(e_sig, 1)
                act.wait_ge(sp_ready, 1)
                for c in range(NC):
                    it = NC * n + c
                    act.wait_ge(e_sig, NC * (n + 1))
                    act.wait_ge(e_xc, NC)
                    if n:
                        act.wait_ge(e_scan, NC)
                    act.activation(th[:, c, 0:T], rr[:, c, :], ACT.Tanh, scale=sm[:, 6, it:it + 1]).then_inc(e_tanh, 1)
                    act.wait_ge(e_tanh, it + 1)
                    act.activation(rr[:, c, :], rr[:, c, :], ACT.Exp, scale=sm[:, 7, it:it + 1]).then_inc(e_exp, 1)
                for c in range(NC):
                    it = NC * n + c
                    act.wait_ge(e_q, it + 1)
                    act.activation(th[:, c, 0:T], th[:, c, 0:T], ACT.Sqrt).then_inc(e_sqrt, 1)
            act.wait_ge(st_turned, 1)
            act.activation(sm[0:8, 0:16, :].rearrange("p a b -> p (a b)"), ps[0:8, 2, 0:P], ACT.Copy).then_inc(st_kept, 1)
            for c in range(NC):
                act.wait_ge(e_y, c + 1)
                act.activation(hh[:, c, :], tmp[:, 2 + c % 2, 0:T], ACT.Copy).then_inc(e_yhi, 1)

            for c in range(4):
                split_hi(c % 2, EOUT + c + 2, (AB[EOUT] + 1 + c // 2) if c < 2 else AB[FF])
            norm_act(1, lambda k: (evac, 2 * (EOUT + k // 2 + 1)))

            def ff13_evac(slot, n, j, f):
                for h in range(2):
                    act.wait_ge(gemm_out, 2 * n + h + 1)
                    act.activation(sil(h), ps[:, 4 * (slot % 2) + 2 * h, 0:TH], ACT.Silu).then_inc(f_silu, 1)
                for h in range(2):
                    act.wait_ge(evac, 2 * n + h + 1)
                    act.activation(g_hi[:, bass.ds(j, 1), h * TH:(h + 1) * TH].rearrange("p a c -> p (a c)"),
                                   gf(h), ACT.Copy).then_inc(f_hi, 1)

            with act.Fori(0, 2) as f:
                n0, u0 = FF + N_ITEM * f, AB[FF] + AB_ITEM * f
                with act.Fori(0, JT // 2 - 1) as pr:
                    for u in range(2):
                        ff13_evac(u, n0 + 2 * pr + u, 2 * pr + u, f)
                        split_hi(u, n0 + 2 * pr + u + 2, u0 + pr + 1)
                ff13_evac(A_SLOT, n0 + JT - 3, JT - 3, f)
                split_hi(C_SLOT, n0 + JT - 1, f)
                ff13_evac(B_SLOT, n0 + JT - 2, JT - 2, f)
                split_hi(A_SLOT, n0 + JT, u0 + JT // 2, DOWN)
                ff13_evac(C_SLOT, n0 + JT - 1, JT - 1, f)
                split_hi(B_SLOT, n0 + JT + 1, u0 + JT // 2, DOWN)
                with act.Fori(0, KT // 2 - 1) as pr:
                    for u in range(2):
                        split_hi(u, n0 + JT + 2 + 2 * pr + u, u0 + JT // 2 + 1 + pr, DOWN)
                for u in range(2):
                    split_hi(u, n0 + N_ITEM + u, u0 + AB_ITEM)

            act.wait_ge(evac, 2 * M1)
            with act.Fori(0, N_MOD // 2 - 1) as pr:
                for u in range(2):
                    mod_evac(u, M1 + 2 * pr + u, 2 * pr + u, mrow1)
                    split_hi(u, M1 + 2 * pr + u + 2, AB[M1] + pr + 1, fine=True)
            for u in range(2):
                mod_evac(u, M1 + N_MOD - 2 + u, N_MOD - 2 + u, mrow1)
                split_hi(u, OIN + u, AB[OIN] + 3, fine=True)
            norm_act(2, lambda k: (evac, 2 * M1))

            act.wait_ge(gp_pads, 1)
            for c in range(7):
                n = OIN + c
                for h in range(2):
                    act.wait_ge(gemm_out, 2 * n + h + 1)
                    for i in range(2):
                        bank = 4 * (c % 2) + 2 * h + i
                        if c < 3:
                            dst = (qf[:, 2 * c + i, :] if c < 2 else (kf, vf)[i])
                            last = act.activation(dst[:, h * TH:(h + 1) * TH], ps[:, bank, 0:TH], ACT.Copy)
                        elif c < 5:
                            last = act.activation(vp[:, 2 * (c - 3) + i, h * TH:(h + 1) * TH], ps[:, bank, 0:TH], ACT.Copy)
                        else:
                            for lo_t, hi_t, cond in HALF_SEGS[h]:
                                p0 = (GC_P, GC_S)[cond] + lo_t - (0, TP)[cond]
                                last = act.activation(gp[:, 2 * (c - 5) + i, p0:p0 + hi_t - lo_t],
                                                      ps[:, bank, lo_t - TH * h:hi_t - TH * h], ACT.Sigmoid)
                    last.then_inc(evac, 1)
                split_hi(*OIN_NEXT[c])

            act.wait_ge(n_lo, 3 * KT)
            for i in range(5):
                if i >= 2:
                    act.wait_ge(o_sum, i - 1)
                act.activation(tmp[:, i % 2, 0:T], qf[:, i, :] if i < 4 else kf[:, :], ACT.Square).then_inc(o_sq, 1)
            act.wait_ge(o_var, 1)
            act.activation(hrs[:, :], hrs[:, :], ACT.Sqrt).then_inc(o_std, 1)
            act.wait_ge(v_turned, 1)
            act.activation(vt[:, 2:6, :], ps[:, 4, 0:512].rearrange("p (a b) -> p a b", a=4), ACT.Copy).then_inc(v_kept, 1)

            def kept(s):
                h, t = s // TT, s % TT
                act.wait_ge(a_t, s + 1)
                if h >= 2:
                    act.wait_ge(a_pv, h - 1)
                if t == 0:
                    act.activation(ptp[:, h % 2, :], ps[:, 4, 0:P], ACT.Copy).then_inc(a_kept, 1)
                else:
                    act.activation(pt[:, h % 2, 0:4, (t - 1) * P:t * P], ps[:, 4, 0:512].rearrange("p (k c) -> p k c", k=4),
                                   ACT.Copy).then_inc(a_kept, 1)

            def head_hi(h):
                act.wait_ge(a_pv, h + 1)
                r = slice(HD * (h // 4), HD * (h // 4) + HD)
                act.activation(hh[r, 4 + h % 4, 0:TP], ps[r, 7, 0:TP], ACT.Copy)
                act.activation(hh[r, 4 + h % 4, TP:T], ps[r, 6, 0:TS], ACT.Copy).then_inc(a_ohi, 1)

            for s in range(NH * TT + 8):
                if s >= 12 and (s - 2) % TT == 0:
                    head_hi((s - 12) // TT)
                if s == 4:
                    act.wait_ge(v_kept, 2)
                    act.dma_start(a["new_k"][0, 0].rearrange("t h d -> t (h d)"), knew[:, :]).then_inc(kv_stored, 16)
                    act.dma_start(a["new_v"][0, 0].rearrange("t h d -> t (h d)"), vt[:, 0, :]).then_inc(kv_stored, 16)
                if s < NH * TT:
                    act.wait_ge(a_max, s + 1)
                    if s >= 2:
                        act.wait_ge(a_t, s - 1)
                    width = P if s % TT == 0 else T
                    src = ps[:, 2 * (s % 2), 0:P] if s % TT == 0 else ps[:, 2 * (s % 2):2 * (s % 2) + 2, 0:TH]
                    dst = pp[:, s % 2, 0:width] if s % TT == 0 else pp[:, s % 2, :].rearrange("p (a b) -> p a b", a=2)
                    act.activation(dst, src, ACT.Exp, scale=HD ** -0.5, bias=am[:, 1, s % 2:s % 2 + 1],
                                   accum_out=am[:, 2, s % 2:s % 2 + 1]).then_inc(a_exp, 1)
                if 2 <= s < NH * TT + 2:
                    kept(s - 2)
            for c in range(NC):
                act.wait_ge(l_xc, c + 1)
                if c >= 2:
                    act.wait_ge(l_vmm, c - 1)
                for lo_t, hi_t, cond in SEGS:
                    p0 = (0, GC_S - 15)[cond]
                    last = act.activation(tmp[:, c % 2, lo_t:hi_t], vp[:, c, p0:p0 + hi_t - lo_t], ACT.Square)
                last.then_inc(l_sq, 1)
            act.wait_ge(l_var, 1)
            act.activation(rs[:, :], rs[:, :], ACT.Sqrt).then_inc(l_std, 1)
            for c in range(NC):
                act.wait_ge(l_y, c + 1)
                if c >= 2:
                    act.wait_ge(l_lo, c - 1)
                elif c == 0:
                    act.wait_ge(l_vmm, NC)
                act.activation(tmp[:, c % 2, 0:T], tmp[:, 2 + c % 2, 0:T], ACT.Silu, scale=par[:, 1, LNG + c:LNG + c + 1],
                               bias=par[:, 1, LNB + c:LNB + c + 1]).then_inc(l_silu, 1)
                act.wait_ge(l_silu, c + 1)
                act.activation(hh[:, c, :], tmp[:, c % 2, 0:T], ACT.Copy).then_inc(l_hi, 1)

            for c in range(4):
                split_hi(c % 2, OOUT + c + 2, (AB[OOUT] + 3) if c < 2 else AB[MOE])
            norm_act(3, lambda k: (evac, 2 * (OOUT + k // 2 + 1)), hf)
            act.wait_ge(r_mm, 1)
            act.activation(lgt[:, :].rearrange("p (h t) -> p h t", h=2), ps[0:NE, 4:6, 0:TH], ACT.Copy).then_inc(r_mm_kept, 1)
            for g in range(2 * TT):
                act.wait_ge(ht_turned, g + 1)
                act.activation(hrows[:, g // 2, 512 * (g % 2):512 * (g % 2) + 512], ps[:, g % 4, :], ACT.Copy).then_inc(ht_kept, 1)
                if g == 3:
                    act.wait_ge(r_d, 1)
                    act.activation(gw[:, :, 1], gw[:, :, 1], ACT.Exp).then_inc(r_exp, 1)

            for e in range(NE):
                act.wait_ge(r_info, e + 1)
                if e:
                    act.wait_ge(r_info_turned, e)
                act.activation(info_t[:, :].rearrange("p (h t) -> p h t", h=2), ps[0:4, 4 + 2 * (e % 2):6 + 2 * (e % 2), 0:TH],
                               ACT.Copy).then_inc(r_info_kept, 1)

            def tables(e):
                return (act.value_load(size_of[0:1, bass.ds(e, 1)], min_val=0, max_val=len(SIZES) - 1),
                        act.value_load(tiles_before[0:1, bass.ds(e, 1)], min_val=0, max_val=NE * TT))

            def w13(e, width, halves):
                n0, u0, f = MOE + N_ITEM * e, AB[MOE] + AB_ITEM * e, 2 + e

                fine = halves == 1

                def silu(slot, n, j):
                    if wide(width, halves):
                        act.wait_ge(f_silu, 2 * JT * f + 2 * j + 1)
                        act.activation(sil(0, width), sil(0, width), ACT.Silu).then_inc(f_silu, 1)
                        return
                    for h in range(halves):
                        act.wait_ge(gemm_out, 2 * n + h + 1)
                        act.activation(sil(h, width), ps[:, 4 * (slot % 2) + 2 * h, 0:width], ACT.Silu).then_inc(f_silu, 2 // halves)

                def kept(n, j):
                    for h in range(halves):
                        act.wait_ge(evac, 2 * n + 2 // halves * (h + 1))
                        act.activation(g_hi[:, bass.ds(j, 1), h * TH:h * TH + width].rearrange("p a c -> p (a c)"),
                                       gf(h, width), ACT.Copy).then_inc(f_hi, 2 // halves)

                def step(slot, j, slot_next, use, parts=WHOLE, finely=fine):
                    n = n0 + j
                    early = wide(width, halves) and finely
                    if early:
                        if slot == A_SLOT:
                            act.activation(act_warm[:, 0:1], zeros[0:1, 0:1], ACT.Silu)
                        split_hi(slot_next, n + 2, use, parts, True, (0,))
                    silu(slot, n, j)
                    split_hi(slot_next, n + 2, use, parts, finely, (1,) if early else (0, 1))
                    kept(n, j)

                with act.Fori(0, JT // 2 - 1) as pr:
                    for u in range(2):
                        step(u, 2 * pr + u, u, u0 + pr + 1)
                for u in range(2):
                    act.wait_ge(out_rows[u], 16 + 16 * KT * e)
                step(A_SLOT, JT - 3, C_SLOT, 3 + e)
                step(B_SLOT, JT - 2, A_SLOT, u0 + JT // 2, DOWN)
                step(C_SLOT, JT - 1, B_SLOT, u0 + JT // 2, DOWN)

            def gather(e, width, halves, before):
                for g, rows in gather_tiles(width, halves):
                    act.wait_ge(g_turned, before + g + 1)
                    act.activation(hh[:, :, g * P:g * P + rows].rearrange("p (a b) c -> p a b c", a=2),
                                   ps[:, 2 * (g % 2):2 * (g % 2) + 2, :].rearrange("p a (b c) -> p a b c", b=4)[:, :, :, 0:rows],
                                   ACT.Copy).then_inc(g_hi_kept, 1)

            def w2(e, width, halves, last):
                n0, u0 = MOE + N_ITEM * e, AB[MOE] + AB_ITEM * e
                fine = halves == 1

                def kept(u, n, m):
                    if wide(width, halves):
                        return
                    if m is not None:
                        act.wait_ge(y_turned, KT * e + m - 1)
                    for h in range(halves):
                        act.wait_ge(gemm_out, 2 * n + 2 // halves * (h + 1))
                        act.activation(yb[:, u, h * TH:h * TH + width], ps[:, 4 + 2 * u + h, 0:width], ACT.Copy).then_inc(evac, 2 // halves)

                for u in range(2):
                    split_hi(u, n0 + JT + 2 + u, u0 + JT // 2 + 1, DOWN, fine=fine)
                    kept(u, n0 + JT + u, None)
                with act.Fori(1, KT // 2 - 1) as pr:
                    for u in range(2):
                        split_hi(u, n0 + JT + 2 + 2 * pr + u, u0 + JT // 2 + 1 + pr, DOWN, fine=fine)
                        kept(u, n0 + JT + 2 * pr + u, 2 * pr + u)
                for u in range(2):
                    if not last:
                        split_hi(u, n0 + N_ITEM + u, u0 + AB_ITEM, fine=fine)
                    kept(u, n0 + N_ITEM - 2 + u, KT - 2 + u)

            def expert(e, size, last):
                for i, (width, halves) in enumerate(SIZES):
                    with act.If(size == i):
                        w13(e, width, halves)
                if not last:
                    size_next, before_next = tables(e + 1)
                    for i, (width, halves) in enumerate(SIZES):
                        with act.If(size_next == i):
                            gather(e + 1, width, halves, before_next)
                for i, (width, halves) in enumerate(SIZES):
                    with act.If(size == i):
                        w2(e, width, halves, last)

            act.wait_ge(zeros_set, 1)
            act.wait_ge(r_tables, 1)
            size, before = tables(0)
            for i, (width, halves) in enumerate(SIZES):
                with act.If(size == i):
                    gather(0, width, halves, before)
            with act.Fori(0, NE - 1) as e:
                expert(e, tables(e)[0], False)
            expert(NE - 1, tables(NE - 1)[0], True)

            squares(4, lambda k: (c_added, KT * (TT - 1) + k + 1))
            act.wait_ge(n_var, 5)
            act.activation(rs[:, :], rs[:, :], ACT.Sqrt).then_inc(n_std, 1)
            for g in range(1, 2 * TT, 2):
                act.wait_ge(z_turned, g + 1)
                act.wait_ge(z_kept, g)
                act.activation(yrows[:, g // 2, 512 * (g % 2):512 * (g % 2) + 512], ps[:, g % 4, :], ACT.Copy).then_inc(z_kept, 1)

        @block.tensor
        def _(pe):
            def passes(out, w_hi, w_lo, v_hi, v_lo, first, last):
                pe.matmul(out, w_hi, v_hi, start=first, stop=False, skip_group_check=True)
                pe.matmul(out, w_hi, v_lo, start=False, stop=False, skip_group_check=True)
                return pe.matmul(out, w_lo, v_hi, start=False, stop=last, skip_group_check=True)

            def passes_wide(bank, width, w_hi, w_lo, both, first, last):
                pe.matmul(ps[:, bank, 0:2 * width].rearrange("p (a c) -> p a c", a=2), w_hi, both, start=first, stop=False, skip_group_check=True)
                return pe.matmul(ps[:, bank, 0:width], w_lo, both[:, 0], start=False, stop=last, skip_group_check=True)

            def begin(n):
                pe.wait_ge(lo_done, 2 * n + 1)
                pe.wait_ge(evac, 2 * (n - 1))

            def second(n):
                pe.wait_ge(lo_done, 2 * n + 2)

            def down(slot, k, of):
                at = k * P if k < JH else D + (k - JH) * P
                return of[slot][:, at:at + P]

            def mod_chunk(slot, n):
                wh = hi[slot][:, :].rearrange("p (k c) -> p k c", k=KT)
                wl = lo[slot][:, :].rearrange("p (k c) -> p k c", k=KT)
                for k in range(KT):
                    if k == KT // 2:
                        last.then_inc(gemm_out, 1)
                        second(n)
                    pe.matmul(ps[0:4, 4 * slot, 0:256], cs_hl[:, k, :], wh[:, k, :], start=k == 0, stop=False, skip_group_check=True)
                    last = pe.matmul(ps[0:4, 4 * slot, 0:256], cs_h0[:, k, :], wl[:, k, :], start=False, stop=k == KT - 1, skip_group_check=True)
                last.then_inc(gemm_out, 1)

            def gemm_pair(slot, n, ready=None, bank=None):
                wh = hi[slot][:, :].rearrange("p (k c) -> p k c", k=KT)
                wl = lo[slot][:, :].rearrange("p (k c) -> p k c", k=KT)
                bank = 4 * (slot % 2) if bank is None else bank
                for h in range(2):
                    for i in range(2):
                        for k in range(KT):
                            if ready and h == 0 and i == 0:
                                pe.wait_ge(ready[0], ready[1] + k + 1)
                            if h == 0 and i == 0 and k == KT // 2:
                                second(n)
                            last = passes(ps[:, bank + 2 * h + i, 0:TH], wh[:, k, i * P:(i + 1) * P], wl[:, k, i * P:(i + 1) * P],
                                          hh[:, k, h * TH:(h + 1) * TH], hl[:, k, h * TH:(h + 1) * TH], k == 0, k == KT - 1)
                    last.then_inc(gemm_out, 1)

            def gemm_tiles(slot, tiles, start, ready=None):
                wh = hi[slot][:, :].rearrange("p (k c) -> p k c", k=KT)
                wl = lo[slot][:, :].rearrange("p (k c) -> p k c", k=KT)
                for h in range(2):
                    for i in range(2):
                        for k in tiles:
                            if ready and h == 0 and i == 0:
                                pe.wait_ge(ready[0], ready[1] + k + 1)
                            last = passes(ps[:, 4 * slot + 2 * h + i, 0:TH], wh[:, k, i * P:(i + 1) * P], wl[:, k, i * P:(i + 1) * P],
                                          hh[:, k, h * TH:(h + 1) * TH], hl[:, k, h * TH:(h + 1) * TH],
                                          start and k == tiles[0], not start and k == tiles[-1])
                    if not start:
                        last.then_inc(gemm_out, 1)

            def norm_pe(i):
                for k in range(KT):
                    pe.wait_ge(n_sq, KT * i + k + 1)
                    for h in range(2):
                        last = pe.matmul(ps[:, h, 0:TH], ones[:, :], tmp[:, k % 4, h * TH:(h + 1) * TH],
                                         start=k == 0, stop=k == KT - 1, skip_group_check=True)
                    last.then_inc(n_mm, 1)

            pe.wait_ge(mats_in, 16)
            pe.wait_ge(rows_in, 16 * 21)
            for s in range(3):
                last = pe.transpose(ps[:, 5, s * P:(s + 1) * P], prow[:, s, :], ident)
            last.then_inc(par_turned, 1)
            pe.wait_ge(cs_split, 1)
            for s in range(2):
                pe.wait_ge(lo_done, 2 * s + 1)
                mod_chunk(s, s)
            with pe.Fori(1, X_AFTER + 1) as pr:
                for u in range(2):
                    begin(2 * pr + u)
                    mod_chunk(u, 2 * pr + u)
            pe.wait_ge(x_in, 16 * TT)
            for g in range(10):
                t, q = g // 2, g % 2
                if g >= 3:
                    pe.wait_ge(x_kept, g - 2)
                for k in range(4):
                    last = pe.transpose(ps[:, 1 + g % 3, k * P:(k + 1) * P], xrows[:, t, (4 * q + k) * P:(4 * q + k + 1) * P], ident)
                last.then_inc(x_turned, 1)
            with pe.Fori(X_AFTER + 1, N_MOD // 2) as pr:
                for u in range(2):
                    begin(2 * pr + u)
                    mod_chunk(u, 2 * pr + u)
            pe.wait_ge(evac, 2 * N_MOD)
            pe.wait_ge(small_in, 16 * 15)

            def fold(mrow):
                for j in range(48):
                    last = pe.matmul(ps[:, 5, 2 * j:2 * j + 2] if j < 16 else ps[:, 6, 2 * j:2 * j + 2],
                                     mrow[:, j // 2, (j % 2) * P:(j % 2 + 1) * P], sel4[:, :],
                                     start=True, stop=True, skip_group_check=True)
                    if j in (15, 47):
                        last.then_inc(folded, 1)

            norm_pe(0)
            fold(mrow)
            for c in range(6):
                if c == 1:
                    pe.wait_ge(mod_set, 2)
                begin(EIN + c)
                gemm_pair(c % 2, EIN + c, (n_lo, 0) if c == 0 else None)

            pe.wait_ge(evac, 2 * EOUT)
            for it in range(2 * NC):
                n, c = it // NC, it % NC
                pe.wait_ge(e_xc, c + 1)
                if it >= 2:
                    pe.wait_ge(e_sig, it - 1)
                for kind in range(2):
                    for lo_t, hi_t, cond in SEGS:
                        p0 = (0, UA_S - 2)[cond]
                        last = pe.matmul(ps[:, 4 * (it % 2) + 2 * kind + cond, 0:hi_t - lo_t], wg[:, 8 * n + 4 * kind + c, :],
                                         xc[:, c, p0:p0 + hi_t - lo_t], start=True, stop=True)
                last.then_inc(e_gate, 1)
            pe.wait_ge(e_sig, 2 * NC)
            for g in range(NC):
                pe.wait_ge(e_pool, g + 1)
                if g >= 2:
                    pe.wait_ge(e_ylo, g - 1)
                for lo_t, hi_t, cond in SEGS:
                    p0 = (UB_P, UB_S)[cond]
                    last = pe.matmul(ps[:, 2 * (g % 2) + cond, 0:hi_t - lo_t], wp[:, g, :], ub[:, g, p0:p0 + hi_t - lo_t],
                                     start=True, stop=True)
                last.then_inc(e_pmm, 1)
            pe.wait_ge(e_ylo, NC)
            for u in (1, 0):
                if u == 0:
                    pe.wait_ge(st_last, 1)
                    pe.transpose(ps[0:8, 2, 0:P], sm[:, 8, :], ident).then_inc(st_turned, 1)
                    pe.wait_ge(st_kept, 1)
                begin(EOUT + u)
                second(EOUT + u)
                gemm_tiles(u, range(NC, KT), True)
            for u in range(2):
                gemm_tiles(u, range(NC), False, (e_ylo, NC))
            for c in range(2, 4):
                begin(EOUT + c)
                gemm_pair(c % 2, EOUT + c)
            pe.wait_ge(evac, 2 * (EOUT + 3))
            norm_pe(1)

            def ff13(slot, n, ready=None):
                begin(n)
                wh = hi[slot][:, :].rearrange("p (w k c) -> p w k c", w=2, k=KT)
                wl = lo[slot][:, :].rearrange("p (w k c) -> p w k c", w=2, k=KT)
                for h in range(2):
                    for w in range(2):
                        if h == 0 and w == 1:
                            second(n)
                        for k in range(KT):
                            if ready and h == 0 and w == 0:
                                pe.wait_ge(ready[0], ready[1] + k + 1)
                            last = passes(ps[:, 4 * (slot % 2) + 2 * h + w, 0:TH], wh[:, w, k, :], wl[:, w, k, :],
                                          hh[:, k, h * TH:(h + 1) * TH], hl[:, k, h * TH:(h + 1) * TH], k == 0, k == KT - 1)
                    last.then_inc(gemm_out, 1)

            def ff2(slot, n, hidden):
                begin(n)
                for h in range(2):
                    for k in range(JT):
                        if h == 0 and k == JH:
                            second(n)
                        if h == 0 and k == JT - 1:
                            pe.wait_ge(f_lo, hidden)
                        if k == 0 and h == 0:
                            pe.wait_ge(f_lo, hidden - 2)
                        last = passes(ps[:, 4 + 2 * slot + h, 0:TH], down(slot, k, hi), down(slot, k, lo),
                                      g_hi[:, k, h * TH:(h + 1) * TH], g_lo[:, k, h * TH:(h + 1) * TH], k == 0, k == JT - 1)
                    last.then_inc(gemm_out, 1)

            with pe.Fori(0, 2) as f:
                n0 = FF + N_ITEM * f
                with pe.Fori(0, JT // 2) as pr:
                    for u in range(2):
                        ff13(u, n0 + 2 * pr + u, (n_lo, KT) if u == 0 else None)
                ff13(C_SLOT, n0 + JT - 1)
                with pe.Fori(0, KT // 2) as pr:
                    for u in range(2):
                        ff2(u, n0 + JT + 2 * pr + u, 2 * JT * (f + 1))

            with pe.Fori(0, N_MOD // 2) as pr:
                for u in range(2):
                    begin(M1 + 2 * pr + u)
                    mod_chunk(u, M1 + 2 * pr + u)
            pe.wait_ge(evac, 2 * OIN)
            norm_pe(2)
            fold(mrow1)
            for c in range(7):
                if c == 1:
                    pe.wait_ge(mod_set, 4)
                begin(OIN + c)
                gemm_pair((A_SLOT, B_SLOT, C_SLOT, A_SLOT, B_SLOT, A_SLOT, B_SLOT)[c], OIN + c, (n_lo, 2 * KT) if c == 0 else None, 4 * (c % 2))
            pe.wait_ge(evac, 2 * OOUT)
            pe.wait_ge(odd_in, 16 * 6)
            for i in range(5):
                pe.wait_ge(o_sq, i + 1)
                for h in range(2):
                    last = pe.matmul(ps[0:10, 4 + h, 0:TH], hsel[:, i, 0:10], tmp[:, i % 2, h * TH:(h + 1) * TH],
                                     start=i == 0, stop=i == 4, skip_group_check=True)
                last.then_inc(o_sum, 1)
            pe.wait_ge(o_var, 1)
            for t in range(4):
                last = pe.transpose(ps[:, 4, t * P:(t + 1) * P], vf[:, (t + 1) * P:(t + 2) * P], ident)
            last.then_inc(v_turned, 1)
            pe.transpose(ps[:, 5, 0:P], vf[:, 0:P], ident)
            pe.transpose(ps[:, 5, P:2 * P], krow[:, :], ident)
            pe.wait_ge(o_rs, 1)

            def spread(i):
                if i >= 2:
                    pe.wait_ge(o_qn, i - 1)
                for h in range(2):
                    last = pe.matmul(ps[:, 2 * (i % 2) + h, 0:TH], hspread[:, i, :], hrs[:, h * TH:(h + 1) * TH],
                                     start=True, stop=True)
                last.then_inc(o_spread, 1)

            def swap(i):
                pe.wait_ge(o_qn, i + 1)
                if i >= 2:
                    pe.wait_ge(o_sw_read, i - 1)
                pe.matmul(ps[:, 6 + i % 2, 0:TS], mats[:, SWAP, :], (qf[:, i, :] if i < 4 else kf[:, :])[:, TP:T],
                          start=True, stop=True).then_inc(o_swap, 1)

            for i in range(5):
                spread(i)
                if i >= 1:
                    swap(i - 1)
            swap(4)
            pe.transpose(ps[:, 5, 2 * P:3 * P], kf[:, 0:P], ident).then_inc(v_turned, 1)

            def turn(s):
                pe.wait_ge(a_norm, s + 1)
                if s:
                    pe.wait_ge(a_kept, s)
                if s > 1:
                    pe.wait_ge(a_kept5, s - 1 - (s - 1) // TT)
                if s % TT == 0:
                    pe.transpose(ps[:, 4, 0:P], pp[:, s % 2, 0:P], ident).then_inc(a_t, 1)
                    return
                for k in range(5):
                    last = pe.transpose(ps[:, 4 + k // 4, (k % 4) * P:(k % 4 + 1) * P], pp[:, s % 2, k * P:(k + 1) * P], ident)
                last.then_inc(a_t, 1)

            def weigh(h, k):
                r = slice(HD * (h // 4), HD * (h // 4) + HD)
                if k == 0:
                    pe.wait_ge(a_kept, TT * (h + 1))
                    pe.wait_ge(a_kept5, (TT - 1) * (h + 1))
                    if h:
                        pe.wait_ge(a_ohi, h)
                        pe.wait_ge(a_olo, h)
                    pe.matmul(ps[r, 7, 0:TP], vt[:, 0, r], ptp[:, h % 2, :], start=True, stop=True)
                last = pe.matmul(ps[r, 6, 0:TS], vt[:, 1 + k, r], pt[:, h % 2, k, :], start=k == 0, stop=k == 4, skip_group_check=True)
                if k == 4:
                    last.then_inc(a_pv, 1)

            pe.wait_ge(v_kept, 2)
            pe.wait_ge(o_rope, 5)
            for s in range(NH * TT + 7):
                if s < NH * TT:
                    h, t = s // TT, s % TT
                    r = slice(HD * (h // 4), HD * (h // 4) + HD)
                    if s >= 2:
                        pe.wait_ge(a_exp, s - 1)
                    q = qf[r, h % 4, t * P:(t + 1) * P]
                    if t == 0:
                        last = pe.matmul(ps[:, 2 * (s % 2), 0:P], q, kf[r, 0:P], start=True, stop=True)
                    else:
                        for i in range(2):
                            last = pe.matmul(ps[:, 2 * (s % 2) + i, 0:TH], q, kk[r, i * TH:(i + 1) * TH], start=True, stop=True)
                    last.then_inc(a_s, 1)
                if 2 <= s < NH * TT + 2:
                    turn(s - 2)
                if s >= 7:
                    weigh((s - 7) // TT, (s - 7) % TT)
            pe.wait_ge(c_dve, 3)
            pe.wait_ge(c_pool, 1)
            pe.wait_ge(a_exp, NH * TT)
            for c in range(NC):
                for lo_t, hi_t, cond in SEGS:
                    p0 = (0, GC_S - 15)[cond]
                    last = pe.matmul(ps[:, cond, 0:hi_t - lo_t], ones[:, :], vp[:, c, p0:p0 + hi_t - lo_t],
                                     start=c == 0, stop=c == NC - 1, skip_group_check=True)
            last.then_inc(l_mean, 1)
            for c in range(NC):
                pe.wait_ge(l_sq, c + 1)
                for lo_t, hi_t, cond in SEGS:
                    last = pe.matmul(ps[:, 2 + cond, 0:hi_t - lo_t], ones[:, :], tmp[:, c % 2, lo_t:hi_t],
                                     start=c == 0, stop=c == NC - 1, skip_group_check=True)
                last.then_inc(l_vmm, 1)
            pe.wait_ge(a_olo, NH)
            for u in (1, 0):
                if u == 0:
                    pe.wait_ge(l_var, 1)
                begin(OOUT + u)
                second(OOUT + u)
                gemm_tiles(u, range(NC, KT), True)
            for u in range(2):
                gemm_tiles(u, range(NC), False, (l_lo, 0))
            for c in range(2, 4):
                begin(OOUT + c)
                gemm_pair(c % 2, OOUT + c)
            pe.wait_ge(evac, 2 * (OOUT + 3))
            norm_pe(3)

            pe.wait_ge(wr_l, 1)
            for k in range(KT):
                pe.wait_ge(n_lo, 3 * KT + k + 1)
                for h in range(2):
                    last = passes(ps[0:NE, 4 + h, 0:TH], wr_hi[:, k, :], wr_lo[:, k, :],
                                  hh[:, k, h * TH:(h + 1) * TH], hl[:, k, h * TH:(h + 1) * TH], k == 0, k == KT - 1)
            last.then_inc(r_mm, 1)
            pe.wait_ge(r_mm_kept, 1)
            for t in range(TT):
                last = pe.transpose(ps[:, 4, NE * t:NE * (t + 1)], lgt[:, t * P:(t + 1) * P], ident[0:NE, 0:NE])
            last.then_inc(r_turned, 1)
            for g in range(2 * TT):
                if g >= 4:
                    pe.wait_ge(ht_kept, g - 3)
                for k in range(4):
                    last = pe.transpose(ps[:, g % 4, k * P:(k + 1) * P], hf[:, 4 * (g % 2) + k, (g // 2) * P:(g // 2 + 1) * P], ident)
                last.then_inc(ht_turned, 1)
                if g == 9:
                    pe.wait_ge(r_members, 1)
                    for t in range(TT + 1):
                        out = ps[:, 5, NE * t:NE * (t + 1)]
                        for b in range(min(t, TT)):
                            last = pe.matmul(out, ones[:, :], both[:, b, :], start=b == 0, stop=t == TT and b == TT - 1, skip_group_check=True)
                        if t < TT:
                            last = pe.matmul(out, mats[:, BEFORE, :], both[:, t, :], start=t == 0, stop=True, skip_group_check=True)
                    last.then_inc(r_ranks, 1)
            pe.wait_ge(ht_kept, 2 * TT)
            for e in range(NE + 1):
                if e < NE:
                    pe.wait_ge(r_hot, e + 1)
                    if e >= 2:
                        pe.wait_ge(r_info_kept, e - 1)
                    for h in range(2):
                        for t in range(TT):
                            last = pe.matmul(ps[0:4, 4 + 2 * (e % 2) + h, 0:TH], tok_w[:, t, e, :], hot[e % 2][:, t, h * TH:(h + 1) * TH],
                                             start=t == 0, stop=t == TT - 1)
                    last.then_inc(r_info, 1)
                if e:
                    pe.wait_ge(r_info_kept, e)
                    if e >= 3:
                        pe.wait_ge(r_ids, e - 2)
                    for g in range(TT):
                        last = pe.transpose(ps[:, 2 + (e - 1) % 2, 4 * g:4 * g + 4], info_t[:, g * P:(g + 1) * P], ident[0:4, 0:4])
                    last.then_inc(r_info_turned, 1)

            def tables(e):
                return (pe.value_load(size_of[0:1, bass.ds(e, 1)], min_val=0, max_val=len(SIZES) - 1),
                        pe.value_load(tiles_before[0:1, bass.ds(e, 1)], min_val=0, max_val=NE * TT))

            def gather(e, width, halves, before):
                for g, rows in gather_tiles(width, halves):
                    if g >= 2:
                        wait_apart(pe, g_lo_kept, before + g - 1)
                    wait_apart(pe, g_rows, 16 * (before + min(len(gather_tiles(width, halves)), g - g % 2 + 2)))
                    for k in range(KT):
                        last = pe.transpose(ps[:, 2 * (g % 2) + k // 4, (k % 4) * P:(k % 4) * P + rows],
                                            rows_g[0:rows, g % 2, k * P:(k + 1) * P], ident[0:rows, 0:rows])
                    last.then_inc(g_turned, 1)

            def w13(e, width, halves, before):
                n0 = MOE + N_ITEM * e

                def chunk(slot, n):
                    begin(n)
                    wh = hi[slot][:, :].rearrange("p (w k c) -> p w k c", w=2, k=KT)
                    wl = lo[slot][:, :].rearrange("p (w k c) -> p w k c", w=2, k=KT)
                    for h in range(halves):
                        cols = slice(h * TH, h * TH + width)
                        for w in range(2):
                            if h == 0 and w == 1:
                                second(n)
                            for k in range(KT):
                                if wide(width, halves):
                                    last = passes_wide(4 * (slot % 2) + w, width, wh[:, w, k, :], wl[:, w, k, :],
                                                       h_both[:, :, k, cols], k == 0, k == KT - 1)
                                else:
                                    last = passes(ps[:, 4 * (slot % 2) + 2 * h + w, 0:width], wh[:, w, k, :], wl[:, w, k, :],
                                                  hh[:, k, cols], hl[:, k, cols], k == 0, k == KT - 1)
                            if halves == 1 or w == 1:
                                last.then_inc(gemm_out, 1)

                wait_apart(pe, g_lo_kept, before + len(gather_tiles(width, halves)))
                with pe.Fori(0, JT // 2) as pr:
                    for u in range(2):
                        chunk(u, n0 + 2 * pr + u)
                chunk(C_SLOT, n0 + JT - 1)

            def w2(e, width, halves, gathered):
                n0 = MOE + N_ITEM * e

                def chunk(slot, m):
                    begin(n0 + JT + m)
                    for h in range(halves):
                        cols = slice(h * TH, h * TH + width)
                        for k in range(JT):
                            if h == 0 and k == JH:
                                if halves == 1:
                                    last.then_inc(gemm_out, 1)
                                second(n0 + JT + m)
                            if wide(width, halves):
                                last = passes_wide(4 + 2 * slot, width, down(slot, k, hi), down(slot, k, lo),
                                                   g_both[:, :, k, cols], k == 0, k == JT - 1)
                            else:
                                last = passes(ps[:, 4 + 2 * slot + h, 0:width], down(slot, k, hi), down(slot, k, lo),
                                              g_hi[:, k, cols], g_lo[:, k, cols], k == 0, k == JT - 1)
                        last.then_inc(gemm_out, 1)

                def turn(u, m, first=False):
                    pe.wait_ge(evac, 2 * (n0 + JT + m + 1))
                    if not first:
                        pe.wait_ge(y_rows, KT * e + m - 1)
                    for g, rows in gather_tiles(width, halves):
                        last = pe.transpose(ps[0:rows, 2 * u + g // 4, (g % 4) * P:(g % 4 + 1) * P],
                                            yb[:, u, g * P:g * P + rows], ident)
                    last.then_inc(y_turned, 1)

                pe.wait_ge(f_lo, 2 * JT * (e + 3))
                chunk(A_SLOT, 0)
                chunk(B_SLOT, 1)
                if gathered is not None:
                    pe.wait_ge(g_lo_kept, gathered)
                turn(A_SLOT, 0, True)
                chunk(A_SLOT, 2)
                turn(B_SLOT, 1, True)
                with pe.Fori(1, KT // 2 - 1) as pr:
                    chunk(B_SLOT, 2 * pr + 1)
                    turn(A_SLOT, 2 * pr)
                    chunk(A_SLOT, 2 * pr + 2)
                    turn(B_SLOT, 2 * pr + 1)
                chunk(B_SLOT, KT - 1)
                turn(A_SLOT, KT - 2)
                turn(B_SLOT, KT - 1)

            def expert(e, last):
                size, before = tables(e)
                for i, (width, halves) in enumerate(SIZES):
                    with pe.If(size == i):
                        w13(e, width, halves, before)
                if not last:
                    size_next, before_next = tables(e + 1)
                    wait_apart(pe, evac, 2 * (MOE + N_ITEM * e + JT))
                    for i, (width, halves) in enumerate(SIZES):
                        with pe.If(size_next == i):
                            gather(e + 1, width, halves, before_next)
                    gathered = pe.value_load(tiles_after[0:1, bass.ds(e + 1, 1)], min_val=1, max_val=NE * TT)
                for i, (width, halves) in enumerate(SIZES):
                    with pe.If(size == i):
                        w2(e, width, halves, None if last else gathered)
                wait_apart(pe, y_rows, KT * (e + 1))

            pe.wait_ge(r_tables, 1)
            pe.wait_ge(r_ids, NE)
            size, before = tables(0)
            for i, (width, halves) in enumerate(SIZES):
                with pe.If(size == i):
                    gather(0, width, halves, before)
            with pe.Fori(0, NE - 1) as e:
                expert(e, False)
            expert(NE - 1, True)

            for t in range(TT):
                pe.wait_ge(c_sum, t + 1)
                if t >= 2:
                    pe.wait_ge(c_added, KT * (t - 1))
                for k in range(KT):
                    last = pe.transpose(ps[:, 2 * (t % 2) + k // 4, (k % 4) * P:(k % 4 + 1) * P], rows_c[:, t, 0, k * P:(k + 1) * P], ident)
                last.then_inc(c_turned, 1)
            pe.wait_ge(c_added, KT * TT)
            norm_pe(4)
            for g in range(2 * TT):
                t, q = g // 2, g % 2
                for k in range(4):
                    if t == 0:
                        pe.wait_ge(z_y, 4 * q + k + 1)
                    if g >= 4 and k == 0:
                        pe.wait_ge(z_kept, g - 3)
                    last = pe.transpose(ps[:, g % 4, k * P:(k + 1) * P], xT[:, 4 * q + k, t * P:(t + 1) * P], ident)
                last.then_inc(z_turned, 1)

        @block.vector
        def _(dve):
            links = [0]

            def link(ins):
                links[0] += 1
                ins.then_inc(chain, 1)
                dve.wait_ge(chain, links[0])

            def split_lo(slot, n, parts=WHOLE, which=(0, 1)):
                for h in which:
                    dve.wait_ge(hi_done, 2 * n + h + 1)
                    dve.tensor_tensor(lo[slot][:, parts[h]], raw[slot][:, parts[h]], hi[slot][:, parts[h]].bitcast(F32),
                                      ALU.subtract).then_inc(lo_done, 1)

            dve.memset(prow[:, :, :], 0.0).then_inc(prow_zero, 1)
            dve.memset(ones[:, :], 1.0).then_inc(ones_set, 1)
            dve.memset(wg[:, :, :], 0.0).then_inc(ones_set, 1)
            dve.memset(cs_h0[:, :, :].bitcast(F32), 0.0).then_inc(csz, 1)
            dve.wait_ge(par_turned, 1)
            dve.tensor_copy(par[:, :, :], ps[:, 5, 0:3 * P].rearrange("p (s c) -> p s c", s=3)).then_inc(par_kept, 1)
            dve.wait_ge(cs_silu, 1)
            dve.wait_ge(csz, 1)
            for h in range(2):
                link(dve.tensor_copy(cs_hl[:, :, h], cs[:, h, :]))
                dve.tensor_copy(cs_h0[:, :, h], cs[:, h, :])
                last = dve.tensor_tensor(cs_hl[:, :, 2 + h], cs[:, h, :], cs_hl[:, :, h].bitcast(F32), ALU.subtract)
            last.then_inc(cs_split, 1)
            dve.wait_ge(par_kept, 1)
            lam = par[:, 1, LAM:LAM + 8]
            link(dve.tensor_scalar(sm[:, 2, :], lam, -1.0, None, ALU.mult))
            dve.tensor_tensor(sm[:, 0, :], lam, sm[:, 2, :], ALU.max).then_inc(ab_lam, 1)
            split_lo(0, 0)
            split_lo(1, 1)
            with dve.Fori(0, X_AFTER) as pr:
                for u in range(2):
                    split_lo(u, 2 * pr + u + 2)
            for g in range(0, 10, 2):
                dve.wait_ge(x_turned, g + 1)
                if g >= 2:
                    dve.wait_ge(x_kept, g)
                t, q = g // 2, g % 2
                dve.tensor_copy(xT[:, 4 * q:4 * q + 4, t * P:(t + 1) * P],
                                ps[:, 1 + g % 3, :].rearrange("p (k c) -> p k c", k=4)).then_inc(x_kept, 1)
            with dve.Fori(X_AFTER, N_MOD // 2) as pr:
                for u in range(2):
                    split_lo(u, 2 * pr + u + 2)
            dve.wait_ge(ex_lam, 1)
            link(dve.tensor_scalar(sm[:, 3, :], sm[:, 1, :], 2.0, None, ALU.add))
            link(dve.reciprocal(sm[:, 3, :], sm[:, 3, :]))
            link(dve.tensor_tensor(sm[:, 3, :], sm[:, 1, :], sm[:, 3, :], ALU.mult))
            link(dve.tensor_tensor(sm[:, 4, :], sm[:, 3, :], sm[:, 3, :], ALU.mult))
            link(dve.tensor_scalar(sm[:, 5, :], sm[:, 4, :], 1.0 / 15, None, ALU.mult))
            for odd in (13, 11, 9, 7, 5, 3):
                link(dve.scalar_tensor_tensor(out=sm[:, 5, :], in0=sm[:, 5, :], scalar=1.0 / odd, in1=sm[:, 4, :],
                                              op0=ALU.add, op1=ALU.mult))
            link(dve.scalar_tensor_tensor(out=sm[:, 5, :], in0=sm[:, 5, :], scalar=1.0, in1=sm[:, 3, :],
                                          op0=ALU.add, op1=ALU.mult))
            link(dve.tensor_scalar(sm[:, 5, :], sm[:, 5, :], 2.0, None, ALU.mult))
            link(dve.scalar_tensor_tensor(out=sm[:, 5, :], in0=sm[:, 2, :], scalar=0.0, in1=sm[:, 5, :],
                                          op0=ALU.max, op1=ALU.add))
            dve.tensor_scalar(sm[:, 6, :], sm[:, 5, :], 8.0, None, ALU.mult)
            dve.tensor_scalar(sm[:, 7, :], sm[:, 5, :], -8.0, None, ALU.mult).then_inc(sp_ready, 1)

            def mod_params(layer, part):
                dve.wait_ge(folded, 2 * layer + part + 1)
                j0, j1 = ((0, 16), (16, 48))[part]
                for c in range(2):
                    last = dve.tensor_tensor(mod[:, layer, j0:j1, c], ps[:, 5 + part, 0:96].rearrange("p (j c) -> p j c", c=2)[:, j0:j1, c],
                                             par[:, 0, 48 * layer + j0:48 * layer + j1], ALU.add)
                link(last)
                g0 = (N1, N2)[part] + KT * layer
                for c in range(2):
                    last = dve.scalar_tensor_tensor(out=amod[:, layer, part, :, c], in0=mod[:, layer, 24 * part + 8:24 * part + 16, c],
                                                    scalar=1.0, in1=par[:, 0, g0:g0 + KT], op0=ALU.add, op1=ALU.mult)
                last.then_inc(mod_set, 1)

            mod_params(0, 0)
            dve.wait_ge(wr_h, 1)
            dve.tensor_tensor(wr_lo[:, :, :], wr_raw[:, :, :], wr_hi[:, :, :].bitcast(F32), ALU.subtract).then_inc(wr_l, 1)

            def norm_dve(i, h=None, layer=None):
                dve.wait_ge(n_mm, KT * (i + 1))
                dve.tensor_scalar(rs[:, :].rearrange("p (h t) -> p h t", h=2), ps[:, 0:2, 0:TH], 1.0 / D, EPS,
                                  ALU.mult, ALU.add).then_inc(n_var, 1)
                dve.wait_ge(n_std, i + 1)
                dve.reciprocal(rs[:, :], rs[:, :]).then_inc(n_rs, 1)
                dve.wait_ge(n_rs, i + 1)

                def t_of(k):
                    if k >= 2:
                        dve.wait_ge(n_aff, KT * i + k - 1)
                    dve.tensor_tensor(tmp[:, 2 + k % 2, 0:T], xT[:, k, :], rs[:, :], ALU.mult).then_inc(n_t, 1)

                t_of(0)
                t_of(1)
                for k in range(KT):
                    if k == 3 and layer is not None:
                        mod_params(layer, 1)
                    dve.wait_ge(n_hi, KT * i + k + 1)
                    dve.tensor_tensor(hl[:, k, :], tmp[:, k % 2, 0:T] if h is None else h[:, k, :], hh[:, k, :].bitcast(F32), ALU.subtract).then_inc(n_lo, 1)
                    if k + 2 < KT:
                        t_of(k + 2)

            norm_dve(0, layer=0)
            for c in range(2):
                split_lo(c % 2, EIN + c + 2)
            for c in range(NC):
                dve.wait_ge(evac, 2 * (EIN + c // 2 + 1))
                w = UA_W - 3
                link(dve.tensor_scalar(xc[:, c, 0:w], up[:, c, 0:w], par[:, 1, ACW + c:ACW + c + 1], par[:, 1, ACB + c:ACB + c + 1],
                                       ALU.mult, ALU.add))
                for j in range(1, A_CONV):
                    ins = dve.scalar_tensor_tensor(out=xc[:, c, 0:w], in0=up[:, c, j:j + w], scalar=par[:, 1, ACW + 4 * j + c:ACW + 4 * j + c + 1],
                                                   in1=xc[:, c, 0:w], op0=ALU.mult, op1=ALU.add)
                    if j < A_CONV - 1:
                        link(ins)
                ins.then_inc(e_xc, 1)
                if c % 2:
                    split_lo(0, EIN + 4 + c // 2 * 2)
                    split_lo(1, EIN + 5 + c // 2 * 2)
            for g in range(NC):
                dve.wait_ge(evac, 2 * (EIN + 4 + g // 2 + 1))
                if g:
                    dve.wait_ge(e_pool, g)
                w, half = 2, 1
                left, right = 1, UB_W
                link(dve.tensor_tensor(tmp[:, 0, 1:UB_W], ub[:, g, 1:UB_W], ub[:, g, 0:UB_W - 1], ALU.add))
                level = 0
                while w < WINDOWS[g]:
                    left, right = left + half, right - half
                    link(dve.tensor_tensor(tmp[:, (level + 1) % 2, left:right], tmp[:, level % 2, left - half:right - half],
                                           tmp[:, level % 2, left + half:right + half], ALU.add))
                    w, half, level = 2 * w, w, level + 1
                buf = tmp[:, level % 2, :]
                link(dve.tensor_scalar(buf[:, 8:UB_S + TS], buf[:, 8:UB_S + TS], 1.0 / w, None, ALU.mult))
                for start, size in ((UB_P, TP), (UB_S, TS)):
                    for e, at in ((0, start), (1, start + size - 8)):
                        last = dve.tensor_tensor(buf[:, at:at + 8], buf[:, at:at + 8], edge[:, g, 8 * e:8 * e + 8], ALU.mult)
                link(last)
                dve.tensor_tensor(ub[:, g, 8:UB_S + TS], buf[:, 8:UB_S + TS], ub[:, g, 8:UB_S + TS], ALU.subtract).then_inc(e_pool, 1)

            for n in range(2):
                for c in range(NC):
                    it = NC * n + c
                    dve.wait_ge(e_a2, it + 1)
                    dve.scalar_tensor_tensor(out=th[:, c, 0:T], in0=tmp[:, 2 + it % 2, 0:T], scalar=1.0, in1=th[:, c, 0:T],
                                             op0=ALU.add, op1=ALU.mult).then_inc(e_q, 1)
                    for lo_t, hi_t, cond in SEGS:
                        p0 = (0, UA_S - 2)[cond]
                        last = dve.tensor_tensor(ii[:, c, lo_t:hi_t], ii[:, c, lo_t:hi_t], xc[:, c, p0:p0 + hi_t - lo_t], ALU.mult)
                    link(last)
                if n:
                    for g in range(NC):
                        dve.wait_ge(e_pmm, g + 1)
                        for lo_t, hi_t, cond in SEGS:
                            last = dve.tensor_scalar(hh[:, 4 + g, lo_t:hi_t], ps[:, 2 * (g % 2) + cond, 0:hi_t - lo_t],
                                                     par[:, 1, BSC + g:BSC + g + 1], None, ALU.mult)
                        link(last)
                        for lo_t, hi_t, cond in SEGS:
                            last = dve.scalar_tensor_tensor(out=hl[:, 4 + g, lo_t:hi_t], in0=ps[:, 2 * (g % 2) + cond, 0:hi_t - lo_t],
                                                            scalar=par[:, 1, BSC + g:BSC + g + 1], in1=hh[:, 4 + g, lo_t:hi_t].bitcast(F32),
                                                            op0=ALU.mult, op1=ALU.subtract)
                        last.then_inc(e_ylo, 1)
                for c in range(NC):
                    it = NC * n + c
                    dve.wait_ge(e_sqrt, it + 1)
                    link(dve.tensor_tensor(th[:, c, 0:T], th[:, c, 0:T], ii[:, c, :], ALU.mult))
                    dst = (yf, ii)[n]
                    for lo_t, hi_t, cond in SEGS:
                        h0 = par[:, 1, ST + it:ST + it + 1] if cond else 0.0
                        if n == 0:
                            o, da, db = (x[:, c, lo_t:hi_t] for x in (dst, rr, th))
                        else:
                            back = slice(hi_t - 1, lo_t - 1 if lo_t else None, -1)
                            o, da, db = (x[:, c, back] for x in (dst, rr, th))
                        last = dve.tensor_tensor_scan(o, da, db, h0, ALU.mult, ALU.add)
                    last.then_inc(e_scan, 1)
            dve.wait_ge(e_scan, 2 * NC)
            dve.tensor_copy(sm[:, 8, 0:4], yf[:, :, TP - 1])
            dve.tensor_copy(sm[:, 8, 4:8], ii[:, :, 0]).then_inc(st_last, 1)
            dve.wait_ge(st_last, 1)
            for c in range(NC):
                link(dve.tensor_tensor(yf[:, c, :], yf[:, c, :], ii[:, c, :], ALU.add))
                if c >= 2:
                    dve.wait_ge(e_yhi, c - 1)
                dve.tensor_tensor(tmp[:, 2 + c % 2, 0:T], yf[:, c, :], ga[:, c, :], ALU.mult).then_inc(e_y, 1)
                if c >= 1:
                    dve.wait_ge(e_yhi, c)
                    dve.tensor_tensor(hl[:, c - 1, :], tmp[:, 2 + (c - 1) % 2, 0:T], hh[:, c - 1, :].bitcast(F32), ALU.subtract).then_inc(e_ylo, 1)
            dve.wait_ge(e_yhi, NC)
            dve.tensor_tensor(hl[:, NC - 1, :], tmp[:, 2 + (NC - 1) % 2, 0:T], hh[:, NC - 1, :].bitcast(F32), ALU.subtract).then_inc(e_ylo, 1)

            def residual(bank, m, h, layer, which):
                last = None
                for lo_t, hi_t, cond in HALF_SEGS[h]:
                    x = xT[:, bass.ds(m, 1), lo_t:hi_t].rearrange("p a t -> p (a t)")
                    last = dve.scalar_tensor_tensor(out=x, in0=ps[:, bank, lo_t - TH * h:hi_t - TH * h], scalar=gate_of(layer, which, m, cond),
                                                    in1=x, op0=ALU.mult, op1=ALU.add)
                return last

            def residual_pair(slot, n, c, layer):
                for h in range(2):
                    dve.wait_ge(gemm_out, 2 * n + h + 1)
                    for i in range(2):
                        last = residual(4 * (slot % 2) + 2 * h + i, 2 * c + i, h, layer, 0)
                    last.then_inc(evac, 1)

            for c in range(4):
                residual_pair(c % 2, EOUT + c, c, 0)
                split_lo(c % 2, EOUT + c + 2)
            norm_dve(1)

            def ff13_evac(slot, n, j, f):
                dve.wait_ge(lo_done, 2 * n + 4)
                for h in range(2):
                    dve.wait_ge(f_silu, 2 * JT * f + 2 * j + h + 1)
                    dve.tensor_tensor(gf(h), sil(h), ps[:, 4 * (slot % 2) + 2 * h + 1, 0:TH], ALU.mult).then_inc(evac, 1)
                for h in range(2):
                    dve.wait_ge(f_hi, 2 * JT * f + 2 * j + h + 1)
                    v = [x[:, bass.ds(j, 1), h * TH:(h + 1) * TH].rearrange("p a c -> p (a c)") for x in (g_lo, g_hi)]
                    dve.tensor_tensor(v[0], gf(h), v[1].bitcast(F32), ALU.subtract).then_inc(f_lo, 1)

            def ff2_evac(slot, n, m):
                for h in range(2):
                    dve.wait_ge(gemm_out, 2 * n + h + 1)
                    residual(4 + 2 * slot + h, m, h, 0, 1).then_inc(evac, 1)

            with dve.Fori(0, 2) as f:
                n0 = FF + N_ITEM * f
                with dve.Fori(0, JT // 2 - 1) as pr:
                    for u in range(2):
                        ff13_evac(u, n0 + 2 * pr + u, 2 * pr + u, f)
                        split_lo(u, n0 + 2 * pr + u + 2)
                ff13_evac(A_SLOT, n0 + JT - 3, JT - 3, f)
                split_lo(C_SLOT, n0 + JT - 1)
                ff13_evac(B_SLOT, n0 + JT - 2, JT - 2, f)
                split_lo(A_SLOT, n0 + JT, DOWN)
                ff13_evac(C_SLOT, n0 + JT - 1, JT - 1, f)
                split_lo(B_SLOT, n0 + JT + 1, DOWN)
                with dve.Fori(0, KT // 2 - 1) as pr:
                    for u in range(2):
                        ff2_evac(u, n0 + JT + 2 * pr + u, 2 * pr + u)
                        split_lo(u, n0 + JT + 2 + 2 * pr + u, DOWN)
                for u in range(2):
                    ff2_evac(u, n0 + N_ITEM - 2 + u, KT - 2 + u)
                    split_lo(u, n0 + N_ITEM + u)

            with dve.Fori(0, N_MOD // 2) as pr:
                for u in range(2):
                    split_lo(u, M1 + 2 * pr + u + 2)
            mod_params(1, 0)
            norm_dve(2, layer=1)
            for c in range(5):
                split_lo(*OIN_NEXT[c][:2])
            for c in range(NC):
                if c % 2 == 0:
                    dve.wait_ge(evac, 2 * (OIN + 5 + c // 2 + 1))
                for lo_t, hi_t, cond in SEGS:
                    p0 = (GC_P, GC_S)[cond]
                    last = dve.tensor_tensor(gp[:, c, p0:p0 + hi_t - lo_t], gp[:, c, p0:p0 + hi_t - lo_t], vp[:, c, lo_t:hi_t], ALU.mult)
                last.then_inc(gp_set, 1)
                if c % 2:
                    split_lo(*OIN_NEXT[5 + c // 2][:2])

            conv_w = GC_W - 30
            todo = [(c, j) for c in range(NC - 1) for j in range(C_CONV)]

            def taps(n):
                for c, j in todo[:n]:
                    w = par[:, 2, NC * j + c:NC * j + c + 1]
                    if j == 0:
                        dve.wait_ge(gp_set, NC)
                        ins = dve.tensor_scalar(vp[:, c, 0:conv_w], gp[:, c, 0:conv_w], w, par[:, 1, CCB + c:CCB + c + 1], ALU.mult, ALU.add)
                    else:
                        ins = dve.scalar_tensor_tensor(out=vp[:, c, 0:conv_w], in0=gp[:, c, j:j + conv_w], scalar=w, in1=vp[:, c, 0:conv_w],
                                                       op0=ALU.mult, op1=ALU.add)
                    if j == C_CONV - 1:
                        ins.then_inc(c_dve, 1)
                    else:
                        link(ins)
                del todo[:n]

            taps(4)
            dve.wait_ge(o_sum, 5)
            dve.tensor_scalar(hrs[:, :].rearrange("p (h t) -> p h t", h=2), ps[0:10, 4:6, 0:TH], 1.0 / HD, EPS, ALU.mult, ALU.add).then_inc(o_var, 1)
            taps(2)
            dve.wait_ge(o_std, 1)
            dve.reciprocal(hrs[:, :], hrs[:, :]).then_inc(o_rs, 1)
            taps(2)

            def qn(i):
                x = qf[:, i, :] if i < 4 else kf[:, :]
                g = QN if i < 4 else KN
                dve.wait_ge(o_spread, i + 1)
                dve.scalar_tensor_tensor(out=x.rearrange("p (h t) -> p h t", h=2), in0=ps[:, 2 * (i % 2):2 * (i % 2) + 2, 0:TH],
                                         scalar=par[:, 1, g:g + 1], in1=x.rearrange("p (h t) -> p h t", h=2),
                                         op0=ALU.mult, op1=ALU.mult).then_inc(o_qn, 1)

            def rope(i):
                x = (qf[:, i, :] if i < 4 else kf[:, :])[:, TP:T]
                y = x if i < 4 else kk[:, TP:T]
                dve.wait_ge(o_swap, i + 1)
                if i:
                    dve.wait_ge(o_rope, i)
                dve.tensor_tensor(tmp[:, 2, 0:TS], ps[:, 6 + i % 2, 0:TS], sin_t[:, :], ALU.mult).then_inc(o_sw_read, 1)
                dve.wait_ge(o_qn, i + 1)
                link(dve.tensor_tensor(y, x, cos_t[:, :], ALU.mult))
                dve.wait_ge(o_sw_read, i + 1)
                dve.tensor_tensor(y, y, tmp[:, 2, 0:TS], ALU.add).then_inc(o_rope, 1)

            for i in range(5):
                qn(i)
                if i:
                    rope(i - 1)
            rope(4)
            dve.wait_ge(v_turned, 2)
            dve.tensor_copy(vt[:, 0, :], ps[:, 5, 0:P])
            dve.tensor_copy(kk[:, 0:P], ps[:, 5, P:2 * P])
            dve.tensor_copy(knew[:, :], ps[:, 5, 2 * P:3 * P]).then_inc(v_kept, 1)

            def head_lo(h):
                dve.wait_ge(a_ohi, h + 1)
                r = slice(HD * (h // 4), HD * (h // 4) + HD)
                dve.tensor_tensor(hl[r, 4 + h % 4, 0:TP], ps[r, 7, 0:TP], hh[r, 4 + h % 4, 0:TP].bitcast(F32), ALU.subtract)
                dve.tensor_tensor(hl[r, 4 + h % 4, TP:T], ps[r, 6, 0:TS], hh[r, 4 + h % 4, TP:T].bitcast(F32), ALU.subtract).then_inc(a_olo, 1)

            for s in range(NH * TT + 8):
                if s < NH * TT:
                    dve.wait_ge(a_s, s + 1)
                    if s >= 2:
                        dve.wait_ge(a_exp, s - 1)
                    if s % TT == 0:
                        link(dve.reduce_max(am[:, 0, s % 2:s % 2 + 1], ps[:, 2 * (s % 2), 0:P], AX_X))
                    else:
                        link(dve.reduce_max(am[:, 0, s % 2:s % 2 + 1], ps[:, 2 * (s % 2):2 * (s % 2) + 2, 0:TH], AX_XY))
                    dve.tensor_scalar(am[:, 1, s % 2:s % 2 + 1], am[:, 0, s % 2:s % 2 + 1], -HD ** -0.5, None, ALU.mult).then_inc(a_max, 1)
                if 1 <= s < NH * TT + 1:
                    u = s - 1
                    width = P if u % TT == 0 else T
                    dve.wait_ge(a_exp, u + 1)
                    link(dve.reciprocal(am[:, 3, u % 2:u % 2 + 1], am[:, 2, u % 2:u % 2 + 1]))
                    dve.tensor_scalar(pp[:, u % 2, 0:width], pp[:, u % 2, 0:width], am[:, 3, u % 2:u % 2 + 1], None, ALU.mult).then_inc(a_norm, 1)
                if 2 <= s < NH * TT + 2 and (s - 2) % TT:
                    u = s - 2
                    h, t = u // TT, u % TT
                    dve.wait_ge(a_t, u + 1)
                    if h >= 2:
                        dve.wait_ge(a_pv, h - 1)
                    dve.tensor_copy(pt[:, h % 2, 4, (t - 1) * P:t * P], ps[:, 5, 0:P]).then_inc(a_kept5, 1)
                if s >= 12 and (s - 2) % TT == 0:
                    head_lo((s - 12) // TT)
                taps(2)
            taps(len(todo))
            dve.wait_ge(l_mean, 1)
            for c in range(NC):
                for lo_t, hi_t, cond in SEGS:
                    p0 = (0, GC_S - 15)[cond]
                    last = dve.scalar_tensor_tensor(out=vp[:, c, p0:p0 + hi_t - lo_t], in0=ps[:, cond, 0:hi_t - lo_t], scalar=-1.0 / D_A,
                                                    in1=vp[:, c, p0:p0 + hi_t - lo_t], op0=ALU.mult, op1=ALU.add)
                last.then_inc(l_xc, 1)
            dve.wait_ge(l_vmm, NC)
            for lo_t, hi_t, cond in SEGS:
                last = dve.tensor_scalar(rs[:, lo_t:hi_t], ps[:, 2 + cond, 0:hi_t - lo_t], 1.0 / D_A, EPS, ALU.mult, ALU.add)
            last.then_inc(l_var, 1)
            dve.wait_ge(l_std, 1)
            link(dve.reciprocal(rs[:, :], rs[:, :]))

            def ln_lo(c):
                dve.wait_ge(l_hi, c + 1)
                dve.tensor_tensor(hl[:, c, :], tmp[:, c % 2, 0:T], hh[:, c, :].bitcast(F32), ALU.subtract).then_inc(l_lo, 1)

            for c in range(NC):
                if c >= 2:
                    dve.wait_ge(l_silu, c - 1)
                for lo_t, hi_t, cond in SEGS:
                    p0 = (0, GC_S - 15)[cond]
                    last = dve.tensor_tensor(tmp[:, 2 + c % 2, lo_t:hi_t], vp[:, c, p0:p0 + hi_t - lo_t], rs[:, lo_t:hi_t], ALU.mult)
                last.then_inc(l_y, 1)
                if c:
                    ln_lo(c - 1)
            ln_lo(NC - 1)

            for c in range(4):
                residual_pair(c % 2, OOUT + c, c, 1)
                split_lo(c % 2, OOUT + c + 2)
            norm_dve(3, hf)

            dve.wait_ge(r_turned, 1)
            for t in range(TT):
                last = dve.tensor_tensor(lg[:, t, :], ps[:, 4, NE * t:NE * (t + 1)], brow[:, :], ALU.add)
            link(last)
            for t in range(TT):
                last = dve.max(mx8[:, t, :], lg[:, t, :])
            link(last)
            for t in range(TT):
                last = dve.max_index(ix8[:, t, :], mx8[:, t, :], lg[:, t, :])
            link(last)
            dve.tensor_tensor(gw[:, :, 1], mx8[:, :, 1], mx8[:, :, 0], ALU.subtract).then_inc(r_d, 1)
            link(dve.tensor_copy(ixf[:, :, :], ix8[:, :, 0:2]))
            for t in range(TT):
                for k in range(2):
                    last = dve.tensor_scalar(members[:, k, t, :], iota8[:, :], ixf[:, t, k:k + 1], None, ALU.is_equal)
            link(last)
            dve.tensor_tensor(both[:, :, :], members[:, 0, :, :], members[:, 1, :, :], ALU.add).then_inc(r_members, 1)
            dve.wait_ge(r_exp, 1)
            link(dve.tensor_scalar(gw[:, :, 0], gw[:, :, 1], 1.0, None, ALU.add))
            link(dve.reciprocal(gw[:, :, 0], gw[:, :, 0]))
            link(dve.tensor_tensor(gw[:, :, 1], gw[:, :, 1], gw[:, :, 0], ALU.mult))
            for t in range(TT):
                link(dve.tensor_scalar(comb[:, t, :], members[:, 1, t, :], gw[:, t, 1:2], None, ALU.mult))
                last = dve.scalar_tensor_tensor(out=comb[:, t, :], in0=members[:, 0, t, :], scalar=gw[:, t, 0:1], in1=comb[:, t, :],
                                                op0=ALU.mult, op1=ALU.add)
            link(last)
            link(dve.tensor_copy(tok_w[:, :, :, 1], comb[:, :, :]))
            dve.tensor_tensor(tok_w[:, :, :, 2], comb[:, :, :], tok_w[:, :, :, 1].bitcast(F32), ALU.subtract)
            for t in range(TT):
                for c in (0, 3):
                    last = dve.tensor_scalar(tok_w[:, t, :, c], iota8[:, :], 0.0, tok_id[:, t:t + 1], ALU.mult, ALU.add)
            link(last)
            dve.wait_ge(r_ranks, 1)
            link(dve.tensor_copy(cnt[:, 0, :], ps[:, 5, NE * TT:NE * (TT + 1)]))
            for i, (width, halves) in enumerate(SIZES[:-1]):
                last = dve.tensor_scalar(cnt[:, 1 + i, :], cnt[:, 0, :], float(width), None, ALU.is_gt)
            link(last)
            link(dve.tensor_tensor(cnt[:, 0, :], cnt[:, 1, :], cnt[:, 2, :], ALU.add))
            for i in range(2, len(SIZES) - 1):
                link(dve.tensor_tensor(cnt[:, 0, :], cnt[:, 0, :], cnt[:, 1 + i, :], ALU.add))
            link(dve.tensor_copy(size_of[:, :], cnt[0:1, 0, :]))
            own, one = len(SIZES) + 1, len(SIZES) + 2
            link(dve.tensor_scalar(cnt[:, own, :], cnt[:, 1, :], 0.0, float(TILES[0]), ALU.mult, ALU.add))
            for i in range(len(SIZES) - 1):
                link(dve.scalar_tensor_tensor(out=cnt[:, own, :], in0=cnt[:, 1 + i, :], scalar=float(TILES[i + 1] - TILES[i]), in1=cnt[:, own, :],
                                              op0=ALU.mult, op1=ALU.add))
            link(dve.memset(cnt[:, one, :], 1.0))
            link(dve.tensor_tensor_scan(cnt[:, 0, :], cnt[:, one, :], cnt[:, own, :], 0.0, ALU.mult, ALU.add))
            link(dve.tensor_copy(tiles_after[:, :], cnt[0:1, 0, :]))
            link(dve.tensor_tensor(cnt[:, 0, :], cnt[:, 0, :], cnt[:, own, :], ALU.subtract))
            dve.tensor_scalar(base8[:, :], cnt[:, 0, :], float(P), None, ALU.mult)
            dve.tensor_copy(tiles_before[:, :], cnt[0:1, 0, :]).then_inc(r_tables, 1)
            link(dve.tensor_copy(rank[:, :, :], ps[:, 5, 0:NE * TT].rearrange("p (t e) -> p t e", t=TT)))
            for t in range(TT):
                last = dve.tensor_tensor(lg[:, t, :], rank[:, t, :], base8[:, :], ALU.add)
            link(last)
            for k in range(2):
                link(dve.tensor_tensor(comb[:, :, :], lg[:, :, :], members[:, k, :, :], ALU.mult))
                link(dve.tensor_reduce(slotf[:, :, k], comb[:, :, :], AX_X, ALU.add))
            link(dve.tensor_copy(slots[:, :, :], slotf[:, :, :]))
            link(dve.scalar_tensor_tensor(out=rank[:, :, :], in0=rank[:, :, :], scalar=1.0, in1=both[:, :, :], op0=ALU.add, op1=ALU.mult))
            link(dve.tensor_scalar(rank[:, :, :], rank[:, :, :], -1.0, None, ALU.add))

            def info(e):
                dve.wait_ge(r_info_turned, e + 1)
                v = ps[:, 2 + e % 2, 0:4 * TT].rearrange("p (g c) -> p g c", c=4)
                dve.tensor_copy(ids[:, e, :], v[:, :, 0])
                link(dve.tensor_copy(slot_w[:, e, :], v[:, :, 1]))
                dve.tensor_tensor(slot_w[:, e, :], slot_w[:, e, :], v[:, :, 2], ALU.add).then_inc(r_ids, 1)

            dve.wait_ge(iota_in, 16)
            for e in range(NE):
                if e == 1:
                    dve.wait_ge(ht_turned, 2 * TT)
                elif e >= 2:
                    dve.wait_ge(r_info, e - 1)
                for t in range(TT):
                    last = dve.tensor_scalar(hot[e % 2][:, t, :], iota_t[:, :], rank[:, t, e:e + 1], None, ALU.is_equal)
                last.then_inc(r_hot, 1)
                if e >= 2:
                    info(e - 2)
            for e in range(NE - 2, NE):
                info(e)

            def tables(e):
                return (dve.value_load(size_of[0:1, bass.ds(e, 1)], min_val=0, max_val=len(SIZES) - 1),
                        dve.value_load(tiles_before[0:1, bass.ds(e, 1)], min_val=0, max_val=NE * TT))

            def w13(e, width, halves):
                n0, f = MOE + N_ITEM * e, 2 + e

                def sum1(slot, n, j):
                    if wide(width, halves):
                        dve.wait_ge(evac, 2 * n)
                        dve.wait_ge(gemm_out, 2 * n + 1)
                        b = ps[:, 4 * (slot % 2), 0:2 * width]
                        dve.tensor_reduce(sil(0, width), b.rearrange("p (a c) -> p c a", a=2), AX_X, ALU.add).then_inc(f_silu, 1)

                def gate(slot, n, j):
                    dve.wait_ge(f_lo, 2 * JT * f + 2 * j)
                    if wide(width, halves):
                        dve.wait_ge(gemm_out, 2 * n + 2)
                        b = ps[:, 4 * (slot % 2) + 1, 0:2 * width]
                        dve.tensor_reduce(gf(0, width), b.rearrange("p (a c) -> p c a", a=2), AX_X, ALU.add).then_inc(evac, 1)
                        dve.wait_ge(f_silu, 2 * JT * f + 2 * j + 2)
                        dve.wait_ge(evac, 2 * n + 1)
                        dve.tensor_tensor(gf(0, width), gf(0, width), sil(0, width), ALU.mult).then_inc(evac, 1)
                        return
                    for h in range(halves):
                        dve.wait_ge(gemm_out, 2 * n + 2 // halves * (h + 1))
                        dve.wait_ge(f_silu, 2 * JT * f + 2 * j + 2 // halves * (h + 1))
                        dve.tensor_tensor(gf(h, width), sil(h, width), ps[:, 4 * (slot % 2) + 2 * h + 1, 0:width],
                                          ALU.mult).then_inc(evac, 2 // halves)

                def rest(j):
                    for h in range(halves):
                        dve.wait_ge(f_hi, 2 * JT * f + 2 * j + 2 // halves * (h + 1))
                        v = [x[:, bass.ds(j, 1), h * TH:h * TH + width].rearrange("p a c -> p (a c)") for x in (g_lo, g_hi)]
                        dve.tensor_tensor(v[0], gf(h, width), v[1].bitcast(F32), ALU.subtract).then_inc(f_lo, 2 // halves)

                def step(slot, j, slot_next, parts=WHOLE):
                    n = n0 + j
                    sum1(slot, n, j)
                    if wide(width, halves):
                        split_lo(slot_next, n + 2, parts, (0,))
                    gate(slot, n, j)
                    split_lo(slot_next, n + 2, parts, (1,) if wide(width, halves) else (0, 1))
                    rest(j)

                with dve.Fori(0, JT // 2 - 1) as pr:
                    for u in range(2):
                        step(u, 2 * pr + u, u)
                step(A_SLOT, JT - 3, C_SLOT)
                step(B_SLOT, JT - 2, A_SLOT, DOWN)
                step(C_SLOT, JT - 1, B_SLOT, DOWN)

            def gather(e, width, halves, before):
                for g, rows in gather_tiles(width, halves):
                    dve.wait_ge(g_hi_kept, before + g + 1)
                    dve.tensor_tensor(hl[:, :, g * P:g * P + rows].rearrange("p (a b) c -> p a b c", a=2),
                                      ps[:, 2 * (g % 2):2 * (g % 2) + 2, :].rearrange("p a (b c) -> p a b c", b=4)[:, :, :, 0:rows],
                                      hh[:, :, g * P:g * P + rows].bitcast(F32).rearrange("p (a b) c -> p a b c", a=2),
                                      ALU.subtract).then_inc(g_lo_kept, 1)

            def w2(e, width, halves, last):
                n0 = MOE + N_ITEM * e

                def rows_of(u, pr):
                    dve.wait_ge(y_turned, KT * e + 2 * pr + u + 1)
                    if not isinstance(pr, int) or pr > 0:
                        dve.wait_ge(out_rows[u], 16 + 16 * KT * e + 32 * pr)
                    for g, rows in gather_tiles(width, halves):
                        ins = dve.tensor_scalar(rows_y[0:rows, u, g, :], ps[0:rows, 2 * u + g // 4, (g % 4) * P:(g % 4 + 1) * P],
                                                slot_w[0:rows, bass.ds(e, 1), g:g + 1].rearrange("p a b -> p (a b)"), None, ALU.mult)
                    ins.then_inc(y_rows, 1)

                def add(u, m):
                    if wide(width, halves):
                        dve.wait_ge(gemm_out, 2 * (n0 + JT + m + 1))
                        b = ps[:, 4 + 2 * u, 0:2 * width]
                        dve.tensor_reduce(yb[:, u, 0:width], b.rearrange("p (a c) -> p c a", a=2), AX_X, ALU.add).then_inc(evac, 2)

                for u in range(2):
                    split_lo(u, n0 + JT + 2 + u, DOWN)
                    add(u, u)
                    rows_of(u, 0)
                with dve.Fori(1, KT // 2 - 1) as pr:
                    for u in range(2):
                        split_lo(u, n0 + JT + 2 + 2 * pr + u, DOWN)
                        add(u, 2 * pr + u)
                        rows_of(u, pr)
                for u in range(2):
                    if not last:
                        split_lo(u, n0 + N_ITEM + u)
                    add(u, KT - 2 + u)
                    rows_of(u, KT // 2 - 1)

            def expert(e, last):
                size, before = tables(e)
                for i, (width, halves) in enumerate(SIZES):
                    with dve.If(size == i):
                        w13(e, width, halves)
                if not last:
                    size_next, before_next = tables(e + 1)
                    for i, (width, halves) in enumerate(SIZES):
                        with dve.If(size_next == i):
                            gather(e + 1, width, halves, before_next)
                for i, (width, halves) in enumerate(SIZES):
                    with dve.If(size == i):
                        w2(e, width, halves, last)

            size, before = tables(0)
            for i, (width, halves) in enumerate(SIZES):
                with dve.If(size == i):
                    gather(0, width, halves, before)
            with dve.Fori(0, NE - 1) as e:
                expert(e, False)
            expert(NE - 1, True)

            for t in range(TT + 1):
                if t < TT:
                    dve.wait_ge(c_rows[t], 32)
                    dve.tensor_tensor(rows_c[:, t, 0, :], rows_c[:, t, 0, :], rows_c[:, t, 1, :], ALU.add).then_inc(c_sum, 1)
                if t:
                    dve.wait_ge(c_turned, t)
                    for k in range(KT):
                        x = xT[:, k, (t - 1) * P:t * P]
                        dve.scalar_tensor_tensor(out=x, in0=ps[:, 2 * ((t - 1) % 2) + k // 4, (k % 4) * P:(k % 4 + 1) * P],
                                                 scalar=gate_of(1, 1, k, int(t > 1)), in1=x, op0=ALU.mult, op1=ALU.add).then_inc(c_added, 1)

            dve.wait_ge(n_mm, KT * 5)
            dve.tensor_scalar(rs[:, :].rearrange("p (h t) -> p h t", h=2), ps[:, 0:2, 0:TH], 1.0 / D, EPS,
                              ALU.mult, ALU.add).then_inc(n_var, 1)
            dve.wait_ge(n_std, 5)
            link(dve.reciprocal(rs[:, :], rs[:, :]))
            for k in range(KT):
                dve.scalar_tensor_tensor(out=xT[:, k, :], in0=xT[:, k, :], scalar=par[:, 1, NF + k:NF + k + 1], in1=rs[:, :],
                                         op0=ALU.mult, op1=ALU.mult).then_inc(z_y, 1)
            for g in range(0, 2 * TT, 2):
                dve.wait_ge(z_turned, g + 1)
                if g:
                    dve.wait_ge(z_kept, g)
                dve.tensor_copy(yrows[:, g // 2, 512 * (g % 2):512 * (g % 2) + 512], ps[:, g % 4, :]).then_inc(z_kept, 1)

        @block.gpsimd
        def _(pool):
            pool.dma_start(edge[:, :, :], a["const_edge"].rearrange("(o g) c -> o g c", o=1).to_broadcast([P, NC, 16])).then_inc(small_in, 16)
            pool.dma_start(sel4[:, :], a["const_sel4"]).then_inc(small_in, 16)
            pool.dma_start(iota8[:, :], a["const_iota"].to_broadcast([P, NE])).then_inc(small_in, 16)
            pool.dma_start(tok_id[:, :], a["const_tok"]).then_inc(small_in, 16)
            pool.dma_start(brow[:, :], a["moe_b_router"].to_broadcast([P, NE])).then_inc(small_in, 16)
            pool.dma_start(wr_raw[:, :, :], a["moe_w_router"][0].rearrange("(k p) e -> p k e", p=P)).then_inc(small_in, 16)
            pool.wait_ge(ones_set, 2)
            for i, w in enumerate((a["a_w_r"], a["a_w_i"])):
                v = w[0].rearrange("n (c e) k j -> e k n c j", e=2)
                for e in range(2):
                    for n in range(2):
                        pool.dma_start(wg[e * 64:(e + 1) * 64, 8 * n + 4 * i:8 * n + 4 * i + 4, e * 64:(e + 1) * 64],
                                      v[e, :, n]).then_inc(small_in, 16)
            pool.dma_start(wp[:, :, :], a["b_w_pool"][0].rearrange("g i j -> i g j")).then_inc(small_in, 16)
            for t in range(TT):
                src = a["x_prompt"][0] if t == 0 else a["x_sample"][0, (t - 1) * P:t * P, :]
                pool.dma_start(xrows[:, t, :], src).then_inc(x_in, 16)
            def norm_pool(i, layer, which, h=None):
                for k in range(KT):
                    pool.wait_ge(n_t, KT * i + k + 1)
                    if k >= 2:
                        pool.wait_ge(n_lo, KT * i + k - 1)
                    for lo_t, hi_t, cond in SEGS:
                        last = pool.tensor_scalar((tmp[:, k % 2, :] if h is None else h[:, k, :])[:, lo_t:hi_t], tmp[:, 2 + k % 2, lo_t:hi_t],
                                                  amod[:, layer, which, k, cond:cond + 1], mod[:, layer, 24 * which + k, cond:cond + 1],
                                                  ALU.mult, ALU.add)
                    last.then_inc(n_aff, 1)

            pool.wait_ge(mod_set, 1)
            norm_pool(0, 0, 0)
            pool.wait_ge(x_turned, 10)
            pool.wait_ge(folded, 2)
            pool.memset(zeros[:, :], 0.0).then_inc(zeros_set, 1)
            pool.wait_ge(zeros_set, 1)
            pool.memset(up[:, :, :], 0.0).then_inc(pads, 1)
            pool.memset(ub[:, :, :], 0.0).then_inc(pads, 1)
            for it in range(2 * NC):
                pool.wait_ge(e_exp, it + 1)
                pool.wait_ge(e_pool, NC)
                if it >= 2:
                    pool.wait_ge(e_q, it - 1)
                c = it % NC
                pool.tensor_tensor(tmp[:, 2 + it % 2, 0:T], rr[:, c, :], rr[:, c, :], ALU.mult).then_inc(e_a2, 1)
            norm_pool(1, 0, 1)
            with pool.Fori(0, Y_TILES) as i:
                wait_apart(pool, evac, 2 * (FF + i))
                pool.dma_start(y_dram[bass.ds(i, 1)].rearrange("o p (a c) -> p (o a) c", c=P),
                               zeros[:, :].rearrange("p (o c) -> p o c", o=1).to_broadcast([P, D // P, P])).then_inc(y_zero, 16)
            pool.wait_ge(mod_set, 3)
            norm_pool(2, 1, 0)
            pool.wait_ge(folded, 4)
            pool.memset(gp[:, :, :], 0.0).then_inc(gp_pads, 1)
            pool.wait_ge(gp_set, NC)
            pool.wait_ge(par_kept, 1)
            c, conv_w = NC - 1, GC_W - 30
            for j in range(C_CONV):
                w = par[:, 2, NC * j + c:NC * j + c + 1]
                if j == 0:
                    pool.tensor_scalar(vp[:, c, 0:conv_w], gp[:, c, 0:conv_w], w, par[:, 1, CCB + c:CCB + c + 1], ALU.mult, ALU.add).then_inc(pchain, 1)
                else:
                    pool.tensor_scalar(tmp[:, 3, 0:conv_w], gp[:, c, j:j + conv_w], w, None, ALU.mult).then_inc(pchain, 1)
                    pool.wait_ge(pchain, 2 * j)
                    ins = pool.tensor_tensor(vp[:, c, 0:conv_w], vp[:, c, 0:conv_w], tmp[:, 3, 0:conv_w], ALU.add)
                    ins.then_inc(c_pool if j == C_CONV - 1 else pchain, 1)
                    if j < C_CONV - 1:
                        pool.wait_ge(pchain, 2 * j + 1)
            pool.wait_ge(kv_stored, 32)
            pool.wait_ge(evac, 2 * MOE)
            pool.dma_start(iota_t[:, :], a["const_iota_t"].to_broadcast([P, T])).then_inc(iota_in, 16)
            norm_pool(3, 1, 1, hf)
            for t in range(TT):
                pool.wait_ge(ht_kept, 2 * (t + 1))
                pool.dma_start(h_dram[t * P:(t + 1) * P, :], hrows[:, t, :]).then_inc(out_rows[t] if t < 2 else h_stored, 16)

            def tables(e):
                return (pool.value_load(size_of[0:1, bass.ds(e, 1)], min_val=0, max_val=len(SIZES) - 1),
                        pool.value_load(tiles_before[0:1, bass.ds(e, 1)], min_val=0, max_val=Y_TILES - TT))

            def gather(width, halves, before):
                for g, rows in gather_tiles(width, halves):
                    if g >= 2:
                        wait_apart(pool, g_turned, before + g - 1)
                    pool.indirect_dma_start(rows_g[0:rows, g % 2, :], None, h_dram,
                                            bass.IndirectOffsetOnAxis(ap=ids_now[0:rows, g:g + 1], axis=0)).then_inc(g_rows, 16)

            def gather_any(e):
                size, before = tables(e)
                pool.tensor_copy(ids_now[:, :], ids[:, bass.ds(e, 1), :].rearrange("p a g -> p (a g)")).then_inc(ids_copied, 1)
                wait_apart(pool, ids_copied, e + 1)
                for i, (width, halves) in enumerate(SIZES):
                    with pool.If(size == i):
                        gather(width, halves, before)

            def store(e, width, halves, before):
                full = len(gather_tiles(width, halves)) - 1
                rows = gather_tiles(width, halves)[-1][1]
                with pool.Fori(0, KT // 2) as pr:
                    for u in range(2):
                        m = 2 * pr + u
                        wait_apart(pool, y_rows, KT * e + m + 1)
                        if not full:
                            for p in (0, HD):
                                pool.dma_start(y_dram[bass.ds(before, 1), p:p + HD, bass.ds(m * P, P)].rearrange("g p c -> p (g c)"),
                                               rows_y[p:p + HD, u, 0, :]).then_inc(out_rows[u], 16)
                            continue
                        pool.dma_start(y_dram[bass.ds(before, full), :, bass.ds(m * P, P)].rearrange("g p c -> p g c"),
                                       rows_y[:, u, 0:full, :]).then_inc(out_rows[u], 16)
                        pool.dma_start(y_dram[bass.ds(before + full, 1), 0:rows, bass.ds(m * P, P)].rearrange("g p c -> p (g c)"),
                                       rows_y[0:rows, u, full, :]).then_inc(out_rows[u], 16)

            def store_any(e):
                size, before = tables(e)
                for i, (width, halves) in enumerate(SIZES):
                    with pool.If(size == i):
                        store(e, width, halves, before)

            pool.wait_ge(r_tables, 1)
            pool.wait_ge(r_ids, 1)
            for u in range(2):
                pool.wait_ge(out_rows[u], 16)
            pool.wait_ge(h_stored, 16 * (TT - 2))
            pool.wait_ge(y_zero, 16 * Y_TILES)
            gather_any(0)
            pool.wait_ge(r_ids, NE)
            with pool.Fori(0, NE - 1) as e:
                wait_apart(pool, lo_done, 2 * (MOE + N_ITEM * e + JT))
                gather_any(e + 1)
                store_any(e)
            store_any(NE - 1)
            for u in range(2):
                pool.wait_ge(out_rows[u], 16 + 16 * KT * NE)
            for t in range(TT):
                for k in range(2):
                    pool.indirect_dma_start(rows_c[:, t, k, :], None, y_dram.rearrange("g p c -> (g p) c"),
                                            bass.IndirectOffsetOnAxis(ap=slots[:, t, k:k + 1], axis=0)).then_inc(c_rows[t], 16)


def shape_constants():
    f = np.float32
    mats = np.zeros((3, P, P), f)
    mats[0] = np.eye(P)
    mats[1] = np.triu(np.ones((P, P)), 1)
    swap = np.zeros((P, P), f)
    for d in range(P):
        half = d % 32 // 16
        swap[d + 16 - 32 * half, d] = 2 * half - 1
    mats[2] = swap
    edge = np.ones((4, 16), f)
    for g, w in enumerate((2, 4, 8, 16)):
        for e in range(8):
            edge[g, e] = w / min(w, e + w // 2)
            edge[g, 8 + e] = w / min(w, 8 - e + w // 2)
    t = np.arange(512)
    inv = f(10000.0) ** (-np.arange(16, dtype=f) / f(16))
    ang = np.stack([(t // 64).astype(f)[:, None] * inv, (t % 64).astype(f)[:, None] * inv], axis=1)
    d = np.arange(P) % 64
    table = ang[:, d // 32, d % 16].T
    hsel = np.zeros((P, 5, 16), f)
    hspread = np.zeros((10, 5, P), f)
    for i in range(5):
        for e in range(2):
            r = 8 + e if i == 4 else i + 4 * e
            hsel[64 * e:64 * e + 64, i, r] = 1
            hspread[r, i, 64 * e:64 * e + 64] = 1
    return {"const_mats": mats, "const_edge": edge, "const_sel4": np.array([[1, 0], [0, 1], [1, 0], [0, 1]], f),
            "const_cos": np.cos(table).astype(f), "const_sin": np.sin(table).astype(f), "const_hsel": hsel,
            "const_hspread": hspread, "const_iota": np.arange(8, dtype=f)[None],
            "const_tok": (np.arange(P)[:, None] + P * np.arange(5)[None]).astype(f), "const_iota_t": np.arange(640, dtype=f)[None]}


_INS = ["x_prompt", "x_sample", "c", "state_rglru", "cache_k", "cache_v", "c_ctx", "w_mod", "b_mod", "norm1", "norm2",
        "ev_w_in", "a_conv_w", "a_conv_b", "a_w_r", "a_b_r", "a_w_i", "a_b_i", "a_lam", "b_w_pool", "b_scale", "ev_w_out",
        "od_w_in", "c_conv_w", "c_conv_b", "c_ln_g", "c_ln_b", "q_norm", "k_norm", "od_w_out", "ff_w1", "ff_w3", "ff_w2",
        "moe_w_router", "moe_b_router", "moe_w1", "moe_w3", "moe_w2", "norm_f"]
_OUTS = [("y_prompt", (1, TP, D)), ("y_sample", (1, TS, D)), ("new_state", (1, 1, 2, D_A)),
         ("new_k", (1, 1, TP, 2, HD)), ("new_v", (1, 1, TP, 2, HD))]


def kernel(**inputs):
    import numpy as _np
    import concourse.bacc as _bacc
    from concourse import mybir as _mybir
    from concourse.bass_utils import run_bass_kernel_spmd as _run

    nc = _bacc.Bacc("TRN2", target_bir_lowering=False, num_devices=1)
    given = {name: _np.ascontiguousarray(inputs[name]) for name in _INS}
    given.update(shape_constants())
    arrays, aps = {}, {}
    for name, v in given.items():
        arrays[f"in_{name}_dram"] = v
        aps[name] = nc.dram_tensor(f"in_{name}_dram", v.shape, _mybir.dt.from_np(v.dtype), kind="ExternalInput").ap()
    for name, shape in _OUTS:
        aps[name] = nc.dram_tensor(f"out_{name}_dram", shape, F32, kind="ExternalOutput").ap()
    hybrid_trunk_step(nc, aps)
    r = _run(nc, [arrays], core_ids=[0])
    return tuple(r.results[0][f"out_{name}_dram"] for name, _ in _OUTS)
```
